# Optimizing a Trainium2 kernel written in Bass

```python
import jax, jax.numpy as jnp
from jax import lax
import numpy as np
import jax
import jax.numpy as jnp

D_MODEL = 1024
BATCH = 1
SEQ = 512
DEPTH = 2

N_A_LAYERS = DEPTH // 2
N_B_LAYERS = DEPTH - N_A_LAYERS

LRU_WIDTH = D_MODEL * 3 // 2
LRU_BLOCKS = 16
LRU_BLOCK_W = LRU_WIDTH // LRU_BLOCKS
CONV_WIDTH = 4
LRU_C = 8.0

N_Q_HEADS = 16
N_KV_HEADS = 2
GROUP = N_Q_HEADS // N_KV_HEADS
HEAD_DIM = 64
ATT_WIDTH = N_Q_HEADS * HEAD_DIM
WINDOW = 128
BLOCK = 128

EPS = 1e-6


def rmsnorm(x, g):
    x32 = x.astype(jnp.float32)
    y = x32 * lax.rsqrt(jnp.mean(x32 * x32, axis=-1, keepdims=True) + EPS)
    return (y * g.astype(jnp.float32)).astype(x.dtype)

def causal_depthwise_conv(u, w, b):
    r = u.shape[-1]
    out = lax.conv_general_dilated(
        u, w.astype(u.dtype)[:, None, :], window_strides=(1,),
        padding=[(CONV_WIDTH - 1, 0)],
        dimension_numbers=("NWC", "WIO", "NWC"),
        feature_group_count=r)
    return out + b.astype(u.dtype)

def _linear_combine(c1, c2):
    a1, b1 = c1
    a2, b2 = c2
    return a1 * a2, a2 * b1 + b2

def rglru_layer(x, norm_g, w_in, conv_w, conv_b, wr, br, wi, bi, lam, w_out):
    bsz, seq, _ = x.shape
    h = rmsnorm(x, norm_g)
    u = h @ w_in
    xb, gate = u[..., :LRU_WIDTH], u[..., LRU_WIDTH:]
    xb = causal_depthwise_conv(xb, conv_w, conv_b)
    xs = xb.reshape(bsz, seq, LRU_BLOCKS, LRU_BLOCK_W)
    r = jax.nn.sigmoid((jnp.einsum('bshi,hij->bshj', xs, wr).reshape(bsz, seq, LRU_WIDTH) + br).astype(jnp.float32))
    i = jax.nn.sigmoid((jnp.einsum('bshi,hij->bshj', xs, wi).reshape(bsz, seq, LRU_WIDTH) + bi).astype(jnp.float32))
    log_a = -LRU_C * r * jax.nn.softplus(-lam.astype(jnp.float32))
    a = jnp.exp(log_a)
    b = jnp.sqrt(-jnp.expm1(2.0 * log_a)) * (i * xb.astype(jnp.float32))
    _, hs = lax.associative_scan(_linear_combine, (a, b), axis=1)
    y = hs.astype(x.dtype) * jax.nn.silu(gate)
    return x + y @ w_out

def sliding_window_sink_attention(q, k, v, sinks):
    bsz, seq = q.shape[0], q.shape[1]
    nb = seq // BLOCK
    qb = q.reshape(bsz, nb, BLOCK, N_KV_HEADS, GROUP, HEAD_DIM)

    def band(t):
        cur = t.reshape(bsz, nb, BLOCK, N_KV_HEADS, HEAD_DIM)
        prev = jnp.concatenate([jnp.zeros_like(cur[:, :1]), cur[:, :-1]], axis=1)
        return jnp.concatenate([prev, cur], axis=2)

    kb, vb = band(k), band(v)
    scale = HEAD_DIM ** -0.5
    s = jnp.einsum('bnqkgd,bnskd->bnkgqs', qb, kb).astype(jnp.float32) * scale

    qi = jnp.arange(BLOCK)[:, None] + BLOCK
    kj = jnp.arange(2 * BLOCK)[None, :]
    dist = qi - kj
    abs_k = jnp.arange(nb)[:, None, None] * BLOCK - BLOCK + kj[None]
    valid = (dist >= 0)[None] & (dist < WINDOW)[None] & (abs_k >= 0)

    slopes = jnp.exp2(-8.0 * jnp.arange(1, N_Q_HEADS + 1, dtype=jnp.float32) / N_Q_HEADS)
    slopes = slopes.reshape(N_KV_HEADS, GROUP)
    alibi = -slopes[:, :, None, None] * dist.astype(jnp.float32)[None, None]

    s = jnp.where(valid[None, :, None, None], s + alibi[None, None], -jnp.inf)
    sink = sinks.astype(jnp.float32).reshape(N_KV_HEADS, GROUP)[None, None, :, :, None, None]
    m = jnp.maximum(jnp.max(s, axis=-1, keepdims=True), sink)
    p = jnp.exp(s - m)
    denom = jnp.sum(p, axis=-1, keepdims=True) + jnp.exp(sink - m)
    p = (p / denom).astype(v.dtype)
    o = jnp.einsum('bnkgqs,bnskd->bnqkgd', p, vb)
    return o.reshape(bsz, seq, ATT_WIDTH)

def swa_layer(x, k, v, norm_g, w_in, q_norm_g, sinks, w_out):
    bsz, seq, _ = x.shape
    h = rmsnorm(x, norm_g)
    u = h @ w_in
    q, gate = u[..., :ATT_WIDTH], u[..., ATT_WIDTH:]
    q = rmsnorm(q.reshape(bsz, seq, N_Q_HEADS, HEAD_DIM), q_norm_g)
    o = sliding_window_sink_attention(q, k, v, sinks)
    y = o * jax.nn.silu(gate)
    return x + y @ w_out

def first_inputs(seed: int = 0) -> dict:
    key = jax.random.key(seed)
    ks = jax.random.split(key, 20)
    nA, nB, R, D = N_A_LAYERS, N_B_LAYERS, LRU_WIDTH, D_MODEL
    f32 = jnp.float32
    nrm = lambda k, shape, s: jax.random.normal(k, shape, f32) * s
    x = jax.random.normal(ks[0], (BATCH, SEQ, D), f32)
    a_norm_g = 1.0 + nrm(ks[1], (nA, D), 0.02)
    a_w_in = nrm(ks[2], (nA, D, 2 * R), D ** -0.5)
    a_conv_w = nrm(ks[3], (nA, CONV_WIDTH, R), CONV_WIDTH ** -0.5)
    a_conv_b = nrm(ks[4], (nA, R), 0.01)
    a_gate_r_w = nrm(ks[5], (nA, LRU_BLOCKS, LRU_BLOCK_W, LRU_BLOCK_W), LRU_BLOCK_W ** -0.5)
    a_gate_r_b = nrm(ks[6], (nA, R), 0.01)
    a_gate_i_w = nrm(ks[7], (nA, LRU_BLOCKS, LRU_BLOCK_W, LRU_BLOCK_W), LRU_BLOCK_W ** -0.5)
    a_gate_i_b = nrm(ks[8], (nA, R), 0.01)
    a8 = jax.random.uniform(ks[9], (nA, R), f32, 0.9, 0.999)
    a0 = a8 ** (1.0 / LRU_C)
    a_lambda = jnp.log(a0) - jnp.log1p(-a0)
    a_w_out = nrm(ks[10], (nA, R, D), R ** -0.5)
    kv_norm_g = 1.0 + nrm(ks[11], (D,), 0.02)
    w_kv = nrm(ks[12], (D, 2 * N_KV_HEADS * HEAD_DIM), D ** -0.5)
    k_norm_g = 1.0 + nrm(ks[13], (HEAD_DIM,), 0.02)
    b_norm_g = 1.0 + nrm(ks[14], (nB, D), 0.02)
    b_w_in = nrm(ks[15], (nB, D, 2 * ATT_WIDTH), D ** -0.5)
    q_norm_g = 1.0 + nrm(ks[16], (nB, HEAD_DIM), 0.02)
    sinks = nrm(ks[17], (nB, N_Q_HEADS), 0.5)
    b_w_out = nrm(ks[18], (nB, ATT_WIDTH, D), ATT_WIDTH ** -0.5)
    return {"x": x, "a_norm_g": a_norm_g, "a_w_in": a_w_in, "a_conv_w": a_conv_w,
            "a_conv_b": a_conv_b, "a_gate_r_w": a_gate_r_w, "a_gate_r_b": a_gate_r_b,
            "a_gate_i_w": a_gate_i_w, "a_gate_i_b": a_gate_i_b, "a_lambda": a_lambda,
            "a_w_out": a_w_out, "kv_norm_g": kv_norm_g, "w_kv": w_kv, "k_norm_g": k_norm_g,
            "b_norm_g": b_norm_g, "b_w_in": b_w_in, "q_norm_g": q_norm_g, "sinks": sinks,
            "b_w_out": b_w_out}

def first_block(x, a_norm_g, a_w_in, a_conv_w, a_conv_b, a_gate_r_w, a_gate_r_b,
              a_gate_i_w, a_gate_i_b, a_lambda, a_w_out, kv_norm_g, w_kv, k_norm_g,
              b_norm_g, b_w_in, q_norm_g, sinks, b_w_out):
    bsz, seq, _ = x.shape
    k = v = None
    for layer in range(DEPTH):
        if layer < N_A_LAYERS:
            l = layer
            x = rglru_layer(x, a_norm_g[l], a_w_in[l], a_conv_w[l], a_conv_b[l],
                            a_gate_r_w[l], a_gate_r_b[l], a_gate_i_w[l], a_gate_i_b[l],
                            a_lambda[l], a_w_out[l])
            if layer == N_A_LAYERS - 1:
                kv = rmsnorm(x, kv_norm_g) @ w_kv
                kv = kv.reshape(bsz, seq, 2, N_KV_HEADS, HEAD_DIM)
                k = rmsnorm(kv[:, :, 0], k_norm_g)
                v = kv[:, :, 1]
        else:
            l = layer - N_A_LAYERS
            x = swa_layer(x, k, v, b_norm_g[l], b_w_in[l], q_norm_g[l], sinks[l], b_w_out[l])
    return x


DEPTH_2 = 1

H_NSA = 4
H_DIL = 6
H_SB = 6
DIL_PAIRS = ((128, 1), (512, 4), (2048, 16))
N_DIL_GROUPS = len(DIL_PAIRS)
H_PER_DIL = H_DIL // N_DIL_GROUPS
CMP_LEN = 32
CMP_STRIDE = 16
CMP_HIDDEN = 128
SEL_BLOCK = 64
SEL_TOPK = 16
WIN_NSA = 512
Q_BLOCK = 128
D_FF = 4 * D_MODEL
N_SOFTMAX_HEADS = H_NSA + H_DIL
RMS_EPS = 1e-6
NEG_INF = -1e30
FORCE_BONUS = 1e4

NSA_Q_W = H_NSA * HEAD_DIM
NSA_KV_W = 6 * HEAD_DIM
NSA_GATE_W = 3 * H_NSA
DIL_W = 3 * H_DIL * HEAD_DIM
SB_W = 3 * H_SB * HEAD_DIM
D_PROJ = NSA_Q_W + NSA_KV_W + NSA_GATE_W + DIL_W + SB_W
PROJ_SPLITS = (NSA_Q_W, NSA_Q_W + NSA_KV_W, NSA_Q_W + NSA_KV_W + NSA_GATE_W,
               NSA_Q_W + NSA_KV_W + NSA_GATE_W + DIL_W)
D_CAT = (H_NSA + H_PER_DIL + H_SB) * HEAD_DIM


def rms_norm(x, g):
    xf = x.astype(jnp.float32)
    y = xf * lax.rsqrt(jnp.mean(xf * xf, axis=-1, keepdims=True) + RMS_EPS)
    return (y * g.astype(jnp.float32)).astype(x.dtype)

def alibi_slopes():
    i = jnp.arange(1, N_SOFTMAX_HEADS + 1, dtype=jnp.float32)
    return jnp.exp2(-8.0 * i / N_SOFTMAX_HEADS)

def masked_softmax(s, mask):
    s = jnp.where(mask, s, NEG_INF)
    m = jnp.max(s, axis=-1, keepdims=True)
    p = jnp.where(mask, jnp.exp(s - m), 0.0)
    l = jnp.maximum(jnp.sum(p, axis=-1, keepdims=True), 1e-30)
    return p / l, (m + jnp.log(l))[..., 0]

def unblock(y):
    y = jnp.moveaxis(y, 0, 1)
    return y.reshape((y.shape[0], y.shape[1] * y.shape[2]) + y.shape[3:])

def nsa_mixer(q, kv, gate_logits, qk_gain, cmp_pe, cmp_w1, cmp_w2, slopes):
    B, S = q.shape[0], q.shape[1]
    dt = q.dtype
    scale = HEAD_DIM ** -0.5
    q = rms_norm(q, qk_gain[0])
    k_sel = rms_norm(kv[:, :, 2], qk_gain[2])
    v_sel = kv[:, :, 3]
    k_win = rms_norm(kv[:, :, 4], qk_gain[3])
    v_win = kv[:, :, 5]
    n_cmp = (S - CMP_LEN) // CMP_STRIDE + 1
    cmp_start = CMP_STRIDE * jnp.arange(n_cmp)
    cmp_end = cmp_start + CMP_LEN - 1
    cmp_idx = cmp_start[:, None] + jnp.arange(CMP_LEN)[None]
    raw = kv[:, :, 0:2].transpose(0, 2, 1, 3)[:, :, cmp_idx]
    raw = (raw + cmp_pe[None, :, None]).reshape(B, 2, n_cmp, CMP_LEN * HEAD_DIM)
    hid = jax.nn.gelu(jnp.einsum('bcnf,cfh->bcnh', raw, cmp_w1))
    kv_c = jnp.einsum('bcnh,chd->bcnd', hid, cmp_w2)
    k_c = rms_norm(kv_c[:, 0], qk_gain[1])
    v_c = kv_c[:, 1]
    n_sel = S // SEL_BLOCK
    sel_start = SEL_BLOCK * jnp.arange(n_sel)
    overlap = ((cmp_start[:, None] <= sel_start[None] + SEL_BLOCK - 1)
               & (cmp_end[:, None] >= sel_start[None])).astype(jnp.float32)
    k_top = min(SEL_TOPK, n_sel)
    sel_offsets = jnp.arange(SEL_BLOCK)
    sel_ids = jnp.arange(n_sel)
    k_win_p = jnp.pad(k_win, ((0, 0), (WIN_NSA, 0), (0, 0)))
    v_win_p = jnp.pad(v_win, ((0, 0), (WIN_NSA, 0), (0, 0)))
    win_offsets = jnp.arange(WIN_NSA + Q_BLOCK)
    gates = jax.nn.sigmoid(gate_logits.astype(jnp.float32)).astype(dt)
    gather_rows = jax.vmap(lambda a, i: a[i])

    def block(n):
        t0 = n * Q_BLOCK
        t = t0 + jnp.arange(Q_BLOCK)
        qb = lax.dynamic_slice_in_dim(q, t0, Q_BLOCK, axis=1)
        d_c = (t[:, None] - cmp_end[None]).astype(jnp.float32)
        s = jnp.einsum('bqhd,bnd->bhqn', qb, k_c).astype(jnp.float32) * scale - slopes[:, None, None] * d_c
        p_c, _ = masked_softmax(s, d_c >= 0)
        o_c = jnp.einsum('bhqn,bnd->bqhd', p_c.astype(dt), v_c)
        imp = jnp.einsum('bhqn,nj->bqj', p_c, overlap)
        cur = t // SEL_BLOCK
        forced = (sel_ids[None] == 0) | (sel_ids[None] == cur[:, None]) | (sel_ids[None] == cur[:, None] - 1)
        imp = jnp.where(forced, imp + FORCE_BONUS, imp)
        imp = jnp.where(sel_start[None] <= t[:, None], imp, NEG_INF)
        _, top = lax.top_k(imp, k_top)
        tok = (top[..., None] * SEL_BLOCK + sel_offsets).reshape(B, Q_BLOCK, k_top * SEL_BLOCK)
        k_g = gather_rows(k_sel, tok)
        v_g = gather_rows(v_sel, tok)
        d_s = (t[None, :, None] - tok).astype(jnp.float32)
        s = jnp.einsum('bqhd,bqkd->bhqk', qb, k_g).astype(jnp.float32) * scale - slopes[None, :, None, None] * d_s[:, None]
        p_s, _ = masked_softmax(s, (d_s >= 0)[:, None])
        o_s = jnp.einsum('bhqk,bqkd->bqhd', p_s.astype(dt), v_g)
        k_w = lax.dynamic_slice_in_dim(k_win_p, t0, WIN_NSA + Q_BLOCK, axis=1)
        v_w = lax.dynamic_slice_in_dim(v_win_p, t0, WIN_NSA + Q_BLOCK, axis=1)
        kpos = t0 - WIN_NSA + win_offsets
        d_w = (t[:, None] - kpos[None]).astype(jnp.float32)
        mask_w = (d_w >= 0) & (d_w < WIN_NSA) & (kpos[None] >= 0)
        s = jnp.einsum('bqhd,bkd->bhqk', qb, k_w).astype(jnp.float32) * scale - slopes[:, None, None] * d_w
        p_w, _ = masked_softmax(s, mask_w)
        o_w = jnp.einsum('bhqk,bkd->bqhd', p_w.astype(dt), v_w)
        g = lax.dynamic_slice_in_dim(gates, t0, Q_BLOCK, axis=1)
        return g[..., 0:1] * o_c + g[..., 1:2] * o_s + g[..., 2:3] * o_w

    return unblock(lax.map(block, jnp.arange(S // Q_BLOCK)))

def dilated_mixer(qkv, qk_gain, slopes):
    S = qkv.shape[1]
    dt = qkv.dtype
    scale = HEAD_DIM ** -0.5
    q = rms_norm(qkv[:, :, 0], qk_gain[0])
    k = rms_norm(qkv[:, :, 1], qk_gain[1])
    v = qkv[:, :, 2]
    k_groups = [k[:, :, g] for g in range(N_DIL_GROUPS)]
    v_groups = [v[:, :, g] for g in range(N_DIL_GROUPS)]
    slopes_g = slopes.reshape(N_DIL_GROUPS, H_PER_DIL)

    def block(n):
        t0 = n * Q_BLOCK
        t = t0 + jnp.arange(Q_BLOCK)
        qb = lax.dynamic_slice_in_dim(q, t0, Q_BLOCK, axis=1)
        outs, lses = [], []
        for g, (w, r) in enumerate(DIL_PAIRS):
            dist = r * jnp.arange(w // r + 1)
            kidx = t[:, None] - dist[None]
            valid = kidx >= 0
            kidx = jnp.maximum(kidx, 0)
            k_g = k_groups[g][:, kidx]
            v_g = v_groups[g][:, kidx]
            s = (jnp.einsum('bqhd,bqjhd->bhqj', qb[:, :, g], k_g).astype(jnp.float32) * scale
                 - slopes_g[g][:, None, None] * dist.astype(jnp.float32))
            p, lse = masked_softmax(s, valid)
            outs.append(jnp.einsum('bhqj,bqjhd->bqhd', p.astype(dt), v_g))
            lses.append(lse)
        alpha = jax.nn.softmax(jnp.stack(lses), axis=0)
        alpha = jnp.transpose(alpha, (0, 1, 3, 2))[..., None].astype(dt)
        return jnp.sum(alpha * jnp.stack(outs), axis=0)

    return unblock(lax.map(block, jnp.arange(S // Q_BLOCK)))

def stick_breaking_mixer(qkv):
    S = qkv.shape[1]
    dt = qkv.dtype
    scale = HEAD_DIM ** -0.5
    q, k, v = qkv[:, :, 0], qkv[:, :, 1], qkv[:, :, 2]
    kpos = jnp.arange(S)

    def block(n):
        t0 = n * Q_BLOCK
        t = t0 + jnp.arange(Q_BLOCK)
        qb = lax.dynamic_slice_in_dim(q, t0, Q_BLOCK, axis=1)
        z = jnp.einsum('bqhd,bshd->bhqs', qb, k).astype(jnp.float32) * scale
        causal = kpos[None] < t[:, None]
        log_beta = jax.nn.log_sigmoid(z)
        log_fail = jnp.where(causal, jax.nn.log_sigmoid(-z), 0.0)
        after = lax.cumsum(log_fail, axis=3, reverse=True) - log_fail
        a = jnp.where(causal, jnp.exp(log_beta + after), 0.0)
        return jnp.einsum('bhqs,bshd->bqhd', a.astype(dt), v)

    return unblock(lax.map(block, jnp.arange(S // Q_BLOCK)))

def second_inputs(seed: int = 0) -> dict:
    key = jax.random.key(seed)
    ks = jax.random.split(key, 12)
    f32 = jnp.float32

    def nrm(k, shape, fan_in):
        return jax.random.normal(k, shape, f32) * (fan_in ** -0.5)

    def gain(k, shape):
        return 1.0 + 0.02 * jax.random.normal(k, shape, f32)

    return {
        'x': jax.random.normal(ks[0], (BATCH, SEQ, D_MODEL), f32),
        'norm_mix': gain(ks[1], (DEPTH_2, D_MODEL)),
        'norm_mlp': gain(ks[2], (DEPTH_2, D_MODEL)),
        'w_in': nrm(ks[3], (DEPTH_2, D_MODEL, D_PROJ), D_MODEL),
        'qk_gain_nsa': gain(ks[4], (DEPTH_2, 4, HEAD_DIM)),
        'qk_gain_dil': gain(ks[5], (DEPTH_2, 2, HEAD_DIM)),
        'cmp_pe': 0.1 * jax.random.normal(ks[6], (DEPTH_2, 2, CMP_LEN, HEAD_DIM), f32),
        'cmp_w1': nrm(ks[7], (DEPTH_2, 2, CMP_LEN * HEAD_DIM, CMP_HIDDEN), CMP_LEN * HEAD_DIM),
        'cmp_w2': nrm(ks[8], (DEPTH_2, 2, CMP_HIDDEN, HEAD_DIM), CMP_HIDDEN),
        'w_out': nrm(ks[9], (DEPTH_2, D_CAT, D_MODEL), D_CAT),
        'w_up': nrm(ks[10], (DEPTH_2, D_MODEL, D_FF), D_MODEL),
        'w_down': nrm(ks[11], (DEPTH_2, D_FF, D_MODEL), D_FF),
    }

def second_block(x, norm_mix, norm_mlp, w_in, qk_gain_nsa, qk_gain_dil, cmp_pe, cmp_w1, cmp_w2,
              w_out, w_up, w_down):
    B, S, _ = x.shape
    slopes = alibi_slopes()
    slopes_dil = slopes[:H_DIL]
    slopes_nsa = slopes[H_DIL:]
    for l in range(DEPTH_2):
        h = rms_norm(x, norm_mix[l])
        proj = h @ w_in[l]
        a_q, a_kv, a_g, b_qkv, c_qkv = jnp.split(proj, PROJ_SPLITS, axis=-1)
        o_a = nsa_mixer(a_q.reshape(B, S, H_NSA, HEAD_DIM), a_kv.reshape(B, S, 6, HEAD_DIM),
                        a_g.reshape(B, S, H_NSA, 3), qk_gain_nsa[l], cmp_pe[l], cmp_w1[l],
                        cmp_w2[l], slopes_nsa)
        o_b = dilated_mixer(b_qkv.reshape(B, S, 3, N_DIL_GROUPS, H_PER_DIL, HEAD_DIM),
                            qk_gain_dil[l], slopes_dil)
        o_c = stick_breaking_mixer(c_qkv.reshape(B, S, 3, H_SB, HEAD_DIM))
        cat = jnp.concatenate([o_a.reshape(B, S, -1), o_b.reshape(B, S, -1),
                               o_c.reshape(B, S, -1)], axis=-1)
        x = x + cat @ w_out[l]
        h = rms_norm(x, norm_mlp[l])
        x = x + jnp.square(jax.nn.relu(h @ w_up[l])) @ w_down[l]
    return x


def setup_inputs(seed=0):
    out = dict(first_inputs(seed))
    for name, value in second_inputs(seed + 1).items():
        if name != "x":
            out[name + "_2"] = value
    return out


def reference(
    x, a_norm_g, a_w_in, a_conv_w, a_conv_b, a_gate_r_w, a_gate_r_b, a_gate_i_w, a_gate_i_b,
    a_lambda, a_w_out, kv_norm_g, w_kv, k_norm_g, b_norm_g, b_w_in, q_norm_g, sinks, b_w_out,
    norm_mix_2, norm_mlp_2, w_in_2, qk_gain_nsa_2, qk_gain_dil_2, cmp_pe_2, cmp_w1_2, cmp_w2_2,
    w_out_2, w_up_2, w_down_2,
):
    x = first_block(
        x, a_norm_g, a_w_in, a_conv_w, a_conv_b, a_gate_r_w, a_gate_r_b, a_gate_i_w, a_gate_i_b,
        a_lambda, a_w_out, kv_norm_g, w_kv, k_norm_g, b_norm_g, b_w_in, q_norm_g, sinks,
        b_w_out,
    )
    return second_block(
        x, norm_mix_2, norm_mlp_2, w_in_2, qk_gain_nsa_2, qk_gain_dil_2, cmp_pe_2, cmp_w1_2,
        cmp_w2_2, w_out_2, w_up_2, w_down_2,
    )


_drawn_inputs = setup_inputs


def setup_inputs(seed=0):
    import zlib

    import numpy as np

    out = dict(_drawn_inputs(seed))
    spreads = {}
    factors = {'a_norm_g': 4.885,
     'a_gate_r_b': 8.0,
     'a_gate_i_b': 8.0,
     'kv_norm_g': 8.0,
     'k_norm_g': 8.0,
     'b_norm_g': 8.0,
     'q_norm_g': 8.0,
     'sinks': 27.627,
     'norm_mix_2': 18.774,
     'norm_mlp_2': 27.88,
     'qk_gain_nsa_2': 40.587,
     'qk_gain_dil_2': 53.004,
     'cmp_pe_2': 24.816}
    for name, (base, spread) in spreads.items():
        noise = np.random.default_rng([zlib.crc32(name.encode()), seed]).standard_normal(out[name].shape)
        drawn = base * np.exp(spread * noise) if base else spread * noise
        out[name] = jnp.asarray(drawn.astype(out[name].dtype))
    for name, factor in factors.items():
        out[name] = (out[name] * factor).astype(out[name].dtype)
    return out
```

```python
from contextlib import ExitStack

import numpy as np

import concourse.bass as bass
from concourse import mybir

F32 = mybir.dt.float32
F32R = mybir.dt.float32r
ALU = mybir.AluOpType
ACT = mybir.ActivationFunctionType
AX = mybir.AxisListType

P = 128
D = 1024
S = 512
KD = D // P
TB = S // P
R = 1536
RT = R // P
NG = 4
HD = 64
EPS = 1e-6
BIG = 1e30
UNIT = 1024
RING = 4
GATE_TILES = [(0, 0), (1, 0), (0, 1), (1, 1), (2, 1), (1, 2), (2, 2)]

U_RG = 0
U_WOUT = U_RG + 8 * NG
U_KV = U_WOUT + RT
U_GA = U_KV + 2
U_Q0 = U_GA + 2
U_GB = U_Q0 + 4
U_Q1 = U_GB + 3
U_GC = U_Q1 + 4
U_BOUT = U_GC + 3
U_G0 = U_BOUT + 8
U_G1 = U_G0 + 4
U_F0 = U_G1 + 4
U_G2 = U_F0 + 1
U_F1 = U_G2 + 4
U_W1 = U_F1 + 6
U_G3 = U_W1 + 4
U_G4 = U_G3 + 4
U_OUT2 = U_G4 + 4
U_MLP = U_OUT2 + 8
MLP_CHUNKS = 4
UNITS = U_MLP + 16 * MLP_CHUNKS

NRG = 9
PC = {}
_at = 0
for _name, _n in [("rg", NG * 3 * NRG), ("g_a", KD), ("g_kv", KD), ("g_b", KD), ("g_mix", KD), ("g_mlp", KD),
                  ("q", 1), ("k", 1), ("nsa", 4), ("dil", 2), ("sinks", 16), ("pe", 32), ("w2", 2 * HD)]:
    PC[_name] = _at
    _at += _n
NPAR = _at

A_P = 0
A_QRAW, A_SQH = 0, 2048
A_QT, A_KT, A_VS, A_SG = 4096, 8192, 9216, 9728
A_OT, A_BIAS, A_TAB = 13824, 14848, 16128
A_SWA = A_BIAS + 768
A_HID, A_KCR, A_KCD = A_BIAS + 1024, A_BIAS + 1088, A_BIAS + 1152
A_RG = A_OT
A_END = A_TAB + 2432
A_PT1, A_PT2 = 1024, 5120
A_R0, A_R1, A_R2, A_SQG, A_CT, A_RAW, A_ST = 0, 1536, 3072, 4608, 6144, 6656, 7680
A_VD, A_VST, A_VN, A_QN, A_KN = 8192, 9728, 11264, 11776, 12800
T_D0, T_D1, T_D2, T_DC, T_STK, T_CMP = 0, 256, 768, 1280, 1792, 2304
NTAB = 2432


def plan():
    seg1 = [("wout", m, "X") for m in range(8)] + [("kv", t, "A") for t in range(4)] + [("ssq", 1, "N")]
    seg1 += [("gate", 0, "D"), ("gate", 1, "D"), ("rstd", 1, "B")] + [("q0", t, "A") for t in range(4)]
    seg1 += [("gate", j, "D") for j in (2, 3, 4)] + [("kT", j, "A") for j in range(2)]
    seg1 += [("qT", j, "A") for j in range(4)] + [("q1", t, "A") for t in range(4)]
    seg1 += [("gate", j, "D") for j in (5, 6, 7)] + [("qT", j, "A") for j in range(4, 8)]
    seg2 = [("bout", m, "X") for m in range(8)] + [("G0", t, "A") for t in range(4)] + [("ssq", 2, "N")]
    seg2 += [("G1", t, "A") for t in range(4)] + [("rstd", 2, "B"), ("F", 0, "D")]
    seg2 += [("G2", t, "A") for t in range(4)] + [("F", j, "D") for j in range(1, 7)]
    seg2 += [("hid", 0, "A"), ("hid", 1, "A")] + [("G3", t, "A") for t in range(4)] + [("kc", 0, "A")]
    seg2 += [("G4", t, "A") for t in range(4)] + [("nT", j, "A") for j in range(4)]
    seg2 += [("dT", j, "D") for j in range(6)] + [("kcT", 0, "A")]
    bank, free, before = {}, {}, {}
    count = {"A": 0, "D": 0}
    for seg in (seg1, seg2):
        for i, (name, j, who) in enumerate(seg):
            key = (name, j)
            bank[key] = i % 8
            if who in count:
                count[who] += 1
                free[key] = (who, count[who])
            elif who == "X":
                free[key] = (who, j + 1 + (8 if name == "bout" else 0))
            else:
                free[key] = (who, j + 1)
            before[key] = free[seg[i - 8][:2]] if i >= 8 else None
    return bank, free, before


def attention_one():
    batches = [dict(kind="swa", head=h, pair=h // 2, half=h % 2, last=h % 2 == 1) for h in range(16)]
    groups = [dict(b=h, n=n, w=[128 if n == 0 else 256]) for h in range(16) for n in range(TB)]
    return batches, groups


def attention_two():
    batches = []
    for h in range(4):
        for x, kind in enumerate(("cmp", "sel", "win")):
            batches.append(dict(kind=kind, head=h, x=x, pair=h // 2, half=h % 2, last=(h % 2 == 1 and x == 2)))
    batches += [dict(kind="dil", head=h, pair=2, half=h, last=h == 1) for h in range(2)]
    batches += [dict(kind="stick", head=h, pair=3 + h // 2, half=h % 2, last=h % 2 == 1) for h in range(6)]
    groups = []
    for b, batch in enumerate(batches):
        for n in range(TB):
            full = (n + 1) * P
            w = {"cmp": [32], "dil": [min(full, 256), full, full]}.get(batch["kind"], [full])
            groups.append(dict(b=b, n=n, w=w))
    return batches, groups


def with_chunks(groups, batches, per_chunk):
    strip = chunk = 0
    for g in groups:
        g["strip0"] = strip
        strip += len(g["w"])
        kind = batches[g["b"]]["kind"]
        blocks, col = [], 0
        for s, w in enumerate(g["w"]):
            for c in range(0, w, P):
                blocks.append((s, col + c, c // P, 31 if kind == "cmp" else P))
            col += w
        g["chunks"] = [(chunk + i, blocks[c:c + per_chunk]) for i, c in enumerate(range(0, len(blocks), per_chunk))]
        chunk += len(g["chunks"])
    return groups


def two_block_kernel(nc, x_d, weights_d, params_d, tables_d, swa_d, ident_d, out_d):
    BANK, FREE, BEFORE = plan()
    ctx = ExitStack()
    with ctx:
        def sb(name, shape, dt=F32):
            return ctx.enter_context(nc.sbuf_tensor(name, shape, dt))

        def sem(name):
            return ctx.enter_context(nc.semaphore(name))

        x = sb("x", [P, KD, S])
        raw = sb("raw", [P, RING, UNIT])
        wh = sb("wh", [P, RING, UNIT], F32R)
        wl = sb("wl", [P, RING, UNIT], F32R)
        yh = sb("yh", [P, RT, S], F32R)
        yl = sb("yl", [P, RT, S], F32R)
        xh = sb("xh", [P, KD, S], F32R)
        xl = sb("xl", [P, KD, S], F32R)
        arena = sb("arena", [P, A_END])
        par = sb("par", [P, NPAR])
        ident = sb("ident", [P, P])
        ones = sb("ones", [P, P])
        rstd = sb("rstd", [P, S])
        rx = sb("rx", [P, TB])
        v4 = sb("v4", [P, 3, 72])
        rx2 = sb("rx2", [P, TB])
        hold = sb("hold", [P, 2])
        hsc = sb("hsc", [P, 3])
        gates = sb("gates", [P, TB, 12])
        negm = sb("negm", [P, 4, TB])
        rsum = sb("rsum", [P, 4, TB, 3])
        esink = sb("esink", [P, 2, TB])
        mtmp = sb("mtmp", [P, 2])
        den = sb("den", [P, TB])
        kcT = sb("kcT", [P, 32])
        vc = sb("vc", [P, HD])
        skc = sb("skc", [P, 1])
        B = [ctx.enter_context(nc.psum_tensor(f"bank{i}", [P, 512], F32)) for i in range(8)]

        def ar(at, *shape):
            n = int(np.prod(shape))
            v = arena[:, at:at + n]
            if len(shape) == 2:
                v = v.rearrange("p (a b) -> p a b", a=shape[0])
            if len(shape) == 3:
                v = v.rearrange("p (a b c) -> p a b c", a=shape[0], b=shape[1])
            return v

        gp = ar(A_RG, 3, NRG)
        sp = ar(A_RG + 3 * NRG, 4, NG * 3)
        hid, kcr, kcd = ar(A_HID, 2, 32), ar(A_KCR, HD), ar(A_KCD, P)
        tmpo = rstd[:, 0:TB * HD].rearrange("p (t d) -> p t d", t=TB)

        def head_view(i, n):
            return v4[:, i, 0:TB * n].rearrange("p (t h) -> p t h", t=TB)

        loaded = [sem(f"raw_loaded{i}") for i in range(RING)]
        held = sem("unit_held")
        high_done = sem("high_done")
        split_done = sem("split_done")
        units_done = sem("units_done")
        in_x, in_par, in_tab = sem("in_x"), sem("in_par"), sem("in_tab")
        ones_set = sem("ones_set")
        sq_ready = sem("sq_ready")
        ssq_read = sem("ssq_read")
        root_ask, root_done = sem("root_ask"), sem("root_done")
        rx_ready = sem("rx_ready")
        diag_ready = sem("diag_ready")
        rstd_ready = sem("rstd_ready")
        xh_ready = sem("xh_ready")
        xl_ready = sem("xl_ready")
        x_new = sem("x_new")
        dve_step = sem("dve_step")
        rg_high = sem("rg_high")
        xb_evac, gate_evac, xc_ready = sem("xb_evac"), sem("gate_evac"), sem("xc_ready")
        sig_done, decay_done = sem("sig_done"), sem("decay_done")
        var_ready, var_root, y_ready = sem("var_ready"), sem("var_root"), sem("y_ready")
        pe_misc = sem("pe_misc")
        evac_a, evac_d = sem("evac_act"), sem("evac_dve")
        heads_raw = sem("heads_raw")
        heads_summed = sem("heads_summed")
        heads_normed = sem("heads_normed")
        silu_done = sem("silu_done")
        lam_ask, lam_done = sem("lam_ask"), sem("lam_done")
        dil_high = sem("dil_high")
        cmp_ready = sem("cmp_ready")
        up_read, up_sq, ff_ready = sem("up_read"), sem("up_squared"), sem("ff_ready")
        down_read = sem("down_read")
        stored = sem("stored")
        FREESEM = {"A": evac_a, "D": evac_d, "X": x_new, "N": ssq_read, "B": rstd_ready}

        att = {}
        for a in (1, 2):
            att[a] = {n: sem(f"{n}{a}") for n in (
                "scores", "strip_read", "masked", "soft1", "soft2", "probs", "pt_ready", "pt_even", "pt_odd",
                "o_done", "fin", "pairT", "pair_done", "esum")}

        block = ctx.enter_context(nc.Block())

        done = {}
        misc = [0]

        def by_misc(key):
            misc[0] += 1
            done[key] = (pe_misc, misc[0])

        by_misc(("ssq", 0))
        by_misc(("rstd", 0))
        for m in range(7):
            by_misc(("wout", m))
        done[("wout", 7)] = (units_done, U_KV)
        for t in range(4):
            done[("kv", t)] = (units_done, U_GA)
            done[("q0", t)] = (units_done, U_GB)
            done[("q1", t)] = (units_done, U_GC)
            done[("G0", t)] = (units_done, U_G1)
            done[("G1", t)] = (units_done, U_F0)
            done[("G2", t)] = (units_done, U_F1)
            done[("G3", t)] = (units_done, U_G4)
            done[("G4", t)] = (units_done, U_OUT2)
        for j in range(8):
            u = U_GA + j if j < 2 else U_GB + j - 2 if j < 5 else U_GC + j - 5
            done[("gate", j)] = (units_done, u + 1)
            done[("bout", j)] = (units_done, U_BOUT + j + 1)
            done[("out2", j)] = (units_done, U_OUT2 + j + 1)
        for j in range(7):
            done[("F", j)] = (units_done, (U_F0 if j == 0 else U_F1 + j - 1) + 1)
        done[("hid", 0)] = done[("hid", 1)] = (units_done, U_G3)
        for key in ([("ssq", 1), ("rstd", 1), ("kT", 0), ("kT", 1)] + [("qT", j) for j in range(8)]
                    + [("ssq", 2), ("rstd", 2), ("kc", 0)] + [("nT", j) for j in range(4)]
                    + [("dT", j) for j in range(6)] + [("kcT", 0), ("ssq", 3), ("rstd", 3)]):
            by_misc(key)

        def wait_done(eng, key):
            eng.wait_ge(*done[key])

        NORM_UNITS = {0: "g_a", 1: "g_b", 2: "g_mix", 3: "g_mlp"}

        @block.sync
        def _(sp_):
            sp_.dma_start(x[:], x_d).then_inc(in_x, 16)

            def load(j, ahead, u):
                if ahead is not None:
                    sp_.wait_ge(split_done, ahead)
                sp_.dma_start(raw[:, j, :], weights_d[u].rearrange("a p n -> (a p) n")).then_inc(loaded[j], 16)

            load(0, None, bass.ds(0, 1))
            sp_.dma_start(par[:], params_d).then_inc(in_par, 16)
            sp_.dma_start(ident[:], ident_d).then_inc(in_par, 16)
            for j in range(1, RING):
                load(j, None, bass.ds(j, 1))
            sp_.dma_start(ar(A_TAB, NTAB), tables_d).then_inc(in_tab, 16)
            sp_.dma_start(ar(A_SWA, 256), swa_d).then_inc(in_tab, 16)
            with sp_.Fori(1, UNITS // RING) as lap:
                for j in range(RING):
                    load(j, RING * lap + j - RING + 1, bass.ds(RING * lap + j, 1))
            for u in range(UNITS // RING * RING, UNITS):
                load(u % RING, u - RING + 1, bass.ds(u, 1))
            for m in range(KD):
                sp_.wait_ge(down_read, KD * (MLP_CHUNKS - 1) + m + 1)
                sp_.dma_start(out_d[:, m, :], x[:, m, :]).then_inc(stored, 16)
            sp_.wait_ge(stored, 16 * KD)

        @block.gpsimd
        def _(pool):
            pool.memset(hold[:], 0.0).then_inc(held, 1)
            pool.wait_ge(held, 1)

            def split(u, j, lap, first):
                pool.wait_ge(loaded[j], 16 * lap + 16)
                if not first:
                    pool.wait_ge(units_done, u - RING + 1)
                pool.tensor_tensor(hold[:], hold[:], hold[:], ALU.add).then_inc(held, 1)
                pool.tensor_scalar(wh[:, j, :], raw[:, j, :], 1.0, 1.0, ALU.mult, ALU.mult).then_inc(high_done, 1)
                pool.wait_ge(high_done, u + 1)
                pool.tensor_tensor(wl[:, j, :], raw[:, j, :], wh[:, j, :], ALU.subtract).then_inc(split_done, 1)

            for j in range(RING):
                split(j, j, 0, True)
            with pool.Fori(1, UNITS // RING) as lap:
                for j in range(RING):
                    split(RING * lap + j, j, lap, False)
            for u in range(UNITS // RING * RING, UNITS):
                split(u, u % RING, u // RING, False)

        def head_rows(h):
            return slice(HD * (h % 2), HD * (h % 2) + HD)

        qT = ar(A_QT, 8, S)
        kT2 = ar(A_KT, 2, S)
        vS = ar(A_VS, TB, P)
        sg = ar(A_SG, 8, S)
        vd, vst, vn = ar(A_VD, TB, 384), ar(A_VST, TB, 384), ar(A_VN, TB, P)
        qn, kn = ar(A_QN, 2, S), ar(A_KN, 2, S)
        otok = ar(A_OT, 2, TB, P)
        bias = ar(A_BIAS, 1280)
        tabs = ar(A_TAB, NTAB)
        LOOK = 3

        def make_attention(a):
            batches, groups = attention_one() if a == 1 else attention_two()
            width = 256 if a == 1 else 1280
            with_chunks(groups, batches, 2 if a == 1 else 4)
            probs = ar(A_P, 4, width)
            pt = ar(A_PT1, 6, 256) if a == 1 else ar(A_PT2, 6, 512)
            lterm = ar(A_BIAS, 2, 512)
            s = att[a]
            ng = len(groups)
            pairs = [i for i, g in enumerate(groups) if g["n"] == TB - 1 and batches[g["b"]]["last"]]

            def scores_ap(g, k):
                b, n = batches[g["b"]], g["n"]
                h, w, kind = b["head"], g["w"][k], b["kind"]
                rows, qs = head_rows(h), slice(n * P, (n + 1) * P)
                if kind == "swa":
                    return [(qT[rows, h // 2, qs], kT2[rows, h // 8, (n + 1) * P - w:(n + 1) * P])]
                if kind == "cmp":
                    return [(qn[rows, h // 2, qs], kcT[rows, 0:32])]
                if kind in ("sel", "win"):
                    return [(qn[rows, h // 2, qs], kn[rows, kind == "win", 0:w])]
                if kind == "dil":
                    ks = slice((n + 1) * P - w, (n + 1) * P)
                    q, kk = (xh[rows, k, qs], xl[rows, k, qs]), (xh[rows, 3 + k, ks], xl[rows, 3 + k, ks])
                else:
                    t = 6 + h // 2
                    q, kk = (yh[rows, t, qs], yl[rows, t, qs]), (yh[rows, t + 3, 0:w], yl[rows, t + 3, 0:w])
                return [(q[0], kk[0]), (q[0], kk[1]), (q[1], kk[0])]

            def value_ap(g, s_, kb, K):
                b, n = batches[g["b"]], g["n"]
                h, kind = b["head"], b["kind"]
                if kind == "swa":
                    return vS[:, n + 1 - g["w"][0] // P + kb, HD * (h // 8):HD * (h // 8) + HD]
                if kind == "cmp":
                    return vc[0:K, :]
                if kind in ("sel", "win"):
                    c = HD * (kind == "win")
                    return vn[:, kb, c:c + HD]
                if kind == "dil":
                    c = HD * (2 * s_ + h)
                    return vd[:, n + 1 - g["w"][s_] // P + kb, c:c + HD]
                return vst[:, kb, HD * h:HD * h + HD]

            def pe_part(pe):
                def scores(i):
                    g = groups[i]
                    for k, w in enumerate(g["w"]):
                        st = g["strip0"] + k
                        if st >= 3:
                            pe.wait_ge(s["strip_read"], st - 2)
                        terms = scores_ap(g, k)
                        for t, (q, kk) in enumerate(terms):
                            mm = pe.matmul(B[st % 3][:, 0:w], q, kk, start=t == 0, stop=t == len(terms) - 1)
                        mm.then_inc(s["scores"], 1)

                def turn(i):
                    g = groups[i]
                    pe.wait_ge(s["probs"], i + 1)
                    col0 = probs[:, i % 4, :]
                    for c, blocks in g["chunks"]:
                        if c >= 2:
                            pe.wait_ge(s[("pt_even", "pt_odd")[c % 2]], c // 2)
                        for j, (_, col, _, K) in enumerate(blocks):
                            mm = pe.transpose(B[3 + c % 2][0:K, j * P:(j + 1) * P], col0[:, col:col + K], ident[:])
                        mm.then_inc(s["pt_ready"], 1)

                def values(i):
                    g = groups[i]
                    b = g["b"]
                    if g["n"] == 0 and b >= 2:
                        pe.wait_ge(s["fin"], b - 1)
                    first, total = True, sum(len(bl) for _, bl in g["chunks"])
                    for c, blocks in g["chunks"]:
                        pe.wait_ge(s[("pt_even", "pt_odd")[c % 2]], c // 2 + 1)
                        for j, (s_, _, kb, K) in enumerate(blocks):
                            total -= 1
                            mm = pe.matmul(B[5 + b % 2][:, g["n"] * HD:(g["n"] + 1) * HD],
                                           pt[0:K, c % 6, j * P:(j + 1) * P], value_ap(g, s_, kb, K),
                                           start=first, stop=total == 0)
                            first = False
                    mm.then_inc(s["o_done"], 1)

                def pair_turn(p):
                    pe.wait_ge(s["fin"], groups[pairs[p]]["b"] + 1)
                    if p >= 1:
                        pe.wait_ge(s["pair_done"], p)
                    for t in range(TB):
                        mm = pe.transpose(B[7][:, t * P:(t + 1) * P], otok[:, p % 2, t, :], ident[:])
                    mm.then_inc(s["pairT"], 1)

                for i in range(-LOOK - 1, ng + 3):
                    if 0 <= i + LOOK + 1 < ng:
                        scores(i + LOOK + 1)
                    if 0 <= i < ng:
                        turn(i)
                    if 0 <= i - 1 < ng:
                        values(i - 1)
                    if i - 3 in pairs:
                        pair_turn(pairs.index(i - 3))
                for p, i in enumerate(pairs):
                    if i + 3 >= ng + 3:
                        pair_turn(p)

            def act_part(act):
                def soft1(i):
                    g = groups[i]
                    b, n = batches[g["b"]], g["n"]
                    pr = probs[:, i % 4, :]
                    if b["kind"] == "stick":
                        act.wait_ge(s["masked"], stick_count(i) + 1)
                        w = g["w"][0]
                        lt = lterm[:, i % 2, 0:w]
                        act.activation(lt, lt, ACT.Exp).then_inc(s["soft1"], 1)
                        act.wait_ge(s["soft1"], stick_count(i) * 2 + 1)
                        act.activation(lt, lt, ACT.Ln, bias=1.0).then_inc(s["soft1"], 1)
                        return
                    act.wait_ge(s["strip_read"], g["strip0"] + len(g["w"]))
                    col = 0
                    for k, w in enumerate(g["w"]):
                        e = act.activation(pr[:, col:col + w], pr[:, col:col + w], ACT.Exp, scale=-1.0,
                                           bias=negm[:, g["b"] % 4, n:n + 1],
                                           accum_out=rsum[:, g["b"] % 4, n, k:k + 1])
                        col += w
                    e.then_inc(s["probs"], 1)
                    if b["kind"] == "swa" and n == TB - 1:
                        if g["b"] >= 2:
                            act.wait_ge(s["fin"], g["b"] - 1)
                        act.activation(esink[:, g["b"] % 2, :], negm[:, g["b"] % 4, :], ACT.Exp, scale=1.0,
                                       bias=par[:, PC["sinks"] + b["head"]:PC["sinks"] + b["head"] + 1])\
                           .then_inc(s["esum"], 1)

                def soft2(i):
                    g = groups[i]
                    if batches[g["b"]]["kind"] != "stick":
                        return
                    act.wait_ge(s["soft2"], stick_count(i) + 1)
                    pr = probs[:, i % 4, 0:g["w"][0]]
                    act.activation(pr, pr, ACT.Exp).then_inc(s["probs"], 1)

                def copy_out(i):
                    for c, blocks in groups[i]["chunks"]:
                        if c % 2 == 1:
                            pt_copy(act, c, blocks, lambda o, i_: act.activation(o, i_, ACT.Copy))

                for i in range(-LOOK, ng + 3):
                    if 0 <= i + LOOK < ng:
                        soft1(i + LOOK)
                    if 0 <= i + LOOK - 1 < ng:
                        soft2(i + LOOK - 1)
                    if 0 <= i < ng:
                        copy_out(i)

            last_of_chunk = {c: i for i, g in enumerate(groups) for c, _ in g["chunks"]}

            def pt_copy(eng, c, blocks, copy):
                eng.wait_ge(s["pt_ready"], c + 1)
                if c >= 6:
                    eng.wait_ge(s["o_done"], last_of_chunk[c - 6] + 1)
                n, K = len(blocks) * P, blocks[0][3]
                copy(pt[0:K, c % 6, 0:n], B[3 + c % 2][0:K, 0:n]).then_inc(s[("pt_even", "pt_odd")[c % 2]], 1)

            def stick_count(i):
                return sum(1 for g in groups[:i] if batches[g["b"]]["kind"] == "stick")

            def dve_part(dve, link):
                def make_bias(b):
                    kind, h = b["kind"], b["head"]
                    if kind == "swa":
                        parts = [(A_SWA - A_TAB, 256, float(np.exp2(np.float32(-8.0 * (h + 1) / 16))))]
                    elif kind == "cmp":
                        parts = [(T_CMP, 128, slope10(6 + h))]
                    elif kind in ("sel", "win"):
                        parts = [(T_DC, 512, slope10(6 + h))]
                    else:
                        parts = [(T_D0, 256, slope10(h)), (T_D1, 512, slope10(2 + h)), (T_D2, 512, slope10(4 + h))]
                    at = 0
                    for t, w, slope in parts:
                        last = dve.tensor_scalar(bias[:, at:at + w], ar(A_TAB + t, w), -slope, None, ALU.mult)
                        at += w
                    link(last)

                def mask1(i):
                    g = groups[i]
                    b, n = batches[g["b"]], g["n"]
                    kind = b["kind"]
                    if n == 0 and kind != "stick" and not (kind == "win"):
                        make_bias(b)
                    if i >= 4:
                        dve.wait_ge(s["pt_ready"], groups[i - 4]["chunks"][-1][0] + 1)
                    pr = probs[:, i % 4, :]
                    col = at = 0
                    for k, w in enumerate(g["w"]):
                        st = g["strip0"] + k
                        dve.wait_ge(s["scores"], st + 1)
                        z = B[st % 3][:, 0:w]
                        if kind == "stick":
                            dve.tensor_tensor(pr[:, 0:w], z, tabs[:, T_STK + 512 - w:T_STK + 512], ALU.add)\
                               .then_inc(s["strip_read"], 1)
                            dve.wait_ge(s["strip_read"], st + 1)
                            dve.scalar_tensor_tensor(out=lterm[:, i % 2, 0:w], in0=pr[:, 0:w], scalar=-1.0,
                                                     in1=pr[:, 0:w], op0=ALU.mult, op1=ALU.min)\
                               .then_inc(s["masked"], 1)
                            return
                        if kind == "cmp":
                            bb = bias[:, 32 * n:32 * n + 32]
                        else:
                            tw = 256 if (kind == "swa" or (kind == "dil" and k == 0)) else 512
                            bb = bias[:, at + tw - w:at + tw]
                            at += tw
                        final = k == len(g["w"]) - 1
                        out_m = negm[:, g["b"] % 4, n:n + 1] if final else mtmp[:, k:k + 1]
                        if k > 0:
                            init = mtmp[:, k - 1:k]
                        elif kind == "swa":
                            init = nsink[:, b["head"]:b["head"] + 1]
                        else:
                            init = 1e29 if kind == "cmp" else BIG
                        dve.tensor_tensor_reduce(pr[:, col:col + w], z, bb, -1.0, init, ALU.add, ALU.min, out_m)\
                           .then_inc(s["strip_read"], 1)
                        dve.wait_ge(s["strip_read"], st + 1)
                        col += w

                def mask2(i):
                    g = groups[i]
                    if batches[g["b"]]["kind"] != "stick":
                        return
                    w = g["w"][0]
                    lt, pr = lterm[:, i % 2, 0:w], probs[:, i % 4, 0:w]
                    dve.wait_ge(s["soft1"], 2 * stick_count(i) + 2)
                    link(dve.scalar_tensor_tensor(out=lt, in0=pr, scalar=0.0, in1=lt, op0=ALU.max, op1=ALU.add))
                    link(dve.tensor_tensor_scan(lt[:, ::-1], ones[:, 0:1].to_broadcast([P, w]), lt[:, ::-1],
                                                0.0, ALU.mult, ALU.add))
                    dve.tensor_tensor(pr, pr, lt, ALU.subtract).then_inc(s["soft2"], 1)

                def copy_out(i):
                    for c, blocks in groups[i]["chunks"]:
                        if c % 2 == 0:
                            pt_copy(dve, c, blocks, dve.tensor_copy)

                def finish(bi):
                    b = batches[bi]
                    kind, p = b["kind"], b["pair"]
                    if p >= 2 and not b["half"]:
                        dve.wait_ge(s["pairT"], p - 1)
                    o = B[5 + bi % 2][:, 0:TB * HD].rearrange("p (n d) -> p n d", n=TB)
                    dst = otok[:, p % 2, :, HD * b["half"]:HD * b["half"] + HD]
                    rs = rsum[:, bi % 4, :, 0]
                    if kind == "swa":
                        dve.wait_ge(s["esum"], bi + 1)
                        link(dve.tensor_tensor(den[:], rs, esink[:, bi % 2, :], ALU.add))
                    elif kind == "dil":
                        link(dve.tensor_reduce(den[:], rsum[:, bi % 4, :, :], AX.X, ALU.add))
                    elif kind != "stick":
                        link(dve.tensor_scalar(den[:], rs, 1e-30, None, ALU.max))
                    if kind != "stick":
                        link(dve.reciprocal(den[:], den[:]))
                    if kind in ("cmp", "sel", "win"):
                        link(dve.tensor_tensor(den[:], den[:], gates[:, :, 3 * b["head"] + b["x"]], ALU.mult))
                    dve.wait_ge(s["o_done"], TB * (bi + 1))
                    if kind == "stick":
                        dve.tensor_copy(dst, o).then_inc(s["fin"], 1)
                        return
                    scale = den[:].unsqueeze(2).to_broadcast([P, TB, HD])
                    if kind in ("sel", "win"):
                        link(dve.tensor_tensor(tmpo[:], o, scale, ALU.mult))
                        dve.tensor_tensor(dst, dst, tmpo[:], ALU.add).then_inc(s["fin"], 1)
                    else:
                        dve.tensor_tensor(dst, o, scale, ALU.mult).then_inc(s["fin"], 1)
                    dve.wait_ge(s["fin"], bi + 1)

                def pair_out(p):
                    dve.wait_ge(s["pairT"], p + 1)
                    if a == 1:
                        if p == 0:
                            dve.wait_ge(silu_done, 1)
                        yt = ar(A_BIAS + 256, 512)
                        dve.tensor_tensor(yt, B[7][:], sg[:, p, :], ALU.mult).then_inc(s["pair_done"], 1)
                        dve.wait_ge(s["pair_done"], p + 1)
                        link(dve.tensor_copy(yh[:, p, :], yt))
                        dve.tensor_tensor(yl[:, p, :], yt, yh[:, p, :], ALU.subtract).then_inc(y_ready, 1)
                    else:
                        link(dve.tensor_copy(yh[:, p, :], B[7][:]))
                        dve.tensor_tensor(yl[:, p, :], B[7][:], yh[:, p, :], ALU.subtract).then_inc(s["pair_done"], 1)

                for i in range(-LOOK, ng + 3):
                    if 0 <= i + LOOK < ng:
                        mask1(i + LOOK)
                    if 0 <= i + LOOK - 1 < ng:
                        mask2(i + LOOK - 1)
                    if 0 <= i < ng:
                        copy_out(i)
                    if 0 <= i - 1 < ng and groups[i - 1]["n"] == TB - 1:
                        finish(groups[i - 1]["b"])
                    if i - 3 in pairs:
                        pair_out(pairs.index(i - 3))
                for p, i in enumerate(pairs):
                    if i + 3 >= ng + 3:
                        pair_out(p)

            return pe_part, act_part, dve_part, len(pairs)

        def slope10(i):
            return float(np.exp2(np.float32(-8.0) * np.float32(i + 1) / np.float32(10)))

        nsink = sb("nsink", [P, 16])
        ATT1, ATT2 = make_attention(1), make_attention(2)

        @block.tensor
        def _(pe):
            def three(out, lh, ll, rh, rl, start, stop):
                pe.matmul(out, lh, rh, start=start, stop=False)
                pe.matmul(out, lh, rl, start=False, stop=False)
                return pe.matmul(out, ll, rh, start=False, stop=stop)

            def tile(w, j, k):
                return w[:, j, k * P:(k + 1) * P]

            def feature_major(u, j, out, ah, al, n=KD, ready=None):
                pe.wait_ge(split_done, u + 1)
                for k in range(n):
                    if ready:
                        pe.wait_ge(ready[0], ready[1] + ready[2] * k)
                    mm = three(out, tile(wh, j, k), tile(wl, j, k), ah[:, k, :], al[:, k, :], k == 0, k == n - 1)
                mm.then_inc(units_done, 1)

            def free(key):
                if BEFORE[key]:
                    who, value = BEFORE[key]
                    pe.wait_ge(FREESEM[who], value)

            def token_major(u0, units, width, name, ah, al, ready=None):
                per = KD // units
                for u in range(u0, u0 + units):
                    pe.wait_ge(split_done, u + 1)
                    for kk in range(per):
                        k = (u - u0) * per + kk
                        if ready:
                            pe.wait_ge(ready[0], ready[1] + ready[2] * k)
                        cols = slice(kk * (UNIT // per), kk * (UNIT // per) + width)
                        for t in range(TB):
                            if k == 0:
                                free((name, t))
                            ts = slice(t * P, (t + 1) * P)
                            mm = three(B[BANK[(name, t)]][:, 0:width], ah[:, k, ts], al[:, k, ts],
                                       wh[:, u % RING, cols], wl[:, u % RING, cols], k == 0, k == KD - 1)
                    mm.then_inc(units_done, 1)

            def gate_tile(j):
                u = done[("gate", j)][1] - 1
                free(("gate", j))
                feature_major(u, u % RING, B[BANK[("gate", j)]][:], xh, xl,
                              ready=(xl_ready, KD + 2, 2) if j == 0 else None)

            def sum_squares(q, bank):
                sq = ar(A_P, KD, S)
                for k in range(KD):
                    pe.wait_ge(sq_ready, KD * q + k + 1)
                    for t in range(TB):
                        mm = pe.matmul(bank[:, t:t + 1], sq[:, k, t * P:(t + 1) * P], ones[:, 0:1],
                                       start=k == 0 and t == 0, stop=k == KD - 1, skip_group_check=True)
                mm.then_inc(pe_misc, 1)

            def spread_rstd(q, bank):
                pe.wait_ge(diag_ready, q + 1)
                pe.matmul(bank[:], ones[:], ar(A_BIAS, 512), start=True, stop=True).then_inc(pe_misc, 1)

            pe.wait_ge(ones_set, 1)
            sum_squares(0, B[0])
            spread_rstd(0, B[1])

            def rg_group(g, later):
                for i in range(3):
                    if later:
                        pe.wait_ge(sig_done, 6 * g - 3 + i)
                    elif i < 2:
                        pe.wait_ge((ssq_read, rstd_ready)[i], 1)
                    feature_major(8 * g + i, i, B[i][:], xh, xl, ready=(xl_ready, 1, 1) if not later and i == 0 else None)
                for i in range(3):
                    if later:
                        if i == 0:
                            pe.wait_ge(sig_done, 6 * g)
                        else:
                            pe.wait_ge(gate_evac, 3 * g - 2 + i)
                    feature_major(8 * g + 3 + i, (3 + i) % RING, B[3 + i][:], xh, xl)
                pe.wait_ge(xc_ready, 3 * g + 3)
                for r in range(2):
                    pe.wait_ge(split_done, 8 * g + 7 + r)
                    for n, (ki, o) in enumerate(GATE_TILES):
                        bank = (6 + 3 * r + o) % 8
                        first = n == 0 or GATE_TILES[n - 1][1] != o
                        if first:
                            if bank < 3:
                                pe.wait_ge(xb_evac, 3 * g + bank + 1)
                            elif bank == 3:
                                pe.wait_ge(gate_evac, 3 * g + 1)
                            elif later:
                                pe.wait_ge(sig_done, 6 * g - 11 + bank)
                        mm = three(B[bank][:], tile(wh, 2 + r, n), tile(wl, 2 + r, n), yh[:, 9 + ki, :], yl[:, 9 + ki, :],
                                   first, n == 6 or GATE_TILES[n + 1][1] != o)
                    mm.then_inc(units_done, 1)

            rg_group(0, False)
            with pe.Fori(1, NG) as g:
                rg_group(g, True)

            pe.wait_ge(sig_done, 6 * NG)
            pe.wait_ge(gate_evac, 3 * NG)
            for k in range(9):
                u = U_WOUT + k
                pe.wait_ge(split_done, u + 1)
                pe.wait_ge(y_ready, k // 3 + 1)
                for m in range(KD):
                    mm = three(B[m][:], tile(wh, u % RING, m), tile(wl, u % RING, m), yh[:, k, :], yl[:, k, :], k == 0, False)
                mm.then_inc(units_done, 1)
            pe.wait_ge(split_done, U_WOUT + 12)
            pe.wait_ge(y_ready, NG)
            for m in range(KD):
                for k in range(9, 12):
                    u = U_WOUT + k
                    mm = three(B[m][:], tile(wh, u % RING, m), tile(wl, u % RING, m), yh[:, k, :], yl[:, k, :], False, k == 11)
                    if m == KD - 1:
                        mm.then_inc(units_done, 1)
                if m < KD - 1:
                    mm.then_inc(pe_misc, 1)

            token_major(U_KV, 2, 256, "kv", yh, yl, ready=(xl_ready, KD + 1, 2))
            free(("ssq", 1))
            sum_squares(1, B[BANK[("ssq", 1)]])
            gate_tile(0)
            gate_tile(1)
            free(("rstd", 1))
            spread_rstd(1, B[BANK[("rstd", 1)]])
            token_major(U_Q0, 4, 512, "q0", xh, xl)
            for j in (2, 3, 4):
                gate_tile(j)
            pe.wait_ge(heads_normed, 1)
            kd = ar(A_OT, TB, 2, P)
            for j in range(2):
                free(("kT", j))
                for t in range(TB):
                    mm = pe.transpose(B[BANK[("kT", j)]][:, t * P:(t + 1) * P], kd[:, t, j, :], ident[:])
                mm.then_inc(pe_misc, 1)
            qr = ar(A_QRAW, TB, 512)

            def turn_queries(half):
                pe.wait_ge(heads_normed, 2 + half)
                for j in range(4):
                    key = ("qT", 4 * half + j)
                    free(key)
                    for t in range(TB):
                        mm = pe.transpose(B[BANK[key]][:, t * P:(t + 1) * P], qr[:, t, j * P:(j + 1) * P], ident[:])
                    mm.then_inc(pe_misc, 1)

            turn_queries(0)
            token_major(U_Q1, 4, 512, "q1", xh, xl)
            for j in (5, 6, 7):
                gate_tile(j)
            turn_queries(1)
            pe.wait_ge(evac_a, FREE[("qT", 7)][1])
            pe.wait_ge(evac_d, FREE[("gate", 7)][1])
            ATT1[0](pe)

            pe.wait_ge(att[1]["pair_done"], ATT1[3])
            for m in range(KD):
                u = U_BOUT + m
                feature_major(u, u % RING, B[m][:], yh, yl, ready=(y_ready, NG + 1, 1) if m == 0 else None)

            token_major(U_G0, 4, 512, "G0", xh, xl, ready=(xl_ready, 3 * KD + 1, 1))
            free(("ssq", 2))
            sum_squares(2, B[BANK[("ssq", 2)]])
            token_major(U_G1, 4, 396, "G1", xh, xl)
            free(("rstd", 2))
            spread_rstd(2, B[BANK[("rstd", 2)]])

            def f_tile(j):
                u = done[("F", j)][1] - 1
                free(("F", j))
                feature_major(u, u % RING, B[BANK[("F", j)]][:], xh, xl)

            f_tile(0)
            token_major(U_G2, 4, 384, "G2", xh, xl)
            for j in range(1, 7):
                f_tile(j)
            pe.wait_ge(cmp_ready, 1)
            ch, cl = (w[:, 0:2, :].rearrange("p a (l n) -> p (a l) n", n=32) for w in (yh, yl))
            for c in range(2):
                free(("hid", c))
            for u in range(U_W1, U_W1 + 4):
                pe.wait_ge(split_done, u + 1)
                for l8 in range(8):
                    l = (u - U_W1) * 8 + l8
                    for c in range(2):
                        rows = slice(HD * c, HD * c + HD)
                        cols = slice(l8 * P, (l8 + 1) * P)
                        mm = three(B[BANK[("hid", c)]][:, 0:32], wh[rows, u % RING, cols], wl[rows, u % RING, cols],
                                   ch[rows, l, :], cl[rows, l, :], l == 0, l == 31)
                mm.then_inc(units_done, 1)
            token_major(U_G3, 4, 384, "G3", xh, xl)
            pe.wait_ge(evac_a, FREE[("hid", 1)][1])
            free(("kc", 0))
            w2 = par[:, PC["w2"]:PC["w2"] + 2 * HD]
            bk = B[BANK[("kc", 0)]]
            pe.matmul(bk[0:31, 0:HD], hid[:, 0, 0:31], w2[:, 0:HD], start=True, stop=True)
            pe.matmul(bk[0:31, HD:2 * HD], hid[:, 1, 0:31], w2[:, HD:2 * HD], start=True, stop=True).then_inc(pe_misc, 1)
            token_major(U_G4, 4, 384, "G4", xh, xl)
            pe.wait_ge(heads_normed, 4)
            r0, r1, r2 = ar(A_R0, TB, 384), ar(A_R1, TB, 384), ar(A_R2, TB, 384)
            kdn = ar(A_OT, TB, 2, P)
            for j in range(4):
                key = ("nT", j)
                free(key)
                for t in range(TB):
                    src = r0[:, t, j * P:(j + 1) * P] if j < 2 else kdn[:, t, j - 2, :]
                    mm = pe.transpose(B[BANK[key]][:, t * P:(t + 1) * P], src, ident[:])
                mm.then_inc(pe_misc, 1)
            for j in range(6):
                key = ("dT", j)
                free(key)
                for t in range(TB):
                    src = (r1 if j < 3 else r2)[:, t, (j % 3) * P:(j % 3 + 1) * P]
                    mm = pe.transpose(B[BANK[key]][:, t * P:(t + 1) * P], src, ident[:])
                mm.then_inc(pe_misc, 1)
            pe.wait_ge(heads_normed, 5)
            free(("kcT", 0))
            pe.transpose(B[BANK[("kcT", 0)]][:, 0:31], kcd[0:31, :], ident[0:31, 0:31]).then_inc(pe_misc, 1)
            pe.wait_ge(evac_a, FREE[("kcT", 0)][1])
            pe.wait_ge(evac_d, FREE[("dT", 5)][1])
            ATT2[0](pe)

            pe.wait_ge(att[2]["pair_done"], ATT2[3])
            for m in range(KD):
                u = U_OUT2 + m
                feature_major(u, u % RING, B[m][:], yh, yl, n=6)

            def mlp_chunk(c, first, later):
                for i in range(KD):
                    if later:
                        pe.wait_ge(up_read, KD * c + i - 3)
                    elif i >= 4:
                        pe.wait_ge(up_read, i - 3)
                    else:
                        pe.wait_ge(x_new, 2 * KD + i + 1)
                    feature_major(U_MLP + 16 * c + i, (U_MLP + i) % RING, B[i % 4][:], xh, xl,
                                  ready=(xl_ready, 4 * KD + 1, 1) if first and i == 0 else None)
                    if first and i == 1:
                        pe.wait_ge(x_new, 3 * KD)
                        sum_squares(3, B[4])
                    if first and i == 2:
                        spread_rstd(3, B[5])
                for m in range(KD):
                    if later or m >= 4:
                        pe.wait_ge(down_read, KD * c + m - 3)
                    elif m < 2:
                        pe.wait_ge((ssq_read, rstd_ready)[m], 4)
                    feature_major(U_MLP + 16 * c + 8 + m, (U_MLP + m) % RING, B[4 + m % 4][:], yh, yl,
                                  ready=(ff_ready, KD * c + 1, 1) if m == 0 else None)

            mlp_chunk(0, True, False)
            with pe.Fori(1, MLP_CHUNKS) as c:
                mlp_chunk(c, False, True)

        @block.scalar
        def _(act):
            roots = [0]

            def gain(name, k):
                return par[:, PC[name] + k:PC[name] + k + 1]

            def root(rows=P, cols=TB):
                roots[0] += 1
                act.wait_ge(root_ask, roots[0])
                act.activation(v4[0:rows, 1, 0:cols], v4[0:rows, 1, 0:cols], ACT.Sqrt).then_inc(root_done, 1)

            def high_and_square(q, k, ready):
                act.wait_ge(*ready)
                act.activation(xh[:, k, :], x[:, k, :], ACT.Copy, scale=gain(NORM_UNITS[q], k)).then_inc(xh_ready, 1)
                act.activation(ar(A_P, KD, S)[:, k, :], x[:, k, :], ACT.Square).then_inc(sq_ready, 1)

            def take_rstd(q, bank):
                wait_done(act, ("rstd", q))
                act.activation(rstd[:], bank[:], ACT.Copy).then_inc(rstd_ready, 1)

            act.wait_ge(in_par, 32)
            for k in range(KD):
                high_and_square(0, k, (in_x, 16))
            root()
            take_rstd(0, B[1])
            act.wait_ge(lam_ask, 1)
            act.activation(sp[:, 1, :], sp[:, 1, :], ACT.Exp).then_inc(lam_done, 1)

            rg = [ar(1545 + 1536 * i, 3, 512) for i in range(6)]
            xc, gt, rr, ii, aa, th = rg

            def rg_group(g, later):
                if later:
                    act.wait_ge(y_ready, g)
                for r, dst in ((0, rr), (1, ii)):
                    act.wait_ge(units_done, 8 * g + 7 + r)
                    for o in range(3):
                        act.activation(dst[:, o, :], B[(6 + 3 * r + o) % 8][:], ACT.Sigmoid,
                                       bias=gp[:, o, 5 + r:6 + r]).then_inc(sig_done, 1)
                act.wait_ge(gate_evac, 3 * g + 3)
                act.activation(gt[:], gt[:], ACT.Silu)
                act.wait_ge(sig_done, 6 * g + 3)
                for o in range(3):
                    act.activation(aa[:, o, :], rr[:, o, :], ACT.Exp, scale=gp[:, o, 7:8])
                    e = act.activation(th[:, o, :], rr[:, o, :], ACT.Tanh, scale=gp[:, o, 8:9])
                e.then_inc(decay_done, 1)
                act.wait_ge(var_ready, g + 1)
                act.activation(th[:], th[:], ACT.Sqrt).then_inc(var_root, 1)

            rg_group(0, False)
            with act.Fori(1, NG) as g:
                rg_group(g, True)

            for m in range(KD):
                act.wait_ge(x_new, m + 1)
                act.activation(yh[:, m, :], x[:, m, :], ACT.Copy, scale=gain("g_kv", m)).then_inc(xh_ready, 1)
                high_and_square(1, m, (x_new, m + 1))
            root()
            kraw = ar(A_KT, TB, P)
            sqk = ar(A_KT + 512, TB, P)
            act.wait_ge(rx_ready, 2)
            for t in range(TB):
                wait_done(act, ("kv", t))
                bk = B[BANK[("kv", t)]]
                act.activation(kraw[:, t, :], bk[:, 0:P], ACT.Copy)
                e = act.activation(sqk[:, t, :], bk[:, 0:P], ACT.Square)
                if t == TB - 1:
                    e.then_inc(heads_raw, 1)
                act.activation(vS[:, t, :], bk[:, P:2 * P], ACT.Copy, scale=rx[:, t:t + 1]).then_inc(evac_a, 1)
            root(P, TB * 2)
            take_rstd(1, B[BANK[("rstd", 1)]])

            qr, sqh = ar(A_QRAW, TB, 512), ar(A_SQH, TB, 512)

            def raw_heads(name, cols, dst, sq, summed=None, extra=None):
                if summed:
                    act.wait_ge(heads_summed, summed)
                for t in range(TB):
                    wait_done(act, (name, t))
                    bk = B[BANK[(name, t)]]
                    act.activation(dst[:, t, :], bk[:, 0:cols], ACT.Copy)
                    if extra:
                        extra(t, bk)
                    e = act.activation(sq[:, t, :], bk[:, 0:cols], ACT.Square)
                    e.then_inc(evac_a, 1)

            def turned(key, dst, scale):
                wait_done(act, key)
                act.activation(dst, B[BANK[key]][:], ACT.Copy, scale=scale).then_inc(evac_a, 1)

            raw_heads("q0", 512, qr, sqh)
            root(P, TB * 8)
            for j in range(2):
                turned(("kT", j), kT2[:, j, :], gain("k", 0))
            for j in range(4):
                turned(("qT", j), qT[:, j, :], hsc[:, 0:1])
            raw_heads("q1", 512, qr, sqh, summed=1)
            root(P, TB * 8)
            for j in range(4, 8):
                turned(("qT", j), qT[:, j, :], hsc[:, 0:1])
            act.wait_ge(evac_d, FREE[("gate", 7)][1])
            act.activation(ar(A_SG, 8 * S), ar(A_SG, 8 * S), ACT.Silu).then_inc(silu_done, 1)
            ATT1[1](act)

            for m in range(KD):
                high_and_square(2, m, (x_new, KD + m + 1))
            root()
            r0, r1, r2 = ar(A_R0, TB, 384), ar(A_R1, TB, 384), ar(A_R2, TB, 384)
            sqg = ar(A_SQG, TB, 384)
            act.wait_ge(rx_ready, 3)
            raw_heads("G0", 384, r0, sqg, extra=lambda t, bk: act.activation(
                vn[:, t, :], bk[:, 384:512], ACT.Copy, scale=rx[:, t:t + 1]))
            raw_heads("G1", 384, r1, sqg, summed=3, extra=lambda t, bk: act.activation(
                gates[:, t, :], bk[:, 384:396], ACT.Sigmoid, scale=rx[:, t:t + 1]))
            take_rstd(2, B[BANK[("rstd", 2)]])
            raw_heads("G2", 384, r2, sqg, summed=4)
            root(P, TB * 18)
            for c in range(2):
                wait_done(act, ("hid", c))
                act.activation(hid[:, c, :], B[BANK[("hid", c)]][:, 0:32], ACT.Gelu_apprx_tanh).then_inc(evac_a, 1)

            def values(name, dst):
                for t in range(TB):
                    wait_done(act, (name, t))
                    act.activation(dst[:, t, :], B[BANK[(name, t)]][:, 0:384], ACT.Copy,
                                   scale=rx[:, t:t + 1]).then_inc(evac_a, 1)

            values("G3", vd)
            wait_done(act, ("kc", 0))
            bk = B[BANK[("kc", 0)]]
            act.activation(vc[0:31, :], bk[0:31, HD:2 * HD], ACT.Copy)
            act.activation(kcr[0:31, :], bk[0:31, 0:HD], ACT.Copy)
            act.activation(ar(A_SQG, HD)[0:31, :], bk[0:31, 0:HD], ACT.Square, accum_out=skc[0:31, :]).then_inc(evac_a, 1)
            root(31, 1)
            values("G4", vst)
            for j in range(4):
                turned(("nT", j), (qn[:, j, :] if j < 2 else kn[:, j - 2, :]),
                       hsc[:, 1:2] if j < 2 else gain("nsa", j))
            for j in range(6):
                wait_done(act, ("dT", j))
                act.activation(xh[:, j, :], B[BANK[("dT", j)]][:], ACT.Copy,
                               scale=hsc[:, 2:3] if j < 3 else gain("dil", 1)).then_inc(dil_high, 1)
            wait_done(act, ("kcT", 0))
            act.activation(kcT[:, 0:31], B[BANK[("kcT", 0)]][:, 0:31], ACT.Copy, scale=gain("nsa", 1)).then_inc(evac_a, 1)
            ATT2[1](act)

            for m in range(KD):
                high_and_square(3, m, (x_new, 2 * KD + m + 1))
            root()

            up = ar(A_P + 4096, 2, 512)
            sq2 = ar(A_P + 5120, 2, 512)

            def mlp_chunk(c, first):
                for i in range(KD):
                    if first and i == 0:
                        take_rstd(3, B[5])
                    act.wait_ge(up_read, KD * c + i + 1)
                    if not first or i >= 2:
                        act.wait_ge(ff_ready, KD * c + i - 1)
                    act.activation(sq2[:, i % 2, :], up[:, i % 2, :], ACT.Square)
                    act.activation(yh[:, i, :], up[:, i % 2, :], ACT.Square).then_inc(up_sq, 1)

            mlp_chunk(0, True)
            with act.Fori(1, MLP_CHUNKS) as c:
                mlp_chunk(c, False)

        @block.vector
        def _(dve):
            steps = [0]
            base = [0]
            asks = [0]

            def link(ins):
                steps[0] += 1
                ins.then_inc(dve_step, 1)
                dve.wait_ge(dve_step, base[0] + steps[0])

            def gain(name, k):
                return par[:, PC[name] + k:PC[name] + k + 1]

            def rsqrt(rows, cols, y):
                v, r, t = (v4[0:rows, i, 0:cols] for i in range(3))
                dve.reciprocal(r, v).then_inc(root_ask, 1)
                asks[0] += 1
                dve.wait_ge(root_done, asks[0])
                link(dve.tensor_tensor(t, v, r, ALU.mult))
                link(dve.tensor_tensor(t, t, r, ALU.mult))
                link(dve.tensor_scalar(t, t, -0.5, 1.5, ALU.mult, ALU.add))
                return dve.tensor_tensor(y, r, t, ALU.mult)

            def low_part(k, dh, dl, name, high_count):
                dve.wait_ge(xh_ready, high_count)
                dve.scalar_tensor_tensor(out=dl[:, k, :], in0=x[:, k, :], scalar=gain(name, k), in1=dh[:, k, :],
                                         op0=ALU.mult, op1=ALU.subtract).then_inc(xl_ready, 1)

            def token_norm(q, bank):
                wait_done(dve, ("ssq", q))
                dve.tensor_scalar(v4[:, 0, 0:TB], bank[:, 0:TB], 1.0 / D, EPS, ALU.mult, ALU.add).then_inc(ssq_read, 1)
                dve.wait_ge(ssq_read, q + 1)
                rsqrt(P, TB, rx[:]).then_inc(rx_ready, 1)
                dve.wait_ge(rx_ready, q + 1)
                diag = ar(A_BIAS, TB, P)
                for t in range(TB):
                    d_ = dve.tensor_scalar(diag[:, t, :], ident[:], rx[:, t:t + 1], None, ALU.mult)
                d_.then_inc(diag_ready, 1)

            dve.memset(kcT[:], 0.0)
            dve.memset(ones[:], 1.0).then_inc(ones_set, 1)
            dve.wait_ge(ones_set, 1)
            ub = ar(0, 3, 515)
            xc, gt, rr, ii, aa, th = [ar(1545 + 1536 * i, 3, 512) for i in range(6)]
            dve.wait_ge(in_x, 16)
            dve.wait_ge(in_par, 32)
            for k in range(KD):
                low_part(k, xh, xl, "g_a", k + 1)
            token_norm(0, B[0])
            dve.tensor_scalar(hsc[:, 0:1], gain("q", 0), HD ** -0.5, None, ALU.mult)
            dve.tensor_scalar(hsc[:, 1:2], gain("nsa", 0), HD ** -0.5, None, ALU.mult)
            dve.tensor_scalar(hsc[:, 2:3], gain("dil", 0), HD ** -0.5, None, ALU.mult)
            dve.tensor_scalar(nsink[:], par[:, PC["sinks"]:PC["sinks"] + 16], -1.0, None, ALU.mult)
            lam = par[:, 0:NG * 3 * NRG].rearrange("p (t c) -> p t c", c=NRG)[:, :, 7]
            nlam = par[:, 0:NG * 3 * NRG].rearrange("p (t c) -> p t c", c=NRG)[:, :, 8]
            s0, s1, s2, s3 = (sp[:, i, :] for i in range(4))
            dve.scalar_tensor_tensor(out=s1, in0=lam, scalar=-1.0, in1=lam, op0=ALU.mult, op1=ALU.min).then_inc(lam_ask, 1)
            dve.wait_ge(lam_done, 1)
            link(dve.tensor_scalar(s2, s1, 2.0, None, ALU.add))
            link(dve.reciprocal(s2, s2))
            link(dve.tensor_tensor(s1, s1, s2, ALU.mult))
            link(dve.tensor_tensor(s2, s1, s1, ALU.mult))
            link(dve.tensor_scalar(s3, s2, 1.0 / 17.0, None, ALU.mult))
            for c in (15, 13, 11, 9, 7, 5, 3):
                link(dve.scalar_tensor_tensor(out=s3, in0=s3, scalar=1.0 / c, in1=s2, op0=ALU.add, op1=ALU.mult))
            link(dve.scalar_tensor_tensor(out=s3, in0=s3, scalar=1.0, in1=s1, op0=ALU.add, op1=ALU.mult))
            link(dve.tensor_scalar(s0, lam, -1.0, 0.0, ALU.mult, ALU.max))
            link(dve.scalar_tensor_tensor(out=s0, in0=s3, scalar=2.0, in1=s0, op0=ALU.mult, op1=ALU.add))
            link(dve.tensor_scalar(lam, s0, -8.0, None, ALU.mult))
            link(dve.tensor_scalar(nlam, s0, 8.0, None, ALU.mult))
            link(dve.memset(ub[:, :, 0:3], 0.0))

            RG_LINKS = 1 + 3 * 5 + 7

            def rg_group(g, start):
                base[0], steps[0] = start, 0
                if isinstance(g, int):
                    link(dve.tensor_copy(gp[:].rearrange("p a b -> p (a b)"), par[:, 3 * NRG * g:3 * NRG * (g + 1)]))
                else:
                    link(dve.tensor_copy(gp[:].rearrange("p a b -> p (a b)"), par[:, bass.ds(3 * NRG * g, 3 * NRG)]))
                dve.wait_ge(rstd_ready, 1)
                for i in range(3):
                    dve.wait_ge(units_done, 8 * g + i + 1)
                    dve.tensor_tensor(ub[:, i, 3:515], B[i][:], rstd[:], ALU.mult).then_inc(xb_evac, 1)
                    dve.wait_ge(xb_evac, 3 * g + i + 1)
                    link(dve.tensor_scalar(xc[:, i, :], ub[:, i, 0:512], gp[:, i, 0:1], gp[:, i, 4:5], ALU.mult, ALU.add))
                    for j in range(1, 4):
                        link(dve.scalar_tensor_tensor(out=xc[:, i, :], in0=ub[:, i, j:j + 512], scalar=gp[:, i, j:j + 1],
                                                      in1=xc[:, i, :], op0=ALU.mult, op1=ALU.add))
                    link(dve.tensor_copy(yh[:, 9 + i, :], xc[:, i, :]))
                    dve.tensor_tensor(yl[:, 9 + i, :], xc[:, i, :], yh[:, 9 + i, :], ALU.subtract).then_inc(xc_ready, 1)
                for i in range(3):
                    dve.wait_ge(units_done, 8 * g + 4 + i)
                    dve.tensor_tensor(gt[:, i, :], B[3 + i][:], rstd[:], ALU.mult).then_inc(gate_evac, 1)
                dve.wait_ge(sig_done, 6 * g + 6)
                link(dve.tensor_tensor(ii[:], ii[:], xc[:], ALU.mult))
                dve.wait_ge(decay_done, g + 1)
                link(dve.tensor_tensor(rr[:], aa[:], aa[:], ALU.mult))
                dve.scalar_tensor_tensor(out=th[:], in0=rr[:], scalar=1.0, in1=th[:], op0=ALU.add, op1=ALU.mult)\
                   .then_inc(var_ready, 1)
                dve.wait_ge(var_root, g + 1)
                link(dve.tensor_tensor(ii[:], ii[:], th[:], ALU.mult))
                for i in range(3):
                    link(dve.tensor_tensor_scan(rr[:, i, :], aa[:, i, :], ii[:, i, :], 0.0, ALU.mult, ALU.add))
                link(dve.tensor_tensor(rr[:], rr[:], gt[:], ALU.mult))
                at = slice(3 * g, 3 * g + 3) if isinstance(g, int) else bass.ds(3 * g, 3)
                dve.tensor_scalar(yh[:, at, :], rr[:], 1.0, None, ALU.mult).then_inc(rg_high, 1)
                dve.wait_ge(rg_high, g + 1)
                dve.tensor_tensor(yl[:, at, :], rr[:], yh[:, at, :], ALU.subtract).then_inc(y_ready, 1)
                assert steps[0] == RG_LINKS, steps

            before = steps[0]
            rg_group(0, before)
            with dve.Fori(1, NG) as g:
                rg_group(g, g * RG_LINKS + before)
            base[0], steps[0] = before + NG * RG_LINKS, 0

            dve.wait_ge(y_ready, NG)
            for m in range(KD):
                wait_done(dve, ("wout", m))
                dve.tensor_tensor(x[:, m, :], B[m][:], x[:, m, :], ALU.add).then_inc(x_new, 1)
                dve.wait_ge(x_new, m + 1)
                low_part(m, yh, yl, "g_kv", KD + 2 * m + 1)
                low_part(m, xh, xl, "g_b", KD + 2 * m + 2)

            token_norm(1, B[BANK[("ssq", 1)]])

            def head_scales(n):
                v = head_view(0, n)
                link(dve.tensor_tensor(rx2[:], rx[:], rx[:], ALU.mult))
                link(dve.tensor_tensor(v, v, rx2[:].unsqueeze(2).to_broadcast([P, TB, n]), ALU.mult))
                link(dve.tensor_scalar(v4[:, 0, 0:TB * n], v4[:, 0, 0:TB * n], 1.0 / HD, EPS, ALU.mult, ALU.add))
                link(rsqrt(P, TB * n, v4[:, 1, 0:TB * n]))
                link(dve.tensor_tensor(head_view(2, n), head_view(1, n), rx[:].unsqueeze(2).to_broadcast([P, TB, n]),
                                       ALU.mult))

            kraw, sqk = ar(A_KT, TB, P), ar(A_KT + 512, TB, P)
            kd = ar(A_OT, TB, 2, P)
            dve.wait_ge(heads_raw, 1)
            link(dve.tensor_reduce(head_view(0, 2), sqk[:].rearrange("p t (h d) -> p t h d", d=HD), AX.X, ALU.add))
            head_scales(2)
            rq = head_view(2, 2)
            for j in range(2):
                for t in range(TB):
                    e = dve.tensor_scalar(kd[:, t, j, :].rearrange("p (c d) -> p c d", c=2),
                                          kraw[:, t, HD * j:HD * j + HD].unsqueeze(1).to_broadcast([P, 2, HD]),
                                          rq[:, t, j:j + 1], None, ALU.mult)
            e.then_inc(heads_normed, 1)

            def gate_tile(j):
                wait_done(dve, ("gate", j))
                dve.tensor_tensor(sg[:, j, :], B[BANK[("gate", j)]][:], rstd[:], ALU.mult).then_inc(evac_d, 1)

            dve.wait_ge(rstd_ready, 2)
            gate_tile(0)
            gate_tile(1)
            qr, sqh = ar(A_QRAW, TB, 512), ar(A_SQH, TB, 512)

            def norm_queries(half):
                dve.wait_ge(evac_a, FREE[(f"q{half}", TB - 1)][1])
                dve.tensor_reduce(head_view(0, 8), sqh[:].rearrange("p t (h d) -> p t h d", d=HD), AX.X, ALU.add)\
                   .then_inc(heads_summed, 1)
                dve.wait_ge(heads_summed, half + 1)
                head_scales(8)
                rq = head_view(2, 8)
                for t in range(TB):
                    q4 = qr[:, t, :].rearrange("p (h d) -> p h d", d=HD)
                    e = dve.tensor_tensor(q4, q4, rq[:, t, 0:8].unsqueeze(2).to_broadcast([P, 8, HD]), ALU.mult)
                e.then_inc(heads_normed, 1)

            norm_queries(0)
            for j in (2, 3, 4):
                gate_tile(j)
            norm_queries(1)
            for j in (5, 6, 7):
                gate_tile(j)
            dve.wait_ge(in_tab, 32)
            dve.wait_ge(evac_a, FREE[("qT", 7)][1])
            ATT1[2](dve, link)

            for m in range(KD):
                wait_done(dve, ("bout", m))
                dve.tensor_tensor(x[:, m, :], B[m][:], x[:, m, :], ALU.add).then_inc(x_new, 1)
                dve.wait_ge(x_new, KD + m + 1)
                low_part(m, xh, xl, "g_mix", 3 * KD + m + 1)
            token_norm(2, B[BANK[("ssq", 2)]])

            r0, r1, r2 = ar(A_R0, TB, 384), ar(A_R1, TB, 384), ar(A_R2, TB, 384)
            sqg = ar(A_SQG, TB, 384)

            def sum_heads(name, at, count):
                dve.wait_ge(evac_a, FREE[(name, TB - 1)][1])
                dve.tensor_reduce(head_view(0, 18)[:, :, at:at + 6], sqg[:].rearrange("p t (h d) -> p t h d", d=HD), AX.X, ALU.add)\
                   .then_inc(heads_summed, 1)
                dve.wait_ge(heads_summed, count)

            sum_heads("G0", 0, 3)
            sum_heads("G1", 6, 4)
            dve.wait_ge(rstd_ready, 3)
            ct, rawc = ar(A_CT, 512), ar(A_RAW, 32, 32)
            wait_done(dve, ("F", 0))
            dve.tensor_tensor(ct, B[BANK[("F", 0)]][:], rstd[:], ALU.mult).then_inc(evac_d, 1)
            dve.wait_ge(evac_d, FREE[("F", 0)][1])
            link(dve.memset(rawc[:, :, 31:32], 0.0))
            cv = ct.rearrange("p (n s) -> p s n", s=16)
            pe_ = par[:, PC["pe"]:PC["pe"] + 32]
            for half in range(2):
                e = dve.tensor_tensor(rawc[:, 16 * half:16 * half + 16, 0:31], cv[:, :, half:half + 31],
                                      pe_[:, 16 * half:16 * half + 16].unsqueeze(2).to_broadcast([P, 16, 31]), ALU.add)
            link(e)
            rc = rawc[:].rearrange("p l n -> p (l n)").rearrange("p (a b) -> p a b", a=2)
            link(dve.tensor_copy(yh[:, 0:2, :], rc))
            dve.tensor_tensor(yl[:, 0:2, :], rc, yh[:, 0:2, :], ALU.subtract).then_inc(cmp_ready, 1)
            sum_heads("G2", 12, 5)
            head_scales(18)
            rq = head_view(2, 18)
            for t in range(TB):
                for rr_, at, n in ((r0, 0, 4), (r1, 6, 6), (r2, 12, 6)):
                    h4 = rr_[:, t, 0:HD * n].rearrange("p (h d) -> p h d", d=HD)
                    dve.tensor_tensor(h4, h4, rq[:, t, at:at + n].unsqueeze(2).to_broadcast([P, n, HD]), ALU.mult)
                for j in range(2):
                    e = dve.tensor_scalar(kd[:, t, j, :].rearrange("p (c d) -> p c d", c=2),
                                          r0[:, t, 256 + HD * j:256 + HD * j + HD].unsqueeze(1).to_broadcast([P, 2, HD]),
                                          rq[:, t, 4 + j:5 + j], None, ALU.mult)
            e.then_inc(heads_normed, 1)
            st = ar(A_ST, 512)
            for j in range(1, 7):
                wait_done(dve, ("F", j))
                dve.scalar_tensor_tensor(out=st, in0=B[BANK[("F", j)]][:], scalar=HD ** -0.5 if j < 4 else 1.0,
                                         in1=rstd[:], op0=ALU.mult, op1=ALU.mult).then_inc(evac_d, 1)
                dve.wait_ge(evac_d, FREE[("F", j)][1])
                link(dve.tensor_copy(yh[:, 5 + j, :], st))
                link(dve.tensor_tensor(yl[:, 5 + j, :], st, yh[:, 5 + j, :], ALU.subtract))
            dve.wait_ge(evac_a, FREE[("kc", 0)][1])
            link(dve.tensor_scalar(v4[0:31, 0, 0:1], skc[0:31, :], 1.0 / HD, EPS, ALU.mult, ALU.add))
            link(rsqrt(31, 1, v4[0:31, 1, 0:1]))
            dve.tensor_scalar(kcd[0:31, :].rearrange("p (c d) -> p c d", c=2),
                              kcr[0:31, :].unsqueeze(1).to_broadcast([31, 2, HD]),
                              v4[0:31, 1, 0:1], None, ALU.mult).then_inc(heads_normed, 1)
            for j in range(6):
                dve.wait_ge(dil_high, j + 1)
                dve.scalar_tensor_tensor(out=xl[:, j, :], in0=B[BANK[("dT", j)]][:],
                                         scalar=hsc[:, 2:3] if j < 3 else gain("dil", 1), in1=xh[:, j, :],
                                         op0=ALU.mult, op1=ALU.subtract).then_inc(evac_d, 1)
            dve.wait_ge(evac_a, FREE[("kcT", 0)][1])
            ATT2[2](dve, link)

            for m in range(KD):
                wait_done(dve, ("out2", m))
                dve.tensor_tensor(x[:, m, :], B[m][:], x[:, m, :], ALU.add).then_inc(x_new, 1)
                dve.wait_ge(x_new, 2 * KD + m + 1)
                low_part(m, xh, xl, "g_mlp", 4 * KD + m + 1)
            token_norm(3, B[4])

            up, sq2 = ar(A_P + 4096, 2, 512), ar(A_P + 5120, 2, 512)
            dve.wait_ge(rstd_ready, 4)

            def mlp_chunk(c, first):
                def relu(i):
                    dve.wait_ge(units_done, U_MLP + 16 * c + i + 1)
                    if not first or i >= 2:
                        dve.wait_ge(up_sq, KD * c + i - 1)
                    dve.scalar_tensor_tensor(out=up[:, i % 2, :], in0=B[i % 4][:], scalar=0.0, in1=rstd[:],
                                             op0=ALU.max, op1=ALU.mult).then_inc(up_read, 1)

                def low(i):
                    dve.wait_ge(up_sq, KD * c + i + 1)
                    dve.tensor_tensor(yl[:, i, :], sq2[:, i % 2, :], yh[:, i, :], ALU.subtract).then_inc(ff_ready, 1)

                for i in range(KD):
                    relu(i)
                    low(i)
                for m in range(KD):
                    dve.wait_ge(units_done, U_MLP + 16 * c + 8 + m + 1)
                    dve.tensor_tensor(x[:, m, :], B[4 + m % 4][:], x[:, m, :], ALU.add).then_inc(down_read, 1)

            mlp_chunk(0, True)
            with dve.Fori(1, MLP_CHUNKS) as c:
                mlp_chunk(c, False)


def _tables():
    FAR = 1e33
    i = np.arange(P)[:, None]

    def dist(cols, first, ok):
        d = (first + i - np.arange(cols)[None, :]).astype(np.float64)
        return np.where(ok(d), d, FAR)

    t = np.zeros((P, NTAB), np.float32)
    t[:, T_D0:T_D0 + 256] = dist(256, 128, lambda d: (d >= 0) & (d <= 128))
    t[:, T_D1:T_D1 + 512] = dist(512, 384, lambda d: (d >= 0) & (d % 4 == 0))
    t[:, T_D2:T_D2 + 512] = dist(512, 384, lambda d: (d >= 0) & (d % 16 == 0))
    t[:, T_DC:T_DC + 512] = dist(512, 384, lambda d: d >= 0)
    t[:, T_STK:T_STK + 512] = np.where(dist(512, 384, lambda d: d > 0) < FAR, 0.0, -BIG)
    for n in range(TB):
        for w in range(32):
            d = n * P + np.arange(P) - (16 * w + 31)
            t[:, T_CMP + 32 * n + w] = np.where((d >= 0) & (w < 31), d, FAR)
    return t, np.ascontiguousarray(dist(256, 128, lambda d: (d >= 0) & (d < 128)).astype(np.float32))


def _feature_units(w):
    k, m = w.shape[0] // P, w.shape[1] // P
    u = w.reshape(k, P, m, P).transpose(2, 1, 0, 3).reshape(m, P, k * P)
    return np.pad(u, ((0, 0), (0, 0), (0, UNIT - k * P)))


def _token_units(w, units):
    cols = UNIT * units // KD
    w = np.pad(w, ((0, 0), (0, cols - w.shape[1])))
    return w.reshape(units, KD // units, P, cols).transpose(0, 2, 1, 3).reshape(units, P, UNIT)


def _gate_unit(blocks):
    full = np.zeros((3 * P, 3 * P), np.float32)
    n = blocks.shape[1]
    for b in range(blocks.shape[0]):
        full[b * n:(b + 1) * n, b * n:(b + 1) * n] = blocks[b]
    unit = np.zeros((1, P, 8, P), np.float32)
    for t, (i, o) in enumerate(GATE_TILES):
        unit[0, :, t] = full[i * P:(i + 1) * P, o * P:(o + 1) * P]
    return unit.reshape(1, P, UNIT)


def kernel(**inputs):
    import concourse.bacc as _bacc
    from concourse.bass_utils import run_bass_kernel_spmd as _run

    a = {k: np.asarray(v) for k, v in inputs.items()}
    xb, gate = _feature_units(a["a_w_in"][0][:, :R]), _feature_units(a["a_w_in"][0][:, R:])
    parts = []
    for g in range(NG):
        parts += [xb[3 * g:3 * g + 3], gate[3 * g:3 * g + 3], _gate_unit(a["a_gate_r_w"][0][4 * g:4 * g + 4]),
                  _gate_unit(a["a_gate_i_w"][0][4 * g:4 * g + 4])]
    parts.append(a["a_w_out"][0].reshape(RT, P, D))
    parts.append(_token_units(a["w_kv"], 2))
    bq, bg = a["b_w_in"][0][:, :D], _feature_units(a["b_w_in"][0][:, D:])
    parts += [bg[0:2], _token_units(bq[:, 0:512], 4), bg[2:5], _token_units(bq[:, 512:], 4), bg[5:8]]
    parts.append(_feature_units(a["b_w_out"][0]))
    w = a["w_in_2"][0]
    q_, kc, vc, ks, vs, kw, vw, gl = np.split(w[:, 0:652], [256, 320, 384, 448, 512, 576, 640], axis=1)
    dq, dk, dv = np.split(w[:, 652:652 + 1152], 3, axis=1)
    sq, sk, sv = np.split(w[:, 652 + 1152:], 3, axis=1)
    parts.append(_token_units(np.concatenate([q_, ks, kw, vs, vw], 1), 4))
    parts.append(_token_units(np.concatenate([dq, gl], 1), 4))
    parts.append(_feature_units(np.concatenate([kc, vc], 1)))
    parts.append(_token_units(dk, 4))
    parts.append(_feature_units(np.concatenate([sq, sk], 1)))
    parts.append(a["cmp_w1_2"][0].reshape(2, 4, 8, HD, P).transpose(1, 0, 3, 2, 4).reshape(4, P, UNIT))
    parts += [_token_units(dv, 4), _token_units(sv, 4), _feature_units(a["w_out_2"][0])]
    up = _feature_units(a["w_up_2"][0])
    for c in range(MLP_CHUNKS):
        parts += [up[8 * c:8 * c + 8], _feature_units(a["w_down_2"][0][c * D:(c + 1) * D])]
    weights = np.ascontiguousarray(np.concatenate(parts, 0))
    assert weights.shape == (UNITS, P, UNIT), weights.shape
    rg = np.stack([*a["a_conv_w"][0], a["a_conv_b"][0], a["a_gate_r_b"][0], a["a_gate_i_b"][0], a["a_lambda"][0],
                   a["a_lambda"][0]])
    twice = lambda g: np.concatenate([g, g], -1).T
    cols = [rg.reshape(NRG, RT, P).transpose(2, 1, 0).reshape(P, RT * NRG)]
    cols += [a[n].reshape(KD, P).T for n in ("a_norm_g", "kv_norm_g", "b_norm_g", "norm_mix_2", "norm_mlp_2")]
    cols += [twice(a["q_norm_g"]), twice(a["k_norm_g"][None]), twice(a["qk_gain_nsa_2"][0]), twice(a["qk_gain_dil_2"][0])]
    cols += [np.broadcast_to(a["sinks"], (P, 16)), a["cmp_pe_2"][0].transpose(0, 2, 1).reshape(P, 32)]
    cols += [a["cmp_w2_2"][0].transpose(1, 0, 2).reshape(P, 2 * HD)]
    params = np.ascontiguousarray(np.concatenate(cols, 1))
    assert params.shape == (P, NPAR), params.shape
    arrays = {
        "x_in": np.ascontiguousarray(a["x"][0].T.reshape(KD, P, S).transpose(1, 0, 2)),
        "weight_units": weights,
        "params": params,
        "tables": _tables()[0],
        "swa_table": _tables()[1],
        "identity": np.eye(P, dtype=np.float32),
    }
    nc = _bacc.Bacc("TRN2", target_bir_lowering=False, num_devices=1, dynamic_dma_scratch_size=1024)
    args = [nc.dram_tensor(n, v.shape, mybir.dt.from_np(v.dtype), kind="ExternalInput").ap() for n, v in arrays.items()]
    out = nc.dram_tensor("out_fm", (P, KD, S), F32, kind="ExternalOutput").ap()
    two_block_kernel(nc, *args, out)
    r = _run(nc, [arrays], core_ids=[0])
    y = np.asarray(r.results[0]["out_fm"])
    return np.ascontiguousarray(y.transpose(2, 1, 0).reshape(1, S, D))
```

```python
from contextlib import ExitStack

import numpy as np

import concourse.bass as bass
from concourse import mybir

F32 = mybir.dt.float32
F32R = mybir.dt.float32r
ALU = mybir.AluOpType
ACT = mybir.ActivationFunctionType
AX = mybir.AxisListType

P = 128
D = 1024
S = 512
KD = D // P
TB = S // P
R = 1536
RT = R // P
NG = 4
HD = 64
EPS = 1e-6
BIG = 1e30
UNIT = 1024
RING = 4
GATE_TILES = [(0, 0), (1, 0), (0, 1), (1, 1), (2, 1), (1, 2), (2, 2)]

U_RG = 0
U_WOUT = U_RG + 8 * NG
U_KV = U_WOUT + RT
U_GA = U_KV + 2
U_Q0 = U_GA + 2
U_Q1 = U_Q0 + 4
U_GB = U_Q1 + 4
U_BOUT = U_GB + 6
U_G0 = U_BOUT + 8
U_G1 = U_G0 + 4
U_F0 = U_G1 + 4
U_G2 = U_F0 + 1
U_W1 = U_G2 + 4
U_FA = U_W1 + 4
U_G4 = U_FA + 2
U_FB = U_G4 + 4
U_G3 = U_FB + 2
U_FC = U_G3 + 4
U_OUT2 = U_FC + 2
U_MLP = U_OUT2 + 8
MLP_CHUNKS = 4
UNITS = U_MLP + 16 * MLP_CHUNKS

NRG = 9
PC = {}
_at = 0
for _name, _n in [("rg", NG * 3 * NRG), ("g_a", KD), ("g_kv", KD), ("g_b", KD), ("g_mix", KD), ("g_mlp", KD),
                  ("q", 1), ("k", 1), ("nsa", 4), ("dil", 2), ("sinks", 16), ("pe", 32), ("w2", 2 * HD)]:
    PC[_name] = _at
    _at += _n
NPAR = _at

A_P = 0
A_QRAW, A_SQH = 0, 2048
A_QT, A_KT, A_VS, A_SG = 4096, 8192, 9216, 9728
A_OT, A_BIAS, A_TAB = 13824, 14848, 16128
A_SWA = A_BIAS + 768
A_HID, A_KCR, A_KCD = A_BIAS + 1024, A_BIAS + 1088, A_BIAS + 1152
A_RG = A_OT
A_END = A_TAB + 2432
A_PT1, A_PT2 = 1024, 5120
A_R0, A_R1, A_R2, A_SQG, A_CT, A_RAW = 0, 2048, 3584, 5120, 6656, 7168
A_LT = 7168
A_ST, A_TMPO = A_BIAS + 512, A_BIAS + 1024
A_HIDT = A_BIAS + 512
A_QRAW1 = A_SG + 2048
A_TANH = 2560
A_VD, A_VST, A_VN, A_QN, A_KN = 8192, 9728, 11264, 11776, 12800
T_D0, T_D1, T_D2, T_DC, T_STK, T_CMP = 0, 256, 768, 1280, 1792, 2304
NTAB = 2432


ITEMS1 = {-2: ("gate", 4), 12: ("gate", 5), 26: ("gate", 6), 42: ("gate", 7)}
ITEMS2 = {-2: ("G4", 0), 2: ("kcT", 0), 5: ("G4", 1), 10: ("G4", 2), 15: ("G4", 3), 22: ("F", 2), 25: ("F", 5),
          30: ("G3", 0), 35: ("G3", 1), 40: ("G3", 2), 45: ("G3", 3), 50: ("F", 3), 54: ("F", 6),
          60: ("dT", 0), 61: ("dT", 1), 62: ("dT", 2), 63: ("dT", 3), 64: ("dT", 4), 65: ("dT", 5)}
EVAC = {"gate": "D", "G4": "A", "kcT": "A", "F": "D", "G3": "A", "dT": "D"}
F_UNIT = {0: U_F0, 1: U_FA, 4: U_FA + 1, 2: U_FB, 5: U_FB + 1, 3: U_FC, 6: U_FC + 1}


def plan():
    seg1 = [("wout", m, "X") for m in range(8)] + [("kv", t, "A") for t in range(4)] + [("ssq", 1, "N")]
    seg1 += [("gate", 0, "D"), ("gate", 1, "D"), ("rstd", 1, "B")] + [("q0", t, "A") for t in range(4)]
    seg1 += [("q1", t, "A") for t in range(4)] + [("kT", j, "A") for j in range(2)]
    seg1 += [("qT", j, "A") for j in range(4)] + [("gate", j, "D") for j in (2, 3)]
    seg1 += [("qT", j, "A") for j in range(4, 8)]
    seg2 = [("bout", m, "X") for m in range(8)] + [("G0", t, "A") for t in range(4)] + [("ssq", 2, "N")]
    seg2 += [("G1", t, "A") for t in range(4)] + [("rstd", 2, "B"), ("F", 0, "D")]
    seg2 += [("G2", t, "A") for t in range(4)] + [("hid", 0, "A"), ("hid", 1, "A"), ("F", 1, "D"), ("hT", 0, "A")]
    seg2 += [("F", 4, "D"), ("kc", 0, "A")] + [("nT", j, "A") for j in range(4)]
    bank, free, before = {}, {}, {}
    count = {"A": 0, "D": 0}
    for seg, items in ((seg1, ITEMS1), (seg2, ITEMS2)):
        for i, (name, j, who) in enumerate(seg):
            key = (name, j)
            bank[key] = i % 8
            if who in count:
                count[who] += 1
                free[key] = (who, count[who])
            elif who == "X":
                free[key] = (who, j + 1 + (8 if name == "bout" else 0))
            else:
                free[key] = (who, j + 1)
            before[key] = free[seg[i - 8][:2]] if i >= 8 else None
        for key in items.values():
            bank[key] = 7
            count[EVAC[key[0]]] += 1
            free[key] = (EVAC[key[0]], count[EVAC[key[0]]])
    return bank, free, before


def attention_one():
    batches = [dict(kind="swa", head=h, pair=h // 2, half=h % 2, last=h % 2 == 1,
                    turn=h // 2) for h in range(16)]
    groups = [dict(b=h, n=n, w=[128 if n == 0 else 256]) for h in range(16) for n in range(TB)]
    return batches, groups


def attention_two():
    def nsa(p):
        return [dict(kind=kind, head=2 * p + h, x=x, pair=p, half=h, last=(h == 1 and x == 0))
                for h in range(2) for x, kind in ((1, "sel"), (2, "win"), (0, "cmp"))]

    def stick(p):
        return [dict(kind="stick", head=2 * p + h, pair=3 + p, half=h, last=h == 1) for h in range(2)]

    dil = [dict(kind="dil", head=h, pair=2, half=h, last=h == 1) for h in range(2)]
    batches = nsa(0) + stick(0) + nsa(1) + stick(1) + stick(2) + dil
    groups = []
    turn = 0
    for b, batch in enumerate(batches):
        batch["turn"] = turn
        turn += batch["last"]
        for n in range(TB):
            full = (n + 1) * P
            w = {"cmp": [32], "dil": [min(full, 256), full, full]}.get(batch["kind"], [full])
            groups.append(dict(b=b, n=n, w=w))
    return batches, groups


def with_chunks(groups, batches, per_chunk):
    strip = chunk = 0
    for g in groups:
        g["strip0"] = strip
        strip += len(g["w"])
        kind = batches[g["b"]]["kind"]
        blocks, col = [], 0
        for s, w in enumerate(g["w"]):
            for c in range(0, w, P):
                blocks.append((s, col + c, c // P, 31 if kind == "cmp" else P))
            col += w
        g["chunks"] = [(chunk + i, blocks[c:c + per_chunk]) for i, c in enumerate(range(0, len(blocks), per_chunk))]
        chunk += len(g["chunks"])
    return groups


def two_block_kernel(nc, x_d, weights_d, params_d, tables_d, swa_d, ident_d, out_d):
    BANK, FREE, BEFORE = plan()
    ctx = ExitStack()
    with ctx:
        def sb(name, shape, dt=F32):
            return ctx.enter_context(nc.sbuf_tensor(name, shape, dt))

        def sem(name):
            return ctx.enter_context(nc.semaphore(name))

        x = sb("x", [P, KD, S])
        raw = sb("raw", [P, RING, UNIT])
        wh = sb("wh", [P, RING, UNIT], F32R)
        wl = sb("wl", [P, RING, UNIT], F32R)
        yh = sb("yh", [P, RT, S], F32R)
        yl = sb("yl", [P, RT, S], F32R)
        xh = sb("xh", [P, KD, S], F32R)
        xl = sb("xl", [P, KD, S], F32R)
        arena = sb("arena", [P, A_END])
        par = sb("par", [P, NPAR])
        ident = sb("ident", [P, P])
        ones = sb("ones", [P, P])
        rstd = sb("rstd", [P, S])
        rx = sb("rx", [P, TB])
        v4 = sb("v4", [P, 3, 72])
        rx2 = sb("rx2", [P, TB])
        hold = sb("hold", [P, 2])
        hsc = sb("hsc", [P, 3])
        gates = sb("gates", [P, TB, 12])
        negm = sb("negm", [P, 4, TB])
        rsum = sb("rsum", [P, 4, TB, 3])
        esink = sb("esink", [P, 2, TB])
        mtmp = sb("mtmp", [P, 2])
        den = sb("den", [P, TB])
        kcT = sb("kcT", [P, 32])
        vc = sb("vc", [P, HD])
        skc = sb("skc", [P, 1])
        B = [ctx.enter_context(nc.psum_tensor(f"bank{i}", [P, 512], F32)) for i in range(8)]

        def ar(at, *shape):
            n = int(np.prod(shape))
            v = arena[:, at:at + n]
            if len(shape) == 2:
                v = v.rearrange("p (a b) -> p a b", a=shape[0])
            if len(shape) == 3:
                v = v.rearrange("p (a b c) -> p a b c", a=shape[0], b=shape[1])
            return v

        gp = ar(A_RG, 3, NRG)
        sp = ar(A_RG + 3 * NRG, 4, NG * 3)
        hid, kcr, kcd = ar(A_HID, 2, 32), ar(A_KCR, HD), ar(A_KCD, P)
        tmpo = ar(A_TMPO, TB, HD)
        hidt = ar(A_HIDT, 2, P)

        def head_view(i, n):
            return v4[:, i, 0:TB * n].rearrange("p (t h) -> p t h", t=TB)

        loaded = [sem(f"raw_loaded{i}") for i in range(RING)]
        held = sem("unit_held")
        high_done = sem("high_done")
        split_done = sem("split_done")
        units_done = sem("units_done")
        in_x, in_par, in_tab = sem("in_x"), sem("in_par"), sem("in_tab")
        ones_set = sem("ones_set")
        sq_ready = sem("sq_ready")
        ssq_read = sem("ssq_read")
        root_ask, root_done = sem("root_ask"), sem("root_done")
        rx_ready = sem("rx_ready")
        diag_ready = sem("diag_ready")
        rstd_ready = sem("rstd_ready")
        xh_ready = sem("xh_ready")
        xl_ready = sem("xl_ready")
        x_new = sem("x_new")
        dve_step = sem("dve_step")
        rg_high = sem("rg_high")
        xb_evac, gate_evac, xc_ready = sem("xb_evac"), sem("gate_evac"), sem("xc_ready")
        sig_done, decay_done = sem("sig_done"), sem("decay_done")
        var_ready, var_root, y_ready = sem("var_ready"), sem("var_root"), sem("y_ready")
        pe_misc = sem("pe_misc")
        evac_a, evac_d = sem("evac_act"), sem("evac_dve")
        heads_raw = sem("heads_raw")
        heads_summed = sem("heads_summed")
        heads_normed = sem("heads_normed")
        tanh_done = sem("tanh_done")
        heads_split = sem("heads_split")
        lam_ask, lam_done = sem("lam_ask"), sem("lam_done")
        dil_high = sem("dil_high")
        cmp_ready = sem("cmp_ready")
        up_read, up_sq, ff_ready = sem("up_read"), sem("up_squared"), sem("ff_ready")
        down_read = sem("down_read")
        stored = sem("stored")
        FREESEM = {"A": evac_a, "D": evac_d, "X": x_new, "N": ssq_read, "B": rstd_ready}

        att = {}
        for a in (1, 2):
            att[a] = {n: sem(f"{n}{a}") for n in (
                "scores", "strip_read", "masked", "soft1", "soft2", "probs", "pt_ready", "pt_even", "pt_odd",
                "o_done", "fin", "pairT", "pair_done", "esum")}

        block = ctx.enter_context(nc.Block())

        done = {}
        misc = [0]

        def by_misc(key):
            misc[0] += 1
            done[key] = (pe_misc, misc[0])

        by_misc(("ssq", 0))
        by_misc(("rstd", 0))
        for m in range(7):
            by_misc(("wout", m))
        done[("wout", 7)] = (units_done, U_KV)
        for t in range(4):
            done[("kv", t)] = (units_done, U_GA)
            done[("q0", t)] = (units_done, U_Q1)
            done[("q1", t)] = (units_done, U_GB)
            done[("G0", t)] = (units_done, U_G1)
            done[("G1", t)] = (units_done, U_F0)
            done[("G2", t)] = (units_done, U_W1)
        for j in range(8):
            u = U_GA + j if j < 2 else U_GB + j - 2
            done[("gate", j)] = (units_done, u + 1)
            done[("bout", j)] = (units_done, U_BOUT + j + 1)
            done[("out2", j)] = (units_done, U_OUT2 + j + 1)
        for j in range(7):
            done[("F", j)] = (units_done, F_UNIT[j] + 1)
        done[("hid", 0)] = done[("hid", 1)] = (units_done, U_FA)
        for key in ([("ssq", 1), ("rstd", 1), ("kT", 0), ("kT", 1)] + [("qT", j) for j in range(8)]
                    + [("ssq", 2), ("rstd", 2), ("hT", 0), ("kc", 0)] + [("nT", j) for j in range(4)]
                    + [key for key in ITEMS2.values() if key[0] != "F" and key not in (("G3", 3), ("G4", 3))]
                    + [("ssq", 3), ("rstd", 3)]):
            by_misc(key)
        done[("G3", 3)] = (units_done, U_G3 + 4)
        done[("G4", 3)] = (units_done, U_G4 + 4)

        def wait_done(eng, key):
            eng.wait_ge(*done[key])

        NORM_UNITS = {0: "g_a", 1: "g_b", 2: "g_mix", 3: "g_mlp"}

        @block.sync
        def _(sp_):
            sp_.dma_start(x[:], x_d).then_inc(in_x, 16)

            def load(j, ahead, u):
                if ahead is not None:
                    sp_.wait_ge(split_done, ahead)
                sp_.dma_start(raw[:, j, :], weights_d[u].rearrange("a p n -> (a p) n")).then_inc(loaded[j], 16)

            load(0, None, bass.ds(0, 1))
            sp_.dma_start(par[:], params_d).then_inc(in_par, 16)
            sp_.dma_start(ident[:], ident_d).then_inc(in_par, 16)
            for j in range(1, RING):
                load(j, None, bass.ds(j, 1))
            sp_.dma_start(ar(A_TAB, NTAB), tables_d).then_inc(in_tab, 16)
            sp_.dma_start(ar(A_SWA, 256), swa_d).then_inc(in_tab, 16)
            with sp_.Fori(1, UNITS // RING) as lap:
                for j in range(RING):
                    load(j, RING * lap + j - RING + 1, bass.ds(RING * lap + j, 1))
            for u in range(UNITS // RING * RING, UNITS):
                load(u % RING, u - RING + 1, bass.ds(u, 1))
            for m in range(KD):
                sp_.wait_ge(down_read, KD * (MLP_CHUNKS - 1) + m + 1)
                sp_.dma_start(out_d[:, m, :], x[:, m, :]).then_inc(stored, 16)
            sp_.wait_ge(stored, 16 * KD)

        @block.gpsimd
        def _(pool):
            pool.memset(hold[:], 0.0).then_inc(held, 1)
            pool.wait_ge(held, 1)

            def split(u, j, lap, first):
                pool.wait_ge(loaded[j], 16 * lap + 16)
                if not first:
                    pool.wait_ge(units_done, u - RING + 1)
                pool.tensor_tensor(hold[:], hold[:], hold[:], ALU.add).then_inc(held, 1)
                pool.tensor_scalar(wh[:, j, :], raw[:, j, :], 1.0, 1.0, ALU.mult, ALU.mult).then_inc(high_done, 1)
                pool.wait_ge(high_done, u + 1)
                pool.tensor_tensor(wl[:, j, :], raw[:, j, :], wh[:, j, :], ALU.subtract).then_inc(split_done, 1)

            for j in range(RING):
                split(j, j, 0, True)
            with pool.Fori(1, UNITS // RING) as lap:
                for j in range(RING):
                    split(RING * lap + j, j, lap, False)
            for u in range(UNITS // RING * RING, UNITS):
                split(u, u % RING, u // RING, False)

        def head_rows(h):
            return slice(HD * (h % 2), HD * (h % 2) + HD)

        qT = ar(A_QT, 8, S)
        kT2 = ar(A_KT, 2, S)
        vS = ar(A_VS, TB, P)
        sg = ar(A_SG, 8, S)
        vd, vst, vn = ar(A_VD, TB, 384), ar(A_VST, TB, 384), ar(A_VN, TB, P)
        qn, kn = ar(A_QN, 2, S), ar(A_KN, 2, S)
        otok = ar(A_OT, 2, TB, P)
        bias = ar(A_BIAS, 1280)
        tabs = ar(A_TAB, NTAB)
        LOOK = 3

        def make_attention(a):
            batches, groups = attention_one() if a == 1 else attention_two()
            items = ITEMS1 if a == 1 else ITEMS2
            width, slots = (256, 6) if a == 1 else (512, 4)
            with_chunks(groups, batches, 2 if a == 1 else 4)
            probs = ar(A_P, 4, width)
            pt = ar(A_PT1, 6, 256) if a == 1 else ar(A_PT2, 4, 512)
            lterm = ar(A_LT, 2, 512)
            th = ar(A_TANH, 2, 512)
            s = att[a]
            ng = len(groups)
            pairs = [i for i, g in enumerate(groups) if g["n"] == TB - 1 and batches[g["b"]]["last"]]
            before7, last7 = {}, None
            for i in range(-LOOK - 1, ng + 3):
                if i - 3 in pairs:
                    p = pairs.index(i - 3)
                    before7[("pair", p)], last7 = last7, (s["pair_done"], p + 1)
                if i in items:
                    before7[items[i]], last7 = last7, (FREESEM[EVAC[items[i][0]]], FREE[items[i]][1])

            def probs_of(i):
                g = groups[i]
                if batches[g["b"]]["kind"] == "dil":
                    return ar(A_P + (2048, 2432, 3200, 0)[g["n"]], sum(g["w"]))
                return probs[:, i % 4, :]

            def scores_ap(g, k):
                b, n = batches[g["b"]], g["n"]
                h, w, kind = b["head"], g["w"][k], b["kind"]
                rows, qs = head_rows(h), slice(n * P, (n + 1) * P)
                if kind == "swa":
                    return [(qT[rows, h // 2, qs], kT2[rows, h // 8, (n + 1) * P - w:(n + 1) * P])]
                if kind == "cmp":
                    return [(qn[rows, h // 2, qs], kcT[rows, 0:32])]
                if kind in ("sel", "win"):
                    return [(qn[rows, h // 2, qs], kn[rows, kind == "win", 0:w])]
                if kind == "dil":
                    ks = slice((n + 1) * P - w, (n + 1) * P)
                    q, kk = (xh[rows, k, qs], xl[rows, k, qs]), (xh[rows, 3 + k, ks], xl[rows, 3 + k, ks])
                else:
                    t = 6 + h // 2
                    q, kk = (yh[rows, t, qs], yl[rows, t, qs]), (yh[rows, t + 3, 0:w], yl[rows, t + 3, 0:w])
                return [(q[0], kk[0]), (q[0], kk[1]), (q[1], kk[0])]

            def value_ap(g, s_, kb, K):
                b, n = batches[g["b"]], g["n"]
                h, kind = b["head"], b["kind"]
                if kind == "swa":
                    return vS[:, n + 1 - g["w"][0] // P + kb, HD * (h // 8):HD * (h // 8) + HD]
                if kind == "cmp":
                    return vc[0:K, :]
                if kind in ("sel", "win"):
                    c = HD * (kind == "win")
                    return vn[:, kb, c:c + HD]
                if kind == "dil":
                    c = HD * (2 * s_ + h)
                    return vd[:, n + 1 - g["w"][s_] // P + kb, c:c + HD]
                return vst[:, kb, HD * h:HD * h + HD]

            def pe_part(pe, item):
                def scores(i):
                    g = groups[i]
                    kind, h = batches[g["b"]]["kind"], batches[g["b"]]["head"]
                    if g["n"] == 0 and kind == "stick":
                        pe.wait_ge(heads_split, 2 * (h // 2) + 2)
                    if g["n"] == 0 and kind == "cmp":
                        pe.wait_ge(evac_a, FREE[("kcT", 0)][1])
                    if g["n"] == 0 and kind == "dil":
                        pe.wait_ge(evac_d, FREE[("dT", 5)][1])
                    for k, w in enumerate(g["w"]):
                        st = g["strip0"] + k
                        if st >= 3:
                            pe.wait_ge(s["strip_read"], st - 2)
                        terms = scores_ap(g, k)
                        for t, (q, kk) in enumerate(terms):
                            mm = pe.matmul(B[st % 3][:, 0:w], q, kk, start=t == 0, stop=t == len(terms) - 1)
                        mm.then_inc(s["scores"], 1)

                def turn(i):
                    g = groups[i]
                    pe.wait_ge(s["probs"], i + 1)
                    col0 = probs_of(i)
                    for c, blocks in g["chunks"]:
                        if c >= 2:
                            pe.wait_ge(s[("pt_even", "pt_odd")[c % 2]], c // 2)
                        for j, (_, col, _, K) in enumerate(blocks):
                            mm = pe.transpose(B[3 + c % 2][0:K, j * P:(j + 1) * P], col0[:, col:col + K], ident[:])
                        mm.then_inc(s["pt_ready"], 1)

                def values(i):
                    g = groups[i]
                    b = g["b"]
                    if g["n"] == 0 and b >= 2:
                        pe.wait_ge(s["fin"], b - 1)
                    if g["n"] == 0 and batches[b]["kind"] in ("stick", "dil"):
                        pe.wait_ge(evac_a, FREE[("G4" if batches[b]["kind"] == "stick" else "G3", 3)][1])
                    first, total = True, sum(len(bl) for _, bl in g["chunks"])
                    for c, blocks in g["chunks"]:
                        pe.wait_ge(s[("pt_even", "pt_odd")[c % 2]], c // 2 + 1)
                        for j, (s_, _, kb, K) in enumerate(blocks):
                            total -= 1
                            mm = pe.matmul(B[5 + b % 2][:, g["n"] * HD:(g["n"] + 1) * HD],
                                           pt[0:K, c % slots, j * P:(j + 1) * P], value_ap(g, s_, kb, K),
                                           start=first, stop=total == 0)
                            first = False
                    mm.then_inc(s["o_done"], 1)

                def pair_turn(p):
                    pe.wait_ge(s["fin"], groups[pairs[p]]["b"] + 1)
                    if before7[("pair", p)]:
                        pe.wait_ge(*before7[("pair", p)])
                    for t in range(TB):
                        mm = pe.transpose(B[7][:, t * P:(t + 1) * P], otok[:, p % 2, t, :], ident[:])
                    mm.then_inc(s["pairT"], 1)

                for i in range(-LOOK - 1, ng + 3):
                    if 0 <= i + LOOK + 1 < ng:
                        scores(i + LOOK + 1)
                    if 0 <= i < ng:
                        turn(i)
                    if 0 <= i - 1 < ng:
                        values(i - 1)
                    if i - 3 in pairs:
                        pair_turn(pairs.index(i - 3))
                    if i in items:
                        if before7[items[i]]:
                            pe.wait_ge(*before7[items[i]])
                        item(items[i])

            def act_part(act, item):
                def soft1(i):
                    g = groups[i]
                    b, n = batches[g["b"]], g["n"]
                    pr = probs_of(i)
                    if b["kind"] == "stick":
                        act.wait_ge(s["masked"], stick_count(i) + 1)
                        w = g["w"][0]
                        lt = lterm[:, i % 2, 0:w]
                        act.activation(lt, lt, ACT.Exp).then_inc(s["soft1"], 1)
                        act.wait_ge(s["soft1"], stick_count(i) * 2 + 1)
                        act.activation(lt, lt, ACT.Ln, bias=1.0).then_inc(s["soft1"], 1)
                        return
                    act.wait_ge(s["strip_read"], g["strip0"] + len(g["w"]))
                    col = 0
                    for k, w in enumerate(g["w"]):
                        e = act.activation(pr[:, col:col + w], pr[:, col:col + w], ACT.Exp, scale=-1.0,
                                           bias=negm[:, g["b"] % 4, n:n + 1],
                                           accum_out=rsum[:, g["b"] % 4, n, k:k + 1])
                        col += w
                    e.then_inc(s["probs"], 1)
                    if b["kind"] == "swa" and n == TB - 1:
                        if g["b"] >= 2:
                            act.wait_ge(s["fin"], g["b"] - 1)
                        act.activation(esink[:, g["b"] % 2, :], negm[:, g["b"] % 4, :], ACT.Exp, scale=1.0,
                                       bias=par[:, PC["sinks"] + b["head"]:PC["sinks"] + b["head"] + 1])\
                           .then_inc(s["esum"], 1)

                def soft2(i):
                    g = groups[i]
                    if batches[g["b"]]["kind"] != "stick":
                        return
                    act.wait_ge(s["soft2"], stick_count(i) + 1)
                    pr = probs_of(i)[:, 0:g["w"][0]]
                    act.activation(pr, pr, ACT.Exp).then_inc(s["probs"], 1)

                def copy_out(i):
                    for c, blocks in groups[i]["chunks"]:
                        if c % 2 == 1:
                            pt_copy(act, c, blocks, lambda o, i_: act.activation(o, i_, ACT.Copy))

                for i in range(-LOOK, ng + 3):
                    if 0 <= i + LOOK < ng:
                        soft1(i + LOOK)
                    if 0 <= i + LOOK - 1 < ng:
                        soft2(i + LOOK - 1)
                    if 0 <= i < ng:
                        copy_out(i)
                    if i - 1 in items:
                        item(items[i - 1])
                    if a == 1 and i in pairs:
                        p = pairs.index(i)
                        act.wait_ge(evac_d, FREE[("gate", p)][1])
                        if p >= 2:
                            act.wait_ge(s["pair_done"], p - 1)
                        act.activation(th[:, p % 2, :], sg[:, p, :], ACT.Tanh).then_inc(tanh_done, 1)

            last_of_chunk = {c: i for i, g in enumerate(groups) for c, _ in g["chunks"]}

            def pt_copy(eng, c, blocks, copy):
                eng.wait_ge(s["pt_ready"], c + 1)
                if c >= slots:
                    eng.wait_ge(s["o_done"], last_of_chunk[c - slots] + 1)
                n, K = len(blocks) * P, blocks[0][3]
                copy(pt[0:K, c % slots, 0:n], B[3 + c % 2][0:K, 0:n]).then_inc(s[("pt_even", "pt_odd")[c % 2]], 1)

            def stick_count(i):
                return sum(1 for g in groups[:i] if batches[g["b"]]["kind"] == "stick")

            def dve_part(dve, link, item):
                def make_bias(b):
                    kind, h = b["kind"], b["head"]
                    if kind == "swa":
                        parts = [(A_SWA - A_TAB, 256, float(np.exp2(np.float32(-8.0 * (h + 1) / 16))))]
                    elif kind == "cmp":
                        parts = [(T_CMP, 128, slope10(6 + h))]
                    elif kind in ("sel", "win"):
                        parts = [(T_DC, 512, slope10(6 + h))]
                    else:
                        parts = [(T_D0, 256, slope10(h)), (T_D1, 512, slope10(2 + h)), (T_D2, 512, slope10(4 + h))]
                    at = 0
                    for t, w, slope in parts:
                        last = dve.tensor_scalar(bias[:, at:at + w], ar(A_TAB + t, w), -slope, None, ALU.mult)
                        at += w
                    link(last)

                def mask1(i):
                    g = groups[i]
                    b, n = batches[g["b"]], g["n"]
                    kind = b["kind"]
                    if n == 0 and kind not in ("stick", "win"):
                        make_bias(b)
                    if i >= 4:
                        dve.wait_ge(s["pt_ready"], groups[i - 4]["chunks"][-1][0] + 1)
                    pr = probs_of(i)
                    col = at = 0
                    for k, w in enumerate(g["w"]):
                        st = g["strip0"] + k
                        dve.wait_ge(s["scores"], st + 1)
                        z = B[st % 3][:, 0:w]
                        if kind == "stick":
                            dve.tensor_tensor(pr[:, 0:w], z, tabs[:, T_STK + 512 - w:T_STK + 512], ALU.add)\
                               .then_inc(s["strip_read"], 1)
                            dve.wait_ge(s["strip_read"], st + 1)
                            dve.scalar_tensor_tensor(out=lterm[:, i % 2, 0:w], in0=pr[:, 0:w], scalar=-1.0,
                                                     in1=pr[:, 0:w], op0=ALU.mult, op1=ALU.min)\
                               .then_inc(s["masked"], 1)
                            return
                        if kind == "cmp":
                            bb = bias[:, 32 * n:32 * n + 32]
                        else:
                            tw = 256 if (kind == "swa" or (kind == "dil" and k == 0)) else 512
                            bb = bias[:, at + tw - w:at + tw]
                            at += tw
                        final = k == len(g["w"]) - 1
                        out_m = negm[:, g["b"] % 4, n:n + 1] if final else mtmp[:, k:k + 1]
                        if k > 0:
                            init = mtmp[:, k - 1:k]
                        elif kind == "swa":
                            init = nsink[:, b["head"]:b["head"] + 1]
                        else:
                            init = 1e29 if kind == "cmp" else BIG
                        dve.tensor_tensor_reduce(pr[:, col:col + w], z, bb, -1.0, init, ALU.add, ALU.min, out_m)\
                           .then_inc(s["strip_read"], 1)
                        dve.wait_ge(s["strip_read"], st + 1)
                        col += w

                def mask2(i):
                    g = groups[i]
                    if batches[g["b"]]["kind"] != "stick":
                        return
                    w = g["w"][0]
                    lt, pr = lterm[:, i % 2, 0:w], probs_of(i)[:, 0:w]
                    dve.wait_ge(s["soft1"], 2 * stick_count(i) + 2)
                    link(dve.scalar_tensor_tensor(out=lt, in0=pr, scalar=0.0, in1=lt, op0=ALU.max, op1=ALU.add))
                    link(dve.tensor_tensor_scan(lt[:, ::-1], ones[:, 0:1].to_broadcast([P, w]), lt[:, ::-1],
                                                0.0, ALU.mult, ALU.add))
                    dve.tensor_tensor(pr, pr, lt, ALU.subtract).then_inc(s["soft2"], 1)

                def copy_out(i):
                    for c, blocks in groups[i]["chunks"]:
                        if c % 2 == 0:
                            pt_copy(dve, c, blocks, dve.tensor_copy)

                def finish(bi):
                    b = batches[bi]
                    kind, p = b["kind"], b["turn"]
                    if p >= 2 and not b["half"]:
                        dve.wait_ge(s["pairT"], p - 1)
                    o = B[5 + bi % 2][:, 0:TB * HD].rearrange("p (n d) -> p n d", n=TB)
                    dst = otok[:, p % 2, :, HD * b["half"]:HD * b["half"] + HD]
                    rs = rsum[:, bi % 4, :, 0]
                    if kind == "swa":
                        dve.wait_ge(s["esum"], bi + 1)
                        link(dve.tensor_tensor(den[:], rs, esink[:, bi % 2, :], ALU.add))
                    elif kind == "dil":
                        link(dve.tensor_reduce(den[:], rsum[:, bi % 4, :, :], AX.X, ALU.add))
                    elif kind != "stick":
                        link(dve.tensor_scalar(den[:], rs, 1e-30, None, ALU.max))
                    if kind != "stick":
                        link(dve.reciprocal(den[:], den[:]))
                    if kind in ("cmp", "sel", "win"):
                        link(dve.tensor_tensor(den[:], den[:], gates[:, :, 3 * b["head"] + b["x"]], ALU.mult))
                    dve.wait_ge(s["o_done"], TB * (bi + 1))
                    if kind == "stick":
                        dve.tensor_copy(dst, o).then_inc(s["fin"], 1)
                        return
                    scale = den[:].unsqueeze(2).to_broadcast([P, TB, HD])
                    if kind in ("win", "cmp"):
                        link(dve.tensor_tensor(tmpo[:], o, scale, ALU.mult))
                        dve.tensor_tensor(dst, dst, tmpo[:], ALU.add).then_inc(s["fin"], 1)
                    else:
                        dve.tensor_tensor(dst, o, scale, ALU.mult).then_inc(s["fin"], 1)
                    dve.wait_ge(s["fin"], bi + 1)

                def pair_out(p):
                    dve.wait_ge(s["pairT"], p + 1)
                    to = batches[groups[pairs[p]]["b"]]["pair"]
                    if a == 1:
                        yt = ar(A_BIAS + 256, 512)
                        dve.wait_ge(tanh_done, p + 1)
                        link(dve.scalar_tensor_tensor(out=yt, in0=th[:, p % 2, :], scalar=1.0, in1=sg[:, p, :],
                                                      op0=ALU.add, op1=ALU.mult))
                        dve.tensor_tensor(yt, B[7][:], yt, ALU.mult).then_inc(s["pair_done"], 1)
                        dve.wait_ge(s["pair_done"], p + 1)
                        link(dve.tensor_copy(yh[:, to, :], yt))
                        dve.tensor_tensor(yl[:, to, :], yt, yh[:, to, :], ALU.subtract).then_inc(y_ready, 1)
                    else:
                        link(dve.tensor_copy(yh[:, to, :], B[7][:]))
                        dve.tensor_tensor(yl[:, to, :], B[7][:], yh[:, to, :], ALU.subtract).then_inc(s["pair_done"], 1)

                for i in range(-LOOK, ng + 3):
                    if 0 <= i + LOOK < ng:
                        mask1(i + LOOK)
                    if 0 <= i + LOOK - 1 < ng:
                        mask2(i + LOOK - 1)
                    if 0 <= i < ng:
                        copy_out(i)
                    if 0 <= i - 1 < ng and groups[i - 1]["n"] == TB - 1:
                        finish(groups[i - 1]["b"])
                    if i - 1 in items:
                        item(items[i - 1])
                    if i - 3 in pairs:
                        pair_out(pairs.index(i - 3))

            return pe_part, act_part, dve_part, len(pairs)

        def slope10(i):
            return float(np.exp2(np.float32(-8.0) * np.float32(i + 1) / np.float32(10)))

        nsink = sb("nsink", [P, 16])
        ATT1, ATT2 = make_attention(1), make_attention(2)

        @block.tensor
        def _(pe):
            def three(out, lh, ll, rh, rl, start, stop):
                pe.matmul(out, lh, rh, start=start, stop=False)
                pe.matmul(out, lh, rl, start=False, stop=False)
                return pe.matmul(out, ll, rh, start=False, stop=stop)

            def tile(w, j, k):
                return w[:, j, k * P:(k + 1) * P]

            def feature_major(u, j, out, ah, al, n=KD, ready=None):
                pe.wait_ge(split_done, u + 1)
                for k in range(n):
                    if ready:
                        pe.wait_ge(ready[0], ready[1] + ready[2] * k)
                    mm = three(out, tile(wh, j, k), tile(wl, j, k), ah[:, k, :], al[:, k, :], k == 0, k == n - 1)
                mm.then_inc(units_done, 1)

            def free(key):
                if BEFORE[key]:
                    who, value = BEFORE[key]
                    pe.wait_ge(FREESEM[who], value)

            def token_major(u0, units, width, name, ah, al, ready=None):
                per = KD // units
                for u in range(u0, u0 + units):
                    pe.wait_ge(split_done, u + 1)
                    for kk in range(per):
                        k = (u - u0) * per + kk
                        if ready:
                            pe.wait_ge(ready[0], ready[1] + ready[2] * k)
                        cols = slice(kk * (UNIT // per), kk * (UNIT // per) + width)
                        for t in range(TB):
                            if k == 0:
                                free((name, t))
                            ts = slice(t * P, (t + 1) * P)
                            mm = three(B[BANK[(name, t)]][:, 0:width], ah[:, k, ts], al[:, k, ts],
                                       wh[:, u % RING, cols], wl[:, u % RING, cols], k == 0, k == KD - 1)
                    mm.then_inc(units_done, 1)

            def gate_tile(j):
                u = done[("gate", j)][1] - 1
                if j < 4:
                    free(("gate", j))
                feature_major(u, u % RING, B[BANK[("gate", j)]][:], xh, xl,
                              ready=(xl_ready, KD + 2, 2) if j == 0 else None)

            def sum_squares(q, bank):
                sq = ar(A_P, KD, S)
                for k in range(KD):
                    pe.wait_ge(sq_ready, KD * q + k + 1)
                    for t in range(TB):
                        mm = pe.matmul(bank[:, t:t + 1], sq[:, k, t * P:(t + 1) * P], ones[:, 0:1],
                                       start=k == 0 and t == 0, stop=k == KD - 1, skip_group_check=True)
                mm.then_inc(pe_misc, 1)

            def spread_rstd(q, bank):
                pe.wait_ge(diag_ready, q + 1)
                pe.matmul(bank[:], ones[:], ar(A_BIAS, 512), start=True, stop=True).then_inc(pe_misc, 1)

            pe.wait_ge(ones_set, 1)
            sum_squares(0, B[0])
            spread_rstd(0, B[1])

            def rg_group(g, later):
                for i in range(3):
                    if later:
                        pe.wait_ge(sig_done, 6 * g - 3 + i)
                    elif i < 2:
                        pe.wait_ge((ssq_read, rstd_ready)[i], 1)
                    feature_major(8 * g + i, i, B[i][:], xh, xl, ready=(xl_ready, 1, 1) if not later and i == 0 else None)
                for i in range(3):
                    if later:
                        if i == 0:
                            pe.wait_ge(sig_done, 6 * g)
                        else:
                            pe.wait_ge(gate_evac, 3 * g - 2 + i)
                    feature_major(8 * g + 3 + i, (3 + i) % RING, B[3 + i][:], xh, xl)
                pe.wait_ge(xc_ready, 3 * g + 3)
                for r in range(2):
                    pe.wait_ge(split_done, 8 * g + 7 + r)
                    for n, (ki, o) in enumerate(GATE_TILES):
                        bank = (6 + 3 * r + o) % 8
                        first = n == 0 or GATE_TILES[n - 1][1] != o
                        if first:
                            if bank < 3:
                                pe.wait_ge(xb_evac, 3 * g + bank + 1)
                            elif bank == 3:
                                pe.wait_ge(gate_evac, 3 * g + 1)
                            elif later:
                                pe.wait_ge(sig_done, 6 * g - 11 + bank)
                        mm = three(B[bank][:], tile(wh, 2 + r, n), tile(wl, 2 + r, n), yh[:, 9 + ki, :], yl[:, 9 + ki, :],
                                   first, n == 6 or GATE_TILES[n + 1][1] != o)
                    mm.then_inc(units_done, 1)

            rg_group(0, False)
            with pe.Fori(1, NG) as g:
                rg_group(g, True)

            pe.wait_ge(sig_done, 6 * NG)
            pe.wait_ge(gate_evac, 3 * NG)
            for k in range(9):
                u = U_WOUT + k
                pe.wait_ge(split_done, u + 1)
                pe.wait_ge(y_ready, k // 3 + 1)
                for m in range(KD):
                    mm = three(B[m][:], tile(wh, u % RING, m), tile(wl, u % RING, m), yh[:, k, :], yl[:, k, :], k == 0, False)
                mm.then_inc(units_done, 1)
            pe.wait_ge(split_done, U_WOUT + 12)
            pe.wait_ge(y_ready, NG)
            for m in range(KD):
                for k in range(9, 12):
                    u = U_WOUT + k
                    mm = three(B[m][:], tile(wh, u % RING, m), tile(wl, u % RING, m), yh[:, k, :], yl[:, k, :], False, k == 11)
                    if m == KD - 1:
                        mm.then_inc(units_done, 1)
                if m < KD - 1:
                    mm.then_inc(pe_misc, 1)

            token_major(U_KV, 2, 256, "kv", yh, yl, ready=(xl_ready, KD + 1, 2))
            free(("ssq", 1))
            sum_squares(1, B[BANK[("ssq", 1)]])
            gate_tile(0)
            gate_tile(1)
            free(("rstd", 1))
            spread_rstd(1, B[BANK[("rstd", 1)]])
            token_major(U_Q0, 4, 512, "q0", xh, xl)
            token_major(U_Q1, 4, 512, "q1", xh, xl)
            pe.wait_ge(heads_normed, 1)
            kd = ar(A_OT, TB, 2, P)
            for j in range(2):
                free(("kT", j))
                for t in range(TB):
                    mm = pe.transpose(B[BANK[("kT", j)]][:, t * P:(t + 1) * P], kd[:, t, j, :], ident[:])
                mm.then_inc(pe_misc, 1)
            def turn_queries(half):
                qr = ar((A_QRAW, A_QRAW1)[half], TB, 512)
                pe.wait_ge(heads_normed, 2 + half)
                for j in range(4):
                    key = ("qT", 4 * half + j)
                    free(key)
                    for t in range(TB):
                        mm = pe.transpose(B[BANK[key]][:, t * P:(t + 1) * P], qr[:, t, j * P:(j + 1) * P], ident[:])
                    mm.then_inc(pe_misc, 1)

            turn_queries(0)
            gate_tile(2)
            gate_tile(3)
            turn_queries(1)
            pe.wait_ge(evac_a, FREE[("qT", 7)][1])
            pe.wait_ge(evac_d, FREE[("gate", 3)][1])
            ATT1[0](pe, lambda key: gate_tile(key[1]))

            pe.wait_ge(att[1]["pair_done"], ATT1[3])
            for m in range(KD):
                u = U_BOUT + m
                feature_major(u, u % RING, B[m][:], yh, yl, ready=(y_ready, NG + 1, 1) if m == 0 else None)

            token_major(U_G0, 4, 512, "G0", xh, xl, ready=(xl_ready, 3 * KD + 1, 1))
            free(("ssq", 2))
            sum_squares(2, B[BANK[("ssq", 2)]])
            token_major(U_G1, 4, 396, "G1", xh, xl)
            free(("rstd", 2))
            spread_rstd(2, B[BANK[("rstd", 2)]])

            def f_tile(j):
                u = done[("F", j)][1] - 1
                if j in (0, 1, 4):
                    free(("F", j))
                feature_major(u, u % RING, B[BANK[("F", j)]][:], xh, xl)

            f_tile(0)
            token_major(U_G2, 4, 384, "G2", xh, xl)
            pe.wait_ge(cmp_ready, 1)
            ch, cl = (w[:, 0:2, :].rearrange("p a (l n) -> p (a l) n", n=32) for w in (yh, yl))
            for c in range(2):
                free(("hid", c))
            for u in range(U_W1, U_W1 + 4):
                pe.wait_ge(split_done, u + 1)
                for l8 in range(8):
                    l = (u - U_W1) * 8 + l8
                    for c in range(2):
                        rows = slice(HD * c, HD * c + HD)
                        cols = slice(l8 * P, (l8 + 1) * P)
                        mm = three(B[BANK[("hid", c)]][0:32, 0:P], ch[rows, l, :], cl[rows, l, :],
                                   wh[rows, u % RING, cols], wl[rows, u % RING, cols], l == 0, l == 31)
                mm.then_inc(units_done, 1)
            f_tile(1)
            pe.wait_ge(evac_a, FREE[("hid", 1)][1])
            free(("hT", 0))
            for c in range(2):
                mm = pe.transpose(B[BANK[("hT", 0)]][:, 32 * c:32 * c + 31], hidt[0:31, c, :], ident[0:31, 0:31])
            mm.then_inc(pe_misc, 1)
            f_tile(4)
            pe.wait_ge(evac_a, FREE[("hT", 0)][1])
            free(("kc", 0))
            w2 = par[:, PC["w2"]:PC["w2"] + 2 * HD]
            bk = B[BANK[("kc", 0)]]
            pe.matmul(bk[0:31, 0:HD], hid[:, 0, 0:31], w2[:, 0:HD], start=True, stop=True)
            pe.matmul(bk[0:31, HD:2 * HD], hid[:, 1, 0:31], w2[:, HD:2 * HD], start=True, stop=True).then_inc(pe_misc, 1)
            pe.wait_ge(heads_normed, 4)
            r0, r1, r2 = ar(A_R0, TB, 384), ar(A_R1, TB, 384), ar(A_R2, TB, 384)
            kdn = ar(A_OT, TB, 2, P)
            for j in range(4):
                key = ("nT", j)
                free(key)
                for t in range(TB):
                    src = r0[:, t, j * P:(j + 1) * P] if j < 2 else kdn[:, t, j - 2, :]
                    mm = pe.transpose(B[BANK[key]][:, t * P:(t + 1) * P], src, ident[:])
                mm.then_inc(pe_misc, 1)

            def value_piece(name, t):
                u0 = U_G3 if name == "G3" else U_G4
                ts = slice(t * P, (t + 1) * P)
                for k in range(KD):
                    u, cols = u0 + k // 2, slice(k % 2 * 512, k % 2 * 512 + 384)
                    if k % 2 == 0:
                        pe.wait_ge(split_done, u + 1)
                    mm = three(B[7][:, 0:384], xh[:, k, ts], xl[:, k, ts], wh[:, u % RING, cols], wl[:, u % RING, cols],
                               k == 0, k == KD - 1)
                    if t == TB - 1 and k % 2 == 1:
                        mm.then_inc(units_done, 1)
                if t < TB - 1:
                    mm.then_inc(pe_misc, 1)

            def item(key):
                name, j = key
                if name == "F":
                    f_tile(j)
                elif name in ("G3", "G4"):
                    value_piece(name, j)
                elif name == "kcT":
                    pe.wait_ge(heads_normed, 5)
                    pe.transpose(B[7][:, 0:31], kcd[0:31, :], ident[0:31, 0:31]).then_inc(pe_misc, 1)
                else:
                    for t in range(TB):
                        src = (r1 if j < 3 else r2)[:, t, (j % 3) * P:(j % 3 + 1) * P]
                        mm = pe.transpose(B[7][:, t * P:(t + 1) * P], src, ident[:])
                    mm.then_inc(pe_misc, 1)

            pe.wait_ge(evac_a, FREE[("nT", 3)][1])
            pe.wait_ge(evac_d, FREE[("F", 4)][1])
            ATT2[0](pe, item)

            pe.wait_ge(att[2]["pair_done"], ATT2[3])
            for m in range(KD):
                u = U_OUT2 + m
                feature_major(u, u % RING, B[m][:], yh, yl, n=6)

            def mlp_chunk(c, first, later):
                for i in range(KD):
                    if later:
                        pe.wait_ge(up_read, KD * c + i - 3)
                    elif i >= 4:
                        pe.wait_ge(up_read, i - 3)
                    else:
                        pe.wait_ge(x_new, 2 * KD + i + 1)
                    feature_major(U_MLP + 16 * c + i, (U_MLP + i) % RING, B[i % 4][:], xh, xl,
                                  ready=(xl_ready, 4 * KD + 1, 1) if first and i == 0 else None)
                    if first and i == 1:
                        pe.wait_ge(x_new, 3 * KD)
                        sum_squares(3, B[4])
                    if first and i == 2:
                        spread_rstd(3, B[5])
                for m in range(KD):
                    if later or m >= 4:
                        pe.wait_ge(down_read, KD * c + m - 3)
                    elif m < 2:
                        pe.wait_ge((ssq_read, rstd_ready)[m], 4)
                    feature_major(U_MLP + 16 * c + 8 + m, (U_MLP + m) % RING, B[4 + m % 4][:], yh, yl,
                                  ready=(ff_ready, KD * c + 1, 1) if m == 0 else None)

            mlp_chunk(0, True, False)
            with pe.Fori(1, MLP_CHUNKS) as c:
                mlp_chunk(c, False, True)

        @block.scalar
        def _(act):
            roots = [0]

            def gain(name, k):
                return par[:, PC[name] + k:PC[name] + k + 1]

            def root(rows=P, cols=TB):
                roots[0] += 1
                act.wait_ge(root_ask, roots[0])
                act.activation(v4[0:rows, 1, 0:cols], v4[0:rows, 1, 0:cols], ACT.Sqrt).then_inc(root_done, 1)

            def high_and_square(q, k, ready):
                act.wait_ge(*ready)
                act.activation(xh[:, k, :], x[:, k, :], ACT.Copy, scale=gain(NORM_UNITS[q], k)).then_inc(xh_ready, 1)
                act.activation(ar(A_P, KD, S)[:, k, :], x[:, k, :], ACT.Square).then_inc(sq_ready, 1)

            def take_rstd(q, bank):
                wait_done(act, ("rstd", q))
                act.activation(rstd[:], bank[:], ACT.Copy).then_inc(rstd_ready, 1)

            act.wait_ge(in_par, 32)
            for k in range(KD):
                high_and_square(0, k, (in_x, 16))
            root()
            take_rstd(0, B[1])
            act.wait_ge(lam_ask, 1)
            act.activation(sp[:, 1, :], sp[:, 1, :], ACT.Exp).then_inc(lam_done, 1)

            rg = [ar(1545 + 1536 * i, 3, 512) for i in range(6)]
            xc, gt, rr, ii, aa, th = rg

            def rg_group(g, later):
                if later:
                    act.wait_ge(y_ready, g)
                for r, dst in ((0, rr), (1, ii)):
                    act.wait_ge(units_done, 8 * g + 7 + r)
                    for o in range(3):
                        act.activation(dst[:, o, :], B[(6 + 3 * r + o) % 8][:], ACT.Sigmoid,
                                       bias=gp[:, o, 5 + r:6 + r]).then_inc(sig_done, 1)
                act.wait_ge(gate_evac, 3 * g + 3)
                act.activation(gt[:], gt[:], ACT.Silu)
                act.wait_ge(sig_done, 6 * g + 3)
                for o in range(3):
                    act.activation(aa[:, o, :], rr[:, o, :], ACT.Exp, scale=gp[:, o, 7:8])
                    e = act.activation(th[:, o, :], rr[:, o, :], ACT.Tanh, scale=gp[:, o, 8:9])
                e.then_inc(decay_done, 1)
                act.wait_ge(var_ready, g + 1)
                act.activation(th[:], th[:], ACT.Sqrt).then_inc(var_root, 1)

            rg_group(0, False)
            with act.Fori(1, NG) as g:
                rg_group(g, True)

            for m in range(KD):
                act.wait_ge(x_new, m + 1)
                act.activation(yh[:, m, :], x[:, m, :], ACT.Copy, scale=gain("g_kv", m)).then_inc(xh_ready, 1)
                high_and_square(1, m, (x_new, m + 1))
            root()
            kraw = ar(A_KT, TB, P)
            sqk = ar(A_KT + 512, TB, P)
            act.wait_ge(rx_ready, 2)
            for t in range(TB):
                wait_done(act, ("kv", t))
                bk = B[BANK[("kv", t)]]
                act.activation(kraw[:, t, :], bk[:, 0:P], ACT.Copy)
                e = act.activation(sqk[:, t, :], bk[:, 0:P], ACT.Square)
                if t == TB - 1:
                    e.then_inc(heads_raw, 1)
                act.activation(vS[:, t, :], bk[:, P:2 * P], ACT.Copy, scale=rx[:, t:t + 1]).then_inc(evac_a, 1)
            root(P, TB * 2)
            take_rstd(1, B[BANK[("rstd", 1)]])

            qr, sqh = ar(A_QRAW, TB, 512), ar(A_SQH, TB, 512)

            def raw_heads(name, cols, dst, sq, summed=None, extra=None):
                if summed:
                    act.wait_ge(heads_summed, summed)
                for t in range(TB):
                    wait_done(act, (name, t))
                    bk = B[BANK[(name, t)]]
                    act.activation(dst[:, t, :], bk[:, 0:cols], ACT.Copy)
                    if extra:
                        extra(t, bk)
                    e = act.activation(sq[:, t, :], bk[:, 0:cols], ACT.Square)
                    e.then_inc(evac_a, 1)

            def turned(key, dst, scale):
                wait_done(act, key)
                act.activation(dst, B[BANK[key]][:], ACT.Copy, scale=scale).then_inc(evac_a, 1)

            raw_heads("q0", 512, qr, sqh)
            root(P, TB * 8)
            raw_heads("q1", 512, ar(A_QRAW1, TB, 512), sqh, summed=1)
            for j in range(2):
                turned(("kT", j), kT2[:, j, :], gain("k", 0))
            for j in range(4):
                turned(("qT", j), qT[:, j, :], hsc[:, 0:1])
            root(P, TB * 8)
            for j in range(4, 8):
                turned(("qT", j), qT[:, j, :], hsc[:, 0:1])
            ATT1[1](act, lambda key: None)

            for m in range(KD):
                high_and_square(2, m, (x_new, KD + m + 1))
            root()
            r0, r1, r2 = ar(A_R0, TB, 384), ar(A_R1, TB, 384), ar(A_R2, TB, 384)
            sqg = ar(A_SQG, TB, 384)
            act.wait_ge(rx_ready, 3)
            raw_heads("G0", 384, r0, sqg, extra=lambda t, bk: act.activation(
                vn[:, t, :], bk[:, 384:512], ACT.Copy, scale=rx[:, t:t + 1]))
            raw_heads("G1", 384, r1, sqg, summed=3, extra=lambda t, bk: act.activation(
                gates[:, t, :], bk[:, 384:396], ACT.Sigmoid, scale=rx[:, t:t + 1]))
            take_rstd(2, B[BANK[("rstd", 2)]])
            raw_heads("G2", 384, r2, sqg, summed=4)
            root(P, TB * 18)
            for c in range(2):
                wait_done(act, ("hid", c))
                act.activation(hidt[0:31, c, :], B[BANK[("hid", c)]][0:31, 0:P], ACT.Gelu_apprx_tanh).then_inc(evac_a, 1)
            wait_done(act, ("hT", 0))
            act.activation(hid[:, :, 0:31], B[BANK[("hT", 0)]][:, 0:64].rearrange("p (c n) -> p c n", c=2)[:, :, 0:31],
                           ACT.Copy).then_inc(evac_a, 1)
            wait_done(act, ("kc", 0))
            bk = B[BANK[("kc", 0)]]
            act.activation(vc[0:31, :], bk[0:31, HD:2 * HD], ACT.Copy)
            act.activation(kcr[0:31, :], bk[0:31, 0:HD], ACT.Copy)
            act.activation(ar(A_SQG, HD)[0:31, :], bk[0:31, 0:HD], ACT.Square, accum_out=skc[0:31, :]).then_inc(evac_a, 1)
            for j in range(4):
                turned(("nT", j), (qn[:, j, :] if j < 2 else kn[:, j - 2, :]),
                       hsc[:, 1:2] if j < 2 else gain("nsa", j))
            root(31, 1)

            def item(key):
                name, j = key
                if name in ("G3", "G4"):
                    wait_done(act, key)
                    act.activation((vd if name == "G3" else vst)[:, j, :], B[7][:, 0:384], ACT.Copy,
                                   scale=rx[:, j:j + 1]).then_inc(evac_a, 1)
                elif name == "kcT":
                    wait_done(act, key)
                    act.activation(kcT[:, 0:31], B[7][:, 0:31], ACT.Copy, scale=gain("nsa", 1)).then_inc(evac_a, 1)
                elif name == "dT":
                    wait_done(act, key)
                    act.activation(xh[:, j, :], B[7][:], ACT.Copy,
                                   scale=hsc[:, 2:3] if j < 3 else gain("dil", 1)).then_inc(dil_high, 1)

            act.preload_act_table_set("natural_log_exp_and_others")
            ATT2[1](act, item)

            for m in range(KD):
                high_and_square(3, m, (x_new, 2 * KD + m + 1))
            root()

            up = ar(A_P + 4096, 2, 512)
            sq2 = ar(A_P + 5120, 2, 512)

            def mlp_chunk(c, first):
                for i in range(KD):
                    if first and i == 0:
                        take_rstd(3, B[5])
                    act.wait_ge(up_read, KD * c + i + 1)
                    if not first or i >= 2:
                        act.wait_ge(ff_ready, KD * c + i - 1)
                    act.activation(sq2[:, i % 2, :], up[:, i % 2, :], ACT.Square)
                    act.activation(yh[:, i, :], up[:, i % 2, :], ACT.Square).then_inc(up_sq, 1)

            mlp_chunk(0, True)
            with act.Fori(1, MLP_CHUNKS) as c:
                mlp_chunk(c, False)

        @block.vector
        def _(dve):
            steps = [0]
            base = [0]
            asks = [0]

            def link(ins):
                steps[0] += 1
                ins.then_inc(dve_step, 1)
                dve.wait_ge(dve_step, base[0] + steps[0])

            def gain(name, k):
                return par[:, PC[name] + k:PC[name] + k + 1]

            def rsqrt(rows, cols, y):
                v, r, t = (v4[0:rows, i, 0:cols] for i in range(3))
                dve.reciprocal(r, v).then_inc(root_ask, 1)
                asks[0] += 1
                dve.wait_ge(root_done, asks[0])
                link(dve.tensor_tensor(t, v, r, ALU.mult))
                link(dve.tensor_tensor(t, t, r, ALU.mult))
                link(dve.tensor_scalar(t, t, -0.5, 1.5, ALU.mult, ALU.add))
                return dve.tensor_tensor(y, r, t, ALU.mult)

            def low_part(k, dh, dl, name, high_count):
                dve.wait_ge(xh_ready, high_count)
                dve.scalar_tensor_tensor(out=dl[:, k, :], in0=x[:, k, :], scalar=gain(name, k), in1=dh[:, k, :],
                                         op0=ALU.mult, op1=ALU.subtract).then_inc(xl_ready, 1)

            def token_norm(q, bank):
                wait_done(dve, ("ssq", q))
                dve.tensor_scalar(v4[:, 0, 0:TB], bank[:, 0:TB], 1.0 / D, EPS, ALU.mult, ALU.add).then_inc(ssq_read, 1)
                dve.wait_ge(ssq_read, q + 1)
                rsqrt(P, TB, rx[:]).then_inc(rx_ready, 1)
                dve.wait_ge(rx_ready, q + 1)
                diag = ar(A_BIAS, TB, P)
                for t in range(TB):
                    d_ = dve.tensor_scalar(diag[:, t, :], ident[:], rx[:, t:t + 1], None, ALU.mult)
                d_.then_inc(diag_ready, 1)

            dve.memset(kcT[:], 0.0)
            dve.memset(ones[:], 1.0).then_inc(ones_set, 1)
            dve.wait_ge(ones_set, 1)
            ub = ar(0, 3, 515)
            xc, gt, rr, ii, aa, th = [ar(1545 + 1536 * i, 3, 512) for i in range(6)]
            dve.wait_ge(in_x, 16)
            dve.wait_ge(in_par, 32)
            for k in range(KD):
                low_part(k, xh, xl, "g_a", k + 1)
            token_norm(0, B[0])
            dve.tensor_scalar(hsc[:, 0:1], gain("q", 0), HD ** -0.5, None, ALU.mult)
            dve.tensor_scalar(hsc[:, 1:2], gain("nsa", 0), HD ** -0.5, None, ALU.mult)
            dve.tensor_scalar(hsc[:, 2:3], gain("dil", 0), HD ** -0.5, None, ALU.mult)
            dve.tensor_scalar(nsink[:], par[:, PC["sinks"]:PC["sinks"] + 16], -1.0, None, ALU.mult)
            lam = par[:, 0:NG * 3 * NRG].rearrange("p (t c) -> p t c", c=NRG)[:, :, 7]
            nlam = par[:, 0:NG * 3 * NRG].rearrange("p (t c) -> p t c", c=NRG)[:, :, 8]
            s0, s1, s2, s3 = (sp[:, i, :] for i in range(4))
            dve.scalar_tensor_tensor(out=s1, in0=lam, scalar=-1.0, in1=lam, op0=ALU.mult, op1=ALU.min).then_inc(lam_ask, 1)
            dve.wait_ge(lam_done, 1)
            link(dve.tensor_scalar(s2, s1, 2.0, None, ALU.add))
            link(dve.reciprocal(s2, s2))
            link(dve.tensor_tensor(s1, s1, s2, ALU.mult))
            link(dve.tensor_tensor(s2, s1, s1, ALU.mult))
            link(dve.tensor_scalar(s3, s2, 1.0 / 17.0, None, ALU.mult))
            for c in (15, 13, 11, 9, 7, 5, 3):
                link(dve.scalar_tensor_tensor(out=s3, in0=s3, scalar=1.0 / c, in1=s2, op0=ALU.add, op1=ALU.mult))
            link(dve.scalar_tensor_tensor(out=s3, in0=s3, scalar=1.0, in1=s1, op0=ALU.add, op1=ALU.mult))
            link(dve.tensor_scalar(s0, lam, -1.0, 0.0, ALU.mult, ALU.max))
            link(dve.scalar_tensor_tensor(out=s0, in0=s3, scalar=2.0, in1=s0, op0=ALU.mult, op1=ALU.add))
            link(dve.tensor_scalar(lam, s0, -8.0, None, ALU.mult))
            link(dve.tensor_scalar(nlam, s0, 8.0, None, ALU.mult))
            link(dve.memset(ub[:, :, 0:3], 0.0))

            def rg_conv(g):
                at = slice(3 * NRG * g, 3 * NRG * (g + 1)) if isinstance(g, int) else bass.ds(3 * NRG * g, 3 * NRG)
                link(dve.tensor_copy(gp[:].rearrange("p a b -> p (a b)"), par[:, at]))
                for i in range(3):
                    dve.wait_ge(units_done, 8 * g + i + 1)
                    dve.tensor_tensor(ub[:, i, 3:515], B[i][:], rstd[:], ALU.mult).then_inc(xb_evac, 1)
                    dve.wait_ge(xb_evac, 3 * g + i + 1)
                    link(dve.tensor_scalar(xc[:, i, :], ub[:, i, 0:512], gp[:, i, 0:1], gp[:, i, 4:5], ALU.mult, ALU.add))
                    for j in range(1, 4):
                        link(dve.scalar_tensor_tensor(out=xc[:, i, :], in0=ub[:, i, j:j + 512], scalar=gp[:, i, j:j + 1],
                                                      in1=xc[:, i, :], op0=ALU.mult, op1=ALU.add))
                    link(dve.tensor_copy(yh[:, 9 + i, :], xc[:, i, :]))
                    dve.tensor_tensor(yl[:, 9 + i, :], xc[:, i, :], yh[:, 9 + i, :], ALU.subtract).then_inc(xc_ready, 1)

            def rg_gate(g):
                for i in range(3):
                    dve.wait_ge(units_done, 8 * g + 4 + i)
                    dve.tensor_tensor(gt[:, i, :], B[3 + i][:], rstd[:], ALU.mult).then_inc(gate_evac, 1)

            def rg_variance(g):
                dve.wait_ge(sig_done, 6 * g + 6)
                link(dve.tensor_tensor(ii[:], ii[:], xc[:], ALU.mult))
                dve.wait_ge(decay_done, g + 1)
                link(dve.tensor_tensor(rr[:], aa[:], aa[:], ALU.mult))
                dve.scalar_tensor_tensor(out=th[:], in0=rr[:], scalar=1.0, in1=th[:], op0=ALU.add, op1=ALU.mult)\
                   .then_inc(var_ready, 1)

            def rg_recurrence(g):
                dve.wait_ge(var_root, g + 1)
                link(dve.tensor_tensor(ii[:], ii[:], th[:], ALU.mult))
                for i in range(3):
                    link(dve.tensor_tensor_scan(rr[:, i, :], aa[:, i, :], ii[:, i, :], 0.0, ALU.mult, ALU.add))
                link(dve.tensor_tensor(rr[:], rr[:], gt[:], ALU.mult))
                at = slice(3 * g, 3 * g + 3) if isinstance(g, int) else bass.ds(3 * g, 3)
                dve.tensor_scalar(yh[:, at, :], rr[:], 1.0, None, ALU.mult).then_inc(rg_high, 1)
                dve.wait_ge(rg_high, g + 1)
                dve.tensor_tensor(yl[:, at, :], rr[:], yh[:, at, :], ALU.subtract).then_inc(y_ready, 1)

            RG_LINKS = 1 + 3 * 5 + 7
            dve.wait_ge(rstd_ready, 1)
            rg_conv(0)
            rg_gate(0)
            before = steps[0]
            with dve.Fori(1, NG) as g:
                base[0], steps[0] = (g - 1) * RG_LINKS + before, 0
                rg_variance(g - 1)
                rg_conv(g)
                rg_recurrence(g - 1)
                rg_gate(g)
                assert steps[0] == RG_LINKS, steps
            base[0], steps[0] = before + (NG - 1) * RG_LINKS, 0
            rg_variance(NG - 1)
            rg_recurrence(NG - 1)

            dve.wait_ge(y_ready, NG)
            for m in range(KD):
                wait_done(dve, ("wout", m))
                dve.tensor_tensor(x[:, m, :], B[m][:], x[:, m, :], ALU.add).then_inc(x_new, 1)
                dve.wait_ge(x_new, m + 1)
                low_part(m, yh, yl, "g_kv", KD + 2 * m + 1)
                low_part(m, xh, xl, "g_b", KD + 2 * m + 2)

            token_norm(1, B[BANK[("ssq", 1)]])

            def head_scales(n):
                v = head_view(0, n)
                link(dve.tensor_tensor(rx2[:], rx[:], rx[:], ALU.mult))
                link(dve.tensor_tensor(v, v, rx2[:].unsqueeze(2).to_broadcast([P, TB, n]), ALU.mult))
                link(dve.tensor_scalar(v4[:, 0, 0:TB * n], v4[:, 0, 0:TB * n], 1.0 / HD, EPS, ALU.mult, ALU.add))
                link(rsqrt(P, TB * n, v4[:, 1, 0:TB * n]))
                link(dve.tensor_tensor(head_view(2, n), head_view(1, n), rx[:].unsqueeze(2).to_broadcast([P, TB, n]),
                                       ALU.mult))

            kraw, sqk = ar(A_KT, TB, P), ar(A_KT + 512, TB, P)
            kd = ar(A_OT, TB, 2, P)
            dve.wait_ge(heads_raw, 1)
            link(dve.tensor_reduce(head_view(0, 2), sqk[:].rearrange("p t (h d) -> p t h d", d=HD), AX.X, ALU.add))
            head_scales(2)
            rq = head_view(2, 2)
            for j in range(2):
                for t in range(TB):
                    e = dve.tensor_scalar(kd[:, t, j, :].rearrange("p (c d) -> p c d", c=2),
                                          kraw[:, t, HD * j:HD * j + HD].unsqueeze(1).to_broadcast([P, 2, HD]),
                                          rq[:, t, j:j + 1], None, ALU.mult)
            e.then_inc(heads_normed, 1)

            def gate_tile(j):
                wait_done(dve, ("gate", j))
                dve.scalar_tensor_tensor(out=sg[:, j, :], in0=B[BANK[("gate", j)]][:], scalar=0.5, in1=rstd[:],
                                         op0=ALU.mult, op1=ALU.mult).then_inc(evac_d, 1)

            dve.wait_ge(rstd_ready, 2)
            gate_tile(0)
            gate_tile(1)
            sqh = ar(A_SQH, TB, 512)

            def norm_queries(half):
                qr = ar((A_QRAW, A_QRAW1)[half], TB, 512)
                dve.wait_ge(evac_a, FREE[(f"q{half}", TB - 1)][1])
                dve.tensor_reduce(head_view(0, 8), sqh[:].rearrange("p t (h d) -> p t h d", d=HD), AX.X, ALU.add)\
                   .then_inc(heads_summed, 1)
                dve.wait_ge(heads_summed, half + 1)
                head_scales(8)
                rq = head_view(2, 8)
                for t in range(TB):
                    q4 = qr[:, t, :].rearrange("p (h d) -> p h d", d=HD)
                    e = dve.tensor_tensor(q4, q4, rq[:, t, 0:8].unsqueeze(2).to_broadcast([P, 8, HD]), ALU.mult)
                e.then_inc(heads_normed, 1)

            norm_queries(0)
            norm_queries(1)
            gate_tile(2)
            gate_tile(3)
            dve.wait_ge(in_tab, 32)
            dve.wait_ge(evac_a, FREE[("qT", 7)][1])
            ATT1[2](dve, link, lambda key: gate_tile(key[1]))

            for m in range(KD):
                wait_done(dve, ("bout", m))
                dve.tensor_tensor(x[:, m, :], B[m][:], x[:, m, :], ALU.add).then_inc(x_new, 1)
                dve.wait_ge(x_new, KD + m + 1)
                low_part(m, xh, xl, "g_mix", 3 * KD + m + 1)
            token_norm(2, B[BANK[("ssq", 2)]])

            r0, r1, r2 = ar(A_R0, TB, 384), ar(A_R1, TB, 384), ar(A_R2, TB, 384)
            sqg = ar(A_SQG, TB, 384)

            def sum_heads(name, at, count):
                dve.wait_ge(evac_a, FREE[(name, TB - 1)][1])
                dve.tensor_reduce(head_view(0, 18)[:, :, at:at + 6], sqg[:].rearrange("p t (h d) -> p t h d", d=HD), AX.X, ALU.add)\
                   .then_inc(heads_summed, 1)
                dve.wait_ge(heads_summed, count)

            sum_heads("G0", 0, 3)
            sum_heads("G1", 6, 4)
            dve.wait_ge(rstd_ready, 3)
            ct, rawc = ar(A_CT, 512), ar(A_RAW, 32, 32)
            wait_done(dve, ("F", 0))
            dve.tensor_tensor(ct, B[BANK[("F", 0)]][:], rstd[:], ALU.mult).then_inc(evac_d, 1)
            dve.wait_ge(evac_d, FREE[("F", 0)][1])
            link(dve.memset(rawc[:, :, 31:32], 0.0))
            cv = ct.rearrange("p (n s) -> p s n", s=16)
            pe_ = par[:, PC["pe"]:PC["pe"] + 32]
            for half in range(2):
                e = dve.tensor_tensor(rawc[:, 16 * half:16 * half + 16, 0:31], cv[:, :, half:half + 31],
                                      pe_[:, 16 * half:16 * half + 16].unsqueeze(2).to_broadcast([P, 16, 31]), ALU.add)
            link(e)
            rc = rawc[:].rearrange("p l n -> p (l n)").rearrange("p (a b) -> p a b", a=2)
            link(dve.tensor_copy(yh[:, 0:2, :], rc))
            dve.tensor_tensor(yl[:, 0:2, :], rc, yh[:, 0:2, :], ALU.subtract).then_inc(cmp_ready, 1)
            sum_heads("G2", 12, 5)
            head_scales(18)
            rq = head_view(2, 18)
            for t in range(TB):
                for rr_, at, n in ((r0, 0, 4), (r1, 6, 6), (r2, 12, 6)):
                    h4 = rr_[:, t, 0:HD * n].rearrange("p (h d) -> p h d", d=HD)
                    dve.tensor_tensor(h4, h4, rq[:, t, at:at + n].unsqueeze(2).to_broadcast([P, n, HD]), ALU.mult)
                for j in range(2):
                    e = dve.tensor_scalar(kd[:, t, j, :].rearrange("p (c d) -> p c d", c=2),
                                          r0[:, t, 256 + HD * j:256 + HD * j + HD].unsqueeze(1).to_broadcast([P, 2, HD]),
                                          rq[:, t, 4 + j:5 + j], None, ALU.mult)
            e.then_inc(heads_normed, 1)
            st = ar(A_ST, 512)

            def split_f(j):
                wait_done(dve, ("F", j))
                dve.scalar_tensor_tensor(out=st, in0=B[BANK[("F", j)]][:], scalar=HD ** -0.5 if j < 4 else 1.0,
                                         in1=rstd[:], op0=ALU.mult, op1=ALU.mult).then_inc(evac_d, 1)
                dve.wait_ge(evac_d, FREE[("F", j)][1])
                link(dve.tensor_copy(yh[:, 5 + j, :], st))
                dve.tensor_tensor(yl[:, 5 + j, :], st, yh[:, 5 + j, :], ALU.subtract).then_inc(heads_split, 1)
                dve.wait_ge(heads_split, {1: 1, 4: 2, 2: 3, 5: 4, 3: 5, 6: 6}[j])

            wait_done(dve, ("hT", 0))
            split_f(1)
            split_f(4)
            dve.wait_ge(evac_a, FREE[("kc", 0)][1])
            link(dve.tensor_scalar(v4[0:31, 0, 0:1], skc[0:31, :], 1.0 / HD, EPS, ALU.mult, ALU.add))
            link(rsqrt(31, 1, v4[0:31, 1, 0:1]))
            dve.tensor_scalar(kcd[0:31, :].rearrange("p (c d) -> p c d", c=2),
                              kcr[0:31, :].unsqueeze(1).to_broadcast([31, 2, HD]),
                              v4[0:31, 1, 0:1], None, ALU.mult).then_inc(heads_normed, 1)

            def item(key):
                name, j = key
                if name == "F":
                    split_f(j)
                elif name == "dT":
                    dve.wait_ge(dil_high, j + 1)
                    dve.scalar_tensor_tensor(out=xl[:, j, :], in0=B[7][:], scalar=hsc[:, 2:3] if j < 3 else gain("dil", 1),
                                             in1=xh[:, j, :], op0=ALU.mult, op1=ALU.subtract).then_inc(evac_d, 1)

            dve.wait_ge(evac_a, FREE[("nT", 3)][1])
            ATT2[2](dve, link, item)

            for m in range(KD):
                wait_done(dve, ("out2", m))
                dve.tensor_tensor(x[:, m, :], B[m][:], x[:, m, :], ALU.add).then_inc(x_new, 1)
                dve.wait_ge(x_new, 2 * KD + m + 1)
                low_part(m, xh, xl, "g_mlp", 4 * KD + m + 1)
            token_norm(3, B[4])

            up, sq2 = ar(A_P + 4096, 2, 512), ar(A_P + 5120, 2, 512)
            dve.wait_ge(rstd_ready, 4)

            def mlp_chunk(c, first):
                def relu(i):
                    dve.wait_ge(units_done, U_MLP + 16 * c + i + 1)
                    if not first or i >= 2:
                        dve.wait_ge(up_sq, KD * c + i - 1)
                    dve.scalar_tensor_tensor(out=up[:, i % 2, :], in0=B[i % 4][:], scalar=0.0, in1=rstd[:],
                                             op0=ALU.max, op1=ALU.mult).then_inc(up_read, 1)

                def low(i):
                    dve.wait_ge(up_sq, KD * c + i + 1)
                    dve.tensor_tensor(yl[:, i, :], sq2[:, i % 2, :], yh[:, i, :], ALU.subtract).then_inc(ff_ready, 1)

                for i in range(KD):
                    relu(i)
                    low(i)
                for m in range(KD):
                    dve.wait_ge(units_done, U_MLP + 16 * c + 8 + m + 1)
                    dve.tensor_tensor(x[:, m, :], B[4 + m % 4][:], x[:, m, :], ALU.add).then_inc(down_read, 1)

            mlp_chunk(0, True)
            with dve.Fori(1, MLP_CHUNKS) as c:
                mlp_chunk(c, False)


def _tables():
    FAR = 1e33
    i = np.arange(P)[:, None]

    def dist(cols, first, ok):
        d = (first + i - np.arange(cols)[None, :]).astype(np.float64)
        return np.where(ok(d), d, FAR)

    t = np.zeros((P, NTAB), np.float32)
    t[:, T_D0:T_D0 + 256] = dist(256, 128, lambda d: (d >= 0) & (d <= 128))
    t[:, T_D1:T_D1 + 512] = dist(512, 384, lambda d: (d >= 0) & (d % 4 == 0))
    t[:, T_D2:T_D2 + 512] = dist(512, 384, lambda d: (d >= 0) & (d % 16 == 0))
    t[:, T_DC:T_DC + 512] = dist(512, 384, lambda d: d >= 0)
    t[:, T_STK:T_STK + 512] = np.where(dist(512, 384, lambda d: d > 0) < FAR, 0.0, -BIG)
    for n in range(TB):
        for w in range(32):
            d = n * P + np.arange(P) - (16 * w + 31)
            t[:, T_CMP + 32 * n + w] = np.where((d >= 0) & (w < 31), d, FAR)
    return t, np.ascontiguousarray(dist(256, 128, lambda d: (d >= 0) & (d < 128)).astype(np.float32))


def _feature_units(w):
    k, m = w.shape[0] // P, w.shape[1] // P
    u = w.reshape(k, P, m, P).transpose(2, 1, 0, 3).reshape(m, P, k * P)
    return np.pad(u, ((0, 0), (0, 0), (0, UNIT - k * P)))


def _token_units(w, units):
    cols = UNIT * units // KD
    w = np.pad(w, ((0, 0), (0, cols - w.shape[1])))
    return w.reshape(units, KD // units, P, cols).transpose(0, 2, 1, 3).reshape(units, P, UNIT)


def _gate_unit(blocks):
    full = np.zeros((3 * P, 3 * P), np.float32)
    n = blocks.shape[1]
    for b in range(blocks.shape[0]):
        full[b * n:(b + 1) * n, b * n:(b + 1) * n] = blocks[b]
    unit = np.zeros((1, P, 8, P), np.float32)
    for t, (i, o) in enumerate(GATE_TILES):
        unit[0, :, t] = full[i * P:(i + 1) * P, o * P:(o + 1) * P]
    return unit.reshape(1, P, UNIT)


def kernel(**inputs):
    import concourse.bacc as _bacc
    from concourse.bass_utils import run_bass_kernel_spmd as _run

    a = {k: np.asarray(v) for k, v in inputs.items()}
    xb, gate = _feature_units(a["a_w_in"][0][:, :R]), _feature_units(a["a_w_in"][0][:, R:])
    parts = []
    for g in range(NG):
        parts += [xb[3 * g:3 * g + 3], gate[3 * g:3 * g + 3], _gate_unit(a["a_gate_r_w"][0][4 * g:4 * g + 4]),
                  _gate_unit(a["a_gate_i_w"][0][4 * g:4 * g + 4])]
    parts.append(a["a_w_out"][0].reshape(RT, P, D))
    parts.append(_token_units(a["w_kv"], 2))
    bq, bg = a["b_w_in"][0][:, :D], _feature_units(a["b_w_in"][0][:, D:])
    parts += [bg[0:2], _token_units(bq[:, 0:512], 4), _token_units(bq[:, 512:], 4), bg[2:8]]
    parts.append(_feature_units(a["b_w_out"][0]))
    w = a["w_in_2"][0]
    q_, kc, vc, ks, vs, kw, vw, gl = np.split(w[:, 0:652], [256, 320, 384, 448, 512, 576, 640], axis=1)
    dq, dk, dv = np.split(w[:, 652:652 + 1152], 3, axis=1)
    sq, sk, sv = np.split(w[:, 652 + 1152:], 3, axis=1)
    parts.append(_token_units(np.concatenate([q_, ks, kw, vs, vw], 1), 4))
    parts.append(_token_units(np.concatenate([dq, gl], 1), 4))
    parts.append(_feature_units(np.concatenate([kc, vc], 1)))
    parts.append(_token_units(dk, 4))
    parts.append(a["cmp_w1_2"][0].reshape(2, 4, 8, HD, P).transpose(1, 0, 3, 2, 4).reshape(4, P, UNIT))
    qk = _feature_units(np.concatenate([sq, sk], 1))
    parts += [qk[0:6:3], _token_units(sv, 4), qk[1:6:3], _token_units(dv, 4), qk[2:6:3], _feature_units(a["w_out_2"][0])]
    up = _feature_units(a["w_up_2"][0])
    for c in range(MLP_CHUNKS):
        parts += [up[8 * c:8 * c + 8], _feature_units(a["w_down_2"][0][c * D:(c + 1) * D])]
    weights = np.ascontiguousarray(np.concatenate(parts, 0))
    assert weights.shape == (UNITS, P, UNIT), weights.shape
    rg = np.stack([*a["a_conv_w"][0], a["a_conv_b"][0], a["a_gate_r_b"][0], a["a_gate_i_b"][0], a["a_lambda"][0],
                   a["a_lambda"][0]])
    twice = lambda g: np.concatenate([g, g], -1).T
    cols = [rg.reshape(NRG, RT, P).transpose(2, 1, 0).reshape(P, RT * NRG)]
    cols += [a[n].reshape(KD, P).T for n in ("a_norm_g", "kv_norm_g", "b_norm_g", "norm_mix_2", "norm_mlp_2")]
    cols += [twice(a["q_norm_g"]), twice(a["k_norm_g"][None]), twice(a["qk_gain_nsa_2"][0]), twice(a["qk_gain_dil_2"][0])]
    cols += [np.broadcast_to(a["sinks"], (P, 16)), a["cmp_pe_2"][0].transpose(0, 2, 1).reshape(P, 32)]
    cols += [a["cmp_w2_2"][0].transpose(1, 0, 2).reshape(P, 2 * HD)]
    params = np.ascontiguousarray(np.concatenate(cols, 1))
    assert params.shape == (P, NPAR), params.shape
    arrays = {
        "x_in": np.ascontiguousarray(a["x"][0].T.reshape(KD, P, S).transpose(1, 0, 2)),
        "weight_units": weights,
        "params": params,
        "tables": _tables()[0],
        "swa_table": _tables()[1],
        "identity": np.eye(P, dtype=np.float32),
    }
    nc = _bacc.Bacc("TRN2", target_bir_lowering=False, num_devices=1, dynamic_dma_scratch_size=1024)
    args = [nc.dram_tensor(n, v.shape, mybir.dt.from_np(v.dtype), kind="ExternalInput").ap() for n, v in arrays.items()]
    out = nc.dram_tensor("out_fm", (P, KD, S), F32, kind="ExternalOutput").ap()
    two_block_kernel(nc, *args, out)
    r = _run(nc, [arrays], core_ids=[0])
    y = np.asarray(r.results[0]["out_fm"])
    return np.ascontiguousarray(y.transpose(2, 1, 0).reshape(1, S, D))
```

```python
from contextlib import ExitStack

import numpy as np

import concourse.bass as bass
from concourse import mybir

F32 = mybir.dt.float32
F32R = mybir.dt.float32r
ALU = mybir.AluOpType
ACT = mybir.ActivationFunctionType
AX = mybir.AxisListType

P = 128
D = 1024
S = 512
KD = D // P
TB = S // P
R = 1536
RT = R // P
NG = 4
HD = 64
EPS = 1e-6
BIG = 1e30
UNIT = 1024
RING = 4
GATE_TILES = [(0, 0), (1, 0), (0, 1), (1, 1), (2, 1), (1, 2), (2, 2)]

U_RG = 0
U_WOUT = U_RG + 8 * NG
U_KV = U_WOUT + RT
U_GA = U_KV + 2
U_Q0 = U_GA + 2
U_Q1 = U_Q0 + 4
U_GB = U_Q1 + 4
U_BOUT = U_GB + 6
U_G0 = U_BOUT + 8
U_G1 = U_G0 + 4
U_F0 = U_G1 + 4
U_G2 = U_F0 + 1
U_W1 = U_G2 + 4
U_FA = U_W1 + 4
U_G4 = U_FA + 2
U_FB = U_G4 + 4
U_G3 = U_FB + 2
U_FC = U_G3 + 4
U_OUT2 = U_FC + 2
U_MLP = U_OUT2 + 8
MLP_CHUNKS = 4
UNITS = U_MLP + 16 * MLP_CHUNKS

NRG = 9
PC = {}
_at = 0
for _name, _n in [("rg", NG * 3 * NRG), ("g_a", KD), ("g_kv", KD), ("g_b", KD), ("g_mix", KD), ("g_mlp", KD),
                  ("q", 1), ("k", 1), ("nsa", 4), ("dil", 2), ("sinks", 16), ("pe", 32), ("w2", 2 * HD)]:
    PC[_name] = _at
    _at += _n
NPAR = _at

A_P = 0
A_QRAW, A_SQH = 0, 2048
A_QT, A_KT, A_VS, A_SG = 4096, 8192, 9216, 9728
A_OT, A_BIAS, A_TAB = 14208, 15232, 16512
A_SWA = A_BIAS + 768
A_HID, A_KCR, A_KCD = A_BIAS + 1024, A_BIAS + 1088, A_BIAS + 1152
A_RG = A_OT
A_END = A_TAB + 2048
A_PT1, A_PT2 = 1024, 5504
A_R0, A_R1, A_R2, A_SQG, A_CT, A_RAW = 0, 2048, 3584, 5120, 6656, 7168
A_CT1 = 5120
A_LT = 7552
A_ST, A_TMPO = A_BIAS + 512, A_BIAS + 1024
A_HIDT = A_BIAS + 512
A_QRAW1 = A_SG + 2048
A_TANH = 2560
A_YT = (3584, A_BIAS + 256)
A_VD, A_VST, A_VN, A_QN, A_KN = 8576, 10112, 11648, 12160, 13184
T_D0, T_D1, T_D2, T_DC, T_STK, T_CMP = 0, 256, 768, 1280, 1792, 1920
NTAB = 2048


ITEMS1 = {-3: ("gate", 4, 8), 14: ("gate", 5, 6), 30: ("gate", 6, 6), 46: ("gate", 7, 6)}
ITEMS2 = {-3: ("G4", 0, 4), 2: ("kcT", 0, 1), 3: ("G4", 1, 3), 6: ("G4", 2, 3), 9: ("G4", 3, 3),
          14: ("F", 2, 3), 17: ("F", 5, 3), 20: ("dT", 0, 1), 22: ("dT", 1, 1), 24: ("G3", 0, 4), 30: ("G3", 1, 6),
          38: ("G3", 2, 6), 46: ("G3", 3, 5), 51: ("dT", 2, 1), 53: ("dT", 3, 1), 55: ("dT", 4, 1), 57: ("dT", 5, 1),
          58: ("F", 3, 5), 63: ("F", 6, 4)}
TURN_LAG, OUT_LAG = 5, 6
TAIL = {-1: (0,), 0: (1,), 1: (2,), TURN_LAG - 1: (3,)}
BEGUN = 4
EVAC = {"gate": "D", "G4": "A", "kcT": "A", "F": "D", "G3": "A", "dT": "A"}
F_UNIT = {0: U_F0, 1: U_FA, 4: U_FA + 1, 2: U_FB, 5: U_FB + 1, 3: U_FC, 6: U_FC + 1}


def plan():
    seg1 = [("wout", m, "X") for m in range(8)] + [("kv", t, "A") for t in range(4)] + [("ssq", 1, "N")]
    seg1 += [("gate", 0, "D"), ("gate", 1, "D"), ("rstd", 1, "B")] + [("q0", t, "A") for t in range(4)]
    seg1 += [("q1", t, "A") for t in range(4)] + [("kT", j, "A") for j in range(2)]
    seg1 += [("qT", j, "A") for j in range(4)] + [("gate", j, "D") for j in (2, 3)]
    seg1 += [("qT", j, "A") for j in range(4, 8)]
    seg2 = [("bout", m, "X") for m in range(8)] + [("G0", t, "A") for t in range(4)] + [("ssq", 2, "N")]
    seg2 += [("G1", t, "A") for t in range(4)] + [("rstd", 2, "B"), ("F", 0, "D")]
    seg2 += [("G2", t, "A") for t in range(4)] + [("hid", 0, "A"), ("hid", 1, "A"), ("F", 1, "D"), ("hT", 0, "A")]
    seg2 += [("nT", j, "A") for j in range(4)] + [("kc", 0, "A"), ("F", 4, "D")]
    bank, free, before = {}, {}, {}
    count = {"A": 0, "D": 0}
    for seg, items in ((seg1, ITEMS1), (seg2, ITEMS2)):
        for i, (name, j, who) in enumerate(seg):
            key = (name, j)
            bank[key] = i % 8
            if who in count:
                count[who] += 1
                free[key] = (who, count[who])
            elif who == "X":
                free[key] = (who, j + 1 + (8 if name == "bout" else 0))
            else:
                free[key] = (who, j + 1)
            before[key] = free[seg[i - 8][:2]] if i >= 8 else None
        for key in (item[:2] for item in items.values()):
            bank[key] = 7
            count[EVAC[key[0]]] += 1
            free[key] = (EVAC[key[0]], count[EVAC[key[0]]])
    bank["F", 4], before["F", 4] = bank["nT", 0], free["nT", 0]
    return bank, free, before


def attention_one():
    batches = [dict(kind="swa", head=h, pair=h // 2, half=h % 2, last=h % 2 == 1,
                    turn=h // 2) for h in range(16)]
    groups = [dict(b=h, n=n, w=[128 if n == 0 else 256]) for h in range(16) for n in range(TB)]
    return batches, groups


def attention_two():
    def nsa(p):
        return [dict(kind=kind, head=2 * p + h, x=x, pair=p, half=h, last=(h == 1 and x == 0))
                for h in range(2) for x, kind in ((1, "sel"), (2, "win"), (0, "cmp"))]

    def stick(p):
        return [dict(kind="stick", head=2 * p + h, pair=3 + p, half=h, last=h == 1) for h in range(2)]

    dil = [dict(kind="dil", head=h, pair=2, half=h, last=h == 1) for h in range(2)]
    batches = nsa(0) + stick(0) + stick(1) + nsa(1) + dil + stick(2)
    groups = []
    turn = 0
    for b, batch in enumerate(batches):
        batch["turn"] = turn
        turn += batch["last"]
        for n in range(TB):
            full = (n + 1) * P
            w = {"cmp": [32], "dil": [min(full, 256), full, full]}.get(batch["kind"], [full])
            groups.append(dict(b=b, n=n, w=w))
    return batches, groups


def with_chunks(groups, batches, per_chunk):
    strip = chunk = 0
    for g in groups:
        g["strip0"] = strip
        strip += len(g["w"])
        kind = batches[g["b"]]["kind"]
        blocks, col = [], 0
        for s, w in enumerate(g["w"]):
            for c in range(0, w, P):
                blocks.append((s, col + c, c // P, 31 if kind == "cmp" else P))
            col += w
        g["chunks"] = [(chunk + i, blocks[c:c + per_chunk]) for i, c in enumerate(range(0, len(blocks), per_chunk))]
        chunk += len(g["chunks"])
    return groups


def two_block_kernel(nc, x_d, weights_d, params_d, tables_d, swa_d, ident_d, out_d):
    BANK, FREE, BEFORE = plan()
    ctx = ExitStack()
    with ctx:
        def sb(name, shape, dt=F32):
            return ctx.enter_context(nc.sbuf_tensor(name, shape, dt))

        def sem(name):
            return ctx.enter_context(nc.semaphore(name))

        x = sb("x", [P, KD, S])
        raw = sb("raw", [P, RING, UNIT])
        wh = sb("wh", [P, RING, UNIT], F32R)
        wl = sb("wl", [P, RING, UNIT], F32R)
        yh = sb("yh", [P, RT, S], F32R)
        yl = sb("yl", [P, RT, S], F32R)
        xh = sb("xh", [P, KD, S], F32R)
        xl = sb("xl", [P, KD, S], F32R)
        arena = sb("arena", [P, A_END])
        par = sb("par", [P, NPAR])
        ident = sb("ident", [P, P])
        ones = sb("ones", [P, P])
        rstd = sb("rstd", [P, S])
        rx = sb("rx", [P, TB])
        v4 = sb("v4", [P, 3, 72])
        rx2 = sb("rx2", [P, TB])
        hold = sb("hold", [P, 2])
        hsc = sb("hsc", [P, 3])
        gates = sb("gates", [P, TB, 12])
        negm = sb("negm", [P, 4, TB])
        rsum = sb("rsum", [P, 4, TB, 3])
        esink = sb("esink", [P, 2, TB])
        mtmp = sb("mtmp", [P, 2])
        den = sb("den", [P, TB])
        kcT = sb("kcT", [P, 32])
        vc = sb("vc", [P, HD])
        skc = sb("skc", [P, 1])
        B = [ctx.enter_context(nc.psum_tensor(f"bank{i}", [P, 512], F32)) for i in range(8)]

        def ar(at, *shape):
            n = int(np.prod(shape))
            v = arena[:, at:at + n]
            if len(shape) == 2:
                v = v.rearrange("p (a b) -> p a b", a=shape[0])
            if len(shape) == 3:
                v = v.rearrange("p (a b c) -> p a b c", a=shape[0], b=shape[1])
            return v

        gp = ar(A_RG, 3, NRG)
        sp = ar(A_RG + 3 * NRG, 4, NG * 3)
        hid, kcr, kcd = ar(A_HID, 2, 32), ar(A_KCR, HD), ar(A_KCD, P)
        tmpo = ar(A_TMPO, TB, HD)
        hidt = ar(A_HIDT, 2, P)

        def head_view(i, n):
            return v4[:, i, 0:TB * n].rearrange("p (t h) -> p t h", t=TB)

        loaded = [sem(f"raw_loaded{i}") for i in range(RING)]
        held = sem("unit_held")
        high_done = sem("high_done")
        split_done = sem("split_done")
        units_done = sem("units_done")
        in_x = [sem(f"in_x{i}") for i in range(4)]
        in_par, in_ident, in_tab = sem("in_par"), sem("in_ident"), sem("in_tab")
        ones_set = sem("ones_set")
        sq_ready = sem("sq_ready")
        sq_added = sem("sq_added")
        ssq_read = sem("ssq_read")
        root_ask, root_done = sem("root_ask"), sem("root_done")
        rx_ready = sem("rx_ready")
        diag_ready = sem("diag_ready")
        rstd_ready = sem("rstd_ready")
        xh_ready = sem("xh_ready")
        xl_ready = sem("xl_ready")
        x_new = sem("x_new")
        dve_step = sem("dve_step")
        pair_high = sem("pair_high")
        rg_high = sem("rg_high")
        xb_evac, gate_evac, xc_ready = sem("xb_evac"), sem("gate_evac"), sem("xc_ready")
        sig_done, decay_done = sem("sig_done"), sem("decay_done")
        var_ready, var_root, y_ready = sem("var_ready"), sem("var_root"), sem("y_ready")
        pe_misc = sem("pe_misc")
        evac_a, evac_d = sem("evac_act"), sem("evac_dve")
        heads_raw = sem("heads_raw")
        heads_summed = sem("heads_summed")
        heads_normed = sem("heads_normed")
        tanh_done = sem("tanh_done")
        heads_split = sem("heads_split")
        lam_ask, lam_done = sem("lam_ask"), sem("lam_done")
        cmp_ready = sem("cmp_ready")
        up_read, up_sq, ff_ready = sem("up_read"), sem("up_squared"), sem("ff_ready")
        down_read = sem("down_read")
        stored = sem("stored")
        FREESEM = {"A": evac_a, "D": evac_d, "X": x_new, "N": ssq_read, "B": rstd_ready}

        att = {}
        for a in (1, 2):
            att[a] = {n: sem(f"{n}{a}") for n in (
                "scores", "read0_", "read1_", "read2_", "soft1", "probs", "pt_ready", "pt_even", "pt_odd",
                "o_done", "fin", "pairT", "pair_done", "esum")}

        block = ctx.enter_context(nc.Block())

        done = {}
        misc = [0]

        def by_misc(key):
            misc[0] += 1
            done[key] = (pe_misc, misc[0])

        by_misc(("ssq", 0))
        by_misc(("rstd", 0))
        for m in range(7):
            by_misc(("wout", m))
        done[("wout", 7)] = (units_done, U_KV)
        for t in range(4):
            done[("kv", t)] = (units_done, U_GA)
            done[("q0", t)] = (units_done, U_Q1)
            done[("q1", t)] = (units_done, U_GB)
            done[("G0", t)] = (units_done, U_G1)
            done[("G1", t)] = (units_done, U_F0)
            done[("G2", t)] = (units_done, U_W1)
        for j in range(8):
            u = U_GA + j if j < 2 else U_GB + j - 2
            done[("gate", j)] = (units_done, u + 1)
            done[("bout", j)] = (units_done, U_BOUT + j + 1)
            done[("out2", j)] = (units_done, U_OUT2 + j + 1)
        for j in range(7):
            done[("F", j)] = (units_done, F_UNIT[j] + 1)
        done[("hid", 0)] = done[("hid", 1)] = (units_done, U_FA)
        for key in ([("ssq", 1), ("rstd", 1), ("kT", 0), ("kT", 1)] + [("qT", j) for j in range(8)]
                    + [("ssq", 2), ("rstd", 2), ("hT", 0)] + [("nT", j) for j in range(4)] + [("kc", 0)]
                    + [key[:2] for key in ITEMS2.values() if key[0] != "F" and key[:2] not in (("G3", 3), ("G4", 3))]
                    + [("ssq", 3), ("rstd", 3)]):
            by_misc(key)
        done[("G3", 3)] = (units_done, U_G3 + 4)
        done[("G4", 3)] = (units_done, U_G4 + 4)

        def wait_done(eng, key):
            eng.wait_ge(*done[key])

        def up_bank(i, first):
            return B[(0, 1, 2, 3, 6, 7, 0, 1)[i] if first else i % 4][:]

        NORM_UNITS = {0: "g_a", 1: "g_b", 2: "g_mix", 3: "g_mlp"}

        @block.sync
        def _(sp_):
            def load(j, ahead, u):
                if ahead is not None:
                    sp_.wait_ge(split_done, ahead)
                sp_.dma_start(raw[:, j, :], weights_d[u].rearrange("a p n -> (a p) n")).then_inc(loaded[j], 16)

            sp_.dma_start(par[:], params_d).then_inc(in_par, 16)
            load(0, None, bass.ds(0, 1))
            for i in range(4):
                sp_.dma_start(x[:, 2 * i:2 * i + 2, :], x_d[:, 2 * i:2 * i + 2, :]).then_inc(in_x[i], 16)
                if i == 1:
                    load(1, None, bass.ds(1, 1))
            sp_.dma_start(ident[:], ident_d).then_inc(in_ident, 16)
            for j in range(2, RING):
                load(j, None, bass.ds(j, 1))
            sp_.dma_start(ar(A_TAB, NTAB), tables_d).then_inc(in_tab, 16)
            sp_.dma_start(ar(A_SWA, 256), swa_d).then_inc(in_tab, 16)
            with sp_.Fori(1, UNITS // RING) as lap:
                for j in range(RING):
                    load(j, RING * lap + j - RING + 1, bass.ds(RING * lap + j, 1))
            for u in range(UNITS // RING * RING, UNITS):
                load(u % RING, u - RING + 1, bass.ds(u, 1))
            for m in range(KD):
                sp_.wait_ge(down_read, KD * (MLP_CHUNKS - 1) + m + 1)
                sp_.dma_start(out_d[:, m, :], x[:, m, :]).then_inc(stored, 16)
            sp_.wait_ge(stored, 16 * KD)

        @block.gpsimd
        def _(pool):
            pool.memset(hold[:], 0.0).then_inc(held, 1)
            pool.wait_ge(held, 1)

            def split(u, j, lap, first):
                pool.wait_ge(loaded[j], 16 * lap + 16)
                if not first:
                    pool.wait_ge(units_done, u - RING + 1)
                pool.tensor_tensor(hold[:], hold[:], hold[:], ALU.add).then_inc(held, 1)
                pool.tensor_scalar(wh[:, j, :], raw[:, j, :], 1.0, 1.0, ALU.mult, ALU.mult).then_inc(high_done, 1)
                pool.wait_ge(high_done, u + 1)
                pool.tensor_tensor(wl[:, j, :], raw[:, j, :], wh[:, j, :], ALU.subtract).then_inc(split_done, 1)

            def split_units(first, end):
                u = first
                while u < end and (u % RING or u < RING):
                    split(u, u % RING, u // RING, u < RING)
                    u += 1
                if (end - u) // RING > 0:
                    with pool.Fori(u // RING, end // RING) as lap:
                        for j in range(RING):
                            split(RING * lap + j, j, lap, False)
                for u in range(max(u, end // RING * RING), end):
                    split(u, u % RING, u // RING, False)

            def split_pair(p):
                yt = ar(A_YT[p % 2], 512)
                pool.wait_ge(att[1]["pair_done"], p + 1)
                pool.tensor_scalar(yh[:, p, :], yt, 1.0, 1.0, ALU.mult, ALU.mult).then_inc(pair_high, 1)
                pool.wait_ge(pair_high, p + 1)
                pool.tensor_tensor(yl[:, p, :], yt, yh[:, p, :], ALU.subtract).then_inc(y_ready, 1)

            assert U_GB + 6 == U_BOUT and len(ITEMS1) == 4
            done_pairs = 0
            last = 0
            for n, step in enumerate(sorted(ITEMS1)):
                while 8 * done_pairs + 7 + TURN_LAG < step:
                    split_pair(done_pairs)
                    done_pairs += 1
                split_units(last, U_BOUT + n + 1)
                last = U_BOUT + n + 1
            for p in range(done_pairs, 8):
                split_pair(p)
            split_units(last, UNITS)

        def head_rows(h):
            return slice(HD * (h % 2), HD * (h % 2) + HD)

        qT = ar(A_QT, 8, S)
        kT2 = ar(A_KT, 2, S)
        vS = ar(A_VS, TB, P)
        sg = ar(A_SG, 8, S)
        vd, vst, vn = ar(A_VD, TB, 384), ar(A_VST, TB, 384), ar(A_VN, TB, P)
        qn, kn = ar(A_QN, 2, S), ar(A_KN, 2, S)
        dq, dk = ar(A_R1, TB, 384), ar(A_R2, TB, 384)
        otok = ar(A_OT, 2, TB, P)
        bias = ar(A_BIAS, 1280)
        tabs = ar(A_TAB, NTAB)
        LOOK = 3

        def make_attention(a):
            batches, groups = attention_one() if a == 1 else attention_two()
            items = ITEMS1 if a == 1 else ITEMS2
            width, slots = (256, 6) if a == 1 else (512, 4)
            with_chunks(groups, batches, 2 if a == 1 else 4)
            pt = ar(A_PT1, 6, 256) if a == 1 else ar(A_PT2, 4, 512)
            th = ar(A_TANH, 2, 512)
            V_LAG = 2 if a == 1 else 1
            FIN_LAG = V_LAG + 1

            def strip_read(st):
                return s[f"read{st % 3}_"], st // 3 + 1

            s = att[a]
            ng = len(groups)
            pairs = [i for i, g in enumerate(groups) if g["n"] == TB - 1 and batches[g["b"]]["last"]]
            before7, last7 = {}, None
            for i in range(-LOOK - 1, ng + OUT_LAG):
                if i - TURN_LAG in pairs:
                    p = pairs.index(i - TURN_LAG)
                    before7[("pair", p)], last7 = last7, (s["pair_done"], p + 1)
                if i in items:
                    name, j, parts = items[i]
                    before7[name, j], last7 = last7, (FREESEM[EVAC[name]], FREE[name, j][1])
            part_at = {i + q: ((name, j), q, parts) for i, (name, j, parts) in items.items() for q in range(parts)}
            evac_at = {i + parts: (name, j) for i, (name, j, parts) in items.items()}

            after_dil = [i for i, g in enumerate(groups) if g["b"] > 0 and batches[g["b"] - 1]["kind"] == "dil"
                         and batches[g["b"]]["kind"] != "dil"]
            moved = after_dil[0] if after_dil else ng

            def probs_of(i):
                g = groups[i]
                if batches[g["b"]]["kind"] == "dil":
                    return ar((A_CT1, A_P, A_LT, A_P + 768)[g["n"]], sum(g["w"]))
                return ar(A_P + (A_R1 if i >= moved else 0) + width * (i % 4), width)

            def sums_of(i, w):
                return ar((A_R1 + 2048 if i >= moved else A_LT) + 512 * (i % 2), w)

            def scores_ap(g, k):
                b, n = batches[g["b"]], g["n"]
                h, w, kind = b["head"], g["w"][k], b["kind"]
                rows, qs = head_rows(h), slice(n * P, (n + 1) * P)
                if kind == "swa":
                    return [(qT[rows, h // 2, qs], kT2[rows, h // 8, (n + 1) * P - w:(n + 1) * P])]
                if kind == "cmp":
                    return [(qn[rows, h // 2, qs], kcT[rows, 0:32])]
                if kind in ("sel", "win"):
                    return [(qn[rows, h // 2, qs], kn[rows, kind == "win", 0:w])]
                if kind == "dil":
                    return [(dq[rows, n, k * P:(k + 1) * P], dk[rows, n + 1 - w // P:n + 1, k * P:(k + 1) * P])]
                t = 6 + h // 2
                q, kk = (yh[rows, t, qs], yl[rows, t, qs]), (yh[rows, t + 3, 0:w], yl[rows, t + 3, 0:w])
                return [(q[0], kk[0]), (q[0], kk[1]), (q[1], kk[0])]

            def value_ap(g, s_, kb, K):
                b, n = batches[g["b"]], g["n"]
                h, kind = b["head"], b["kind"]
                if kind == "swa":
                    return vS[:, n + 1 - g["w"][0] // P + kb, HD * (h // 8):HD * (h // 8) + HD]
                if kind == "cmp":
                    return vc[0:K, :]
                if kind in ("sel", "win"):
                    c = HD * (kind == "win")
                    return vn[:, kb, c:c + HD]
                if kind == "dil":
                    c = HD * (2 * s_ + h)
                    return vd[:, n + 1 - g["w"][s_] // P + kb, c:c + HD]
                return vst[:, kb, HD * h:HD * h + HD]

            last_chunk = groups[-1]["chunks"][-1][0]
            last_strip = groups[-1]["strip0"] + len(groups[-1]["w"]) - 1

            def pe_part(pe, item, tail):
                def scores(i):
                    g = groups[i]
                    kind, h = batches[g["b"]]["kind"], batches[g["b"]]["head"]
                    if g["n"] == 0 and kind == "stick":
                        pe.wait_ge(heads_split, 2 * (h // 2) + 2)
                    if g["n"] == 0 and kind == "cmp":
                        pe.wait_ge(evac_a, FREE[("kcT", 0)][1])
                    if g["n"] == 0 and kind == "dil":
                        pe.wait_ge(evac_a, FREE[("dT", 5)][1])
                    for k, w in enumerate(g["w"]):
                        st = g["strip0"] + k
                        if st >= 3:
                            pe.wait_ge(*strip_read(st - 3))
                        terms = scores_ap(g, k)
                        for t, (q, kk) in enumerate(terms):
                            out = B[st % 3][:, 0:w]
                            if kind == "dil":
                                out = out.rearrange("p (a b) -> p a b", b=P)
                            mm = pe.matmul(out, q, kk, start=t == 0, stop=t == len(terms) - 1)
                            if kind == "stick" and t == 0:
                                pe.matmul(B[st % 3][:, w - P:w], ident[:], ar(A_TAB + T_STK, P), start=False, stop=False)
                        mm.then_inc(s["scores"], 1)

                def turn(i):
                    g = groups[i]
                    if i == 0 and a == 2:
                        pe.wait_ge(evac_d, FREE[("F", 4)][1])
                    pe.wait_ge(s["probs"], i + 1)
                    col0 = probs_of(i)
                    for c, blocks in g["chunks"]:
                        if c >= 2:
                            pe.wait_ge(s[("pt_even", "pt_odd")[c % 2]], c // 2)
                        for j, (_, col, _, K) in enumerate(blocks):
                            mm = pe.transpose(B[3 + c % 2][0:K, j * P:(j + 1) * P], col0[:, col:col + K], ident[:])
                        mm.then_inc(s["pt_ready"], 1)

                def values(i):
                    g = groups[i]
                    b = g["b"]
                    if g["n"] == 0 and b >= 2:
                        pe.wait_ge(s["fin"], b - 1)
                    if g["n"] == 0 and batches[b]["kind"] in ("stick", "dil"):
                        pe.wait_ge(evac_a, FREE[("G4" if batches[b]["kind"] == "stick" else "G3", 3)][1])
                    first, total = True, sum(len(bl) for _, bl in g["chunks"])
                    for c, blocks in g["chunks"]:
                        pe.wait_ge(s[("pt_even", "pt_odd")[c % 2]], c // 2 + 1)
                        for j, (s_, _, kb, K) in enumerate(blocks):
                            total -= 1
                            mm = pe.matmul(B[5 + b % 2][:, g["n"] * HD:(g["n"] + 1) * HD],
                                           pt[0:K, c % slots, j * P:(j + 1) * P], value_ap(g, s_, kb, K),
                                           start=first, stop=total == 0)
                            first = False
                    mm.then_inc(s["o_done"], 1)

                def pair_turn(p):
                    pe.wait_ge(s["fin"], groups[pairs[p]]["b"] + 1)
                    if before7[("pair", p)]:
                        pe.wait_ge(*before7[("pair", p)])
                    for t in range(TB):
                        mm = pe.transpose(B[7][:, t * P:(t + 1) * P], otok[:, p % 2, t, :], ident[:])
                    mm.then_inc(s["pairT"], 1)

                for i in range(-LOOK - 1, ng + OUT_LAG):
                    if 0 <= i + LOOK + 1 < ng:
                        scores(i + LOOK + 1)
                    if 0 <= i < ng:
                        turn(i)
                    if 0 <= i - V_LAG < ng:
                        values(i - V_LAG)
                    if i - TURN_LAG in pairs:
                        pair_turn(pairs.index(i - TURN_LAG))
                    if i in part_at:
                        key, q, parts = part_at[i]
                        if q == 0 and before7[key]:
                            pe.wait_ge(*before7[key])
                        item(key, range(KD * q // parts, KD * (q + 1) // parts))
                    for m in TAIL.get(i - ng, ()):
                        if m < 3:
                            for st in range(last_strip - 2, last_strip + 1):
                                if st % 3 == m:
                                    pe.wait_ge(*strip_read(st))
                        else:
                            pe.wait_ge(s["pt_even"], last_chunk // 2 + 1)
                        tail(m)

            def act_part(act, item):
                def soft1(i):
                    g = groups[i]
                    b, n = batches[g["b"]], g["n"]
                    pr = probs_of(i)
                    if b["kind"] == "stick":
                        st, w = g["strip0"], g["w"][0]
                        lt, n3 = sums_of(i, w), 3 * stick_count(i)
                        act.wait_ge(s["scores"], st + 1)
                        if n3 >= 6:
                            act.wait_ge(*strip_read(st - 2))
                        act.activation(lt, B[st % 3][:, 0:w], ACT.Abs).then_inc(s["soft1"], 1)
                        act.wait_ge(s["soft1"], n3 + 1)
                        act.activation(lt, lt, ACT.Exp, scale=-1.0).then_inc(s["soft1"], 1)
                        act.wait_ge(s["soft1"], n3 + 2)
                        act.activation(lt, lt, ACT.Ln, bias=1.0).then_inc(s["soft1"], 1)
                        return
                    for st in range(g["strip0"], g["strip0"] + len(g["w"])):
                        act.wait_ge(*strip_read(st))
                    col = 0
                    for k, w in enumerate(g["w"]):
                        e = act.activation(pr[:, col:col + w], pr[:, col:col + w], ACT.Exp, scale=-1.0,
                                           bias=negm[:, g["b"] % 4, n:n + 1],
                                           accum_out=rsum[:, g["b"] % 4, n, k:k + 1])
                        col += w
                    e.then_inc(s["probs"], 1)
                    if b["kind"] == "swa" and n == TB - 1:
                        if g["b"] >= 2:
                            act.wait_ge(s["fin"], g["b"] - 1)
                        act.activation(esink[:, g["b"] % 2, :], negm[:, g["b"] % 4, :], ACT.Exp, scale=1.0,
                                       bias=par[:, PC["sinks"] + b["head"]:PC["sinks"] + b["head"] + 1])\
                           .then_inc(s["esum"], 1)

                def soft2(i):
                    g = groups[i]
                    if batches[g["b"]]["kind"] != "stick":
                        return
                    act.wait_ge(*strip_read(g["strip0"]))
                    pr = probs_of(i)[:, 0:g["w"][0]]
                    act.activation(pr, pr, ACT.Exp).then_inc(s["probs"], 1)

                def copy_out(i):
                    for c, blocks in groups[i]["chunks"]:
                        if c % 2 == 1 or a == 1:
                            pt_copy(act, c, blocks, lambda o, i_: act.activation(o, i_, ACT.Copy))

                for i in range(-LOOK, ng + OUT_LAG):
                    if 0 <= i + LOOK < ng:
                        soft1(i + LOOK)
                    if 0 <= i + LOOK - 1 < ng:
                        soft2(i + LOOK - 1)
                    if 0 <= i < ng:
                        copy_out(i)
                    if i in evac_at:
                        item(evac_at[i])
                    if a == 1 and i in pairs:
                        p = pairs.index(i)
                        act.wait_ge(evac_d, FREE[("gate", p)][1])
                        if p >= 2:
                            act.wait_ge(s["pair_done"], p - 1)
                        act.activation(th[:, p % 2, :], sg[:, p, :], ACT.Tanh).then_inc(tanh_done, 1)

            last_of_chunk = {c: i for i, g in enumerate(groups) for c, _ in g["chunks"]}

            def pt_copy(eng, c, blocks, copy):
                eng.wait_ge(s["pt_ready"], c + 1)
                if c >= slots:
                    eng.wait_ge(s["o_done"], last_of_chunk[c - slots] + 1)
                n, K = len(blocks) * P, blocks[0][3]
                copy(pt[0:K, c % slots, 0:n], B[3 + c % 2][0:K, 0:n]).then_inc(s[("pt_even", "pt_odd")[c % 2]], 1)

            def stick_count(i):
                return sum(1 for g in groups[:i] if batches[g["b"]]["kind"] == "stick")

            def dve_part(dve, link, item):
                def bias_part(at, w):
                    return ar(A_QN + at - 256, w) if at >= 256 else bias[:, at:at + w]

                def make_bias(b):
                    kind, h = b["kind"], b["head"]
                    if kind == "swa":
                        parts = [(A_SWA - A_TAB, 256, float(np.exp2(np.float32(-8.0 * (h + 1) / 16))))]
                    elif kind == "cmp":
                        parts = [(T_CMP, 128, slope10(6 + h))]
                    elif kind in ("sel", "win"):
                        parts = [(T_DC, 512, slope10(6 + h))]
                    else:
                        parts = [(T_D0, 256, slope10(h)), (T_D1, 512, slope10(2 + h)), (T_D2, 512, slope10(4 + h))]
                    at = 0
                    for t, w, slope in parts:
                        last = dve.tensor_scalar(bias_part(at, w), ar(A_TAB + t, w), -slope, None, ALU.mult)
                        at += w
                    link(last)

                def mask1(i):
                    g = groups[i]
                    b, n = batches[g["b"]], g["n"]
                    kind = b["kind"]
                    if n == 0 and kind not in ("stick", "win"):
                        make_bias(b)
                    if kind == "stick":
                        return
                    if i >= 4:
                        dve.wait_ge(s["pt_ready"], groups[i - 4]["chunks"][-1][0] + 1)
                    pr = probs_of(i)
                    col = at = 0
                    for k, w in enumerate(g["w"]):
                        st = g["strip0"] + k
                        dve.wait_ge(s["scores"], st + 1)
                        z = B[st % 3][:, 0:w]
                        if kind == "cmp":
                            bb = bias_part(0, P)[:, 32 * n:32 * n + 32]
                        else:
                            tw = 256 if (kind == "swa" or (kind == "dil" and k == 0)) else 512
                            bb = bias_part(at, tw)[:, tw - w:]
                            at += tw
                        final = k == len(g["w"]) - 1
                        out_m = negm[:, g["b"] % 4, n:n + 1] if final else mtmp[:, k:k + 1]
                        if k > 0:
                            init = mtmp[:, k - 1:k]
                        elif kind == "swa":
                            init = nsink[:, b["head"]:b["head"] + 1]
                        else:
                            init = 1e29 if kind == "cmp" else BIG
                        dve.tensor_tensor_reduce(pr[:, col:col + w], z, bb, -1.0, init, ALU.add, ALU.min, out_m)\
                           .then_inc(strip_read(st)[0], 1)
                        dve.wait_ge(*strip_read(st))
                        col += w

                def mask2(i):
                    g = groups[i]
                    if batches[g["b"]]["kind"] != "stick":
                        return
                    w = g["w"][0]
                    lt, pr = sums_of(i, w), probs_of(i)[:, 0:w]
                    z = B[g["strip0"] % 3][:, 0:w]
                    dve.wait_ge(s["soft1"], 3 * stick_count(i) + 3)
                    link(dve.scalar_tensor_tensor(out=lt, in0=z, scalar=0.0, in1=lt, op0=ALU.max, op1=ALU.add))
                    link(dve.tensor_tensor_scan(lt[:, ::-1], ones[:, 0:1].to_broadcast([P, w]), lt[:, ::-1],
                                                0.0, ALU.mult, ALU.add))
                    if i >= 4:
                        dve.wait_ge(s["pt_ready"], groups[i - 4]["chunks"][-1][0] + 1)
                    dve.tensor_tensor(pr, z, lt, ALU.subtract).then_inc(strip_read(g["strip0"])[0], 1)

                def copy_out(i):
                    for c, blocks in groups[i]["chunks"]:
                        if c % 2 == 0 and a == 2:
                            pt_copy(dve, c, blocks, dve.tensor_copy)

                def finish(bi):
                    b = batches[bi]
                    kind, p = b["kind"], b["turn"]
                    if p >= 2 and not b["half"]:
                        dve.wait_ge(s["pairT"], p - 1)
                    o = B[5 + bi % 2][:, 0:TB * HD].rearrange("p (n d) -> p n d", n=TB)
                    dst = otok[:, p % 2, :, HD * b["half"]:HD * b["half"] + HD]
                    rs = rsum[:, bi % 4, :, 0]
                    if kind == "swa":
                        dve.wait_ge(s["esum"], bi + 1)
                        link(dve.tensor_tensor(den[:], rs, esink[:, bi % 2, :], ALU.add))
                    elif kind == "dil":
                        link(dve.tensor_reduce(den[:], rsum[:, bi % 4, :, :], AX.X, ALU.add))
                    elif kind != "stick":
                        link(dve.tensor_scalar(den[:], rs, 1e-30, None, ALU.max))
                    if kind != "stick":
                        link(dve.reciprocal(den[:], den[:]))
                    if kind in ("cmp", "sel", "win"):
                        link(dve.tensor_tensor(den[:], den[:], gates[:, :, 3 * b["head"] + b["x"]], ALU.mult))
                    dve.wait_ge(s["o_done"], TB * (bi + 1))
                    if kind == "stick":
                        dve.tensor_copy(dst, o).then_inc(s["fin"], 1)
                        return
                    scale = den[:].unsqueeze(2).to_broadcast([P, TB, HD])
                    if kind in ("win", "cmp"):
                        link(dve.tensor_tensor(tmpo[:], o, scale, ALU.mult))
                        dve.tensor_tensor(dst, dst, tmpo[:], ALU.add).then_inc(s["fin"], 1)
                    else:
                        dve.tensor_tensor(dst, o, scale, ALU.mult).then_inc(s["fin"], 1)
                    dve.wait_ge(s["fin"], bi + 1)

                def pair_out(p):
                    dve.wait_ge(s["pairT"], p + 1)
                    to = batches[groups[pairs[p]]["b"]]["pair"]
                    if a == 1:
                        yt = ar(A_YT[p % 2], 512)
                        dve.wait_ge(tanh_done, p + 1)
                        if p >= 2:
                            dve.wait_ge(y_ready, NG + p - 1)
                        link(dve.scalar_tensor_tensor(out=yt, in0=th[:, p % 2, :], scalar=1.0, in1=sg[:, p, :],
                                                      op0=ALU.add, op1=ALU.mult))
                        dve.tensor_tensor(yt, B[7][:], yt, ALU.mult).then_inc(s["pair_done"], 1)
                    else:
                        link(dve.tensor_copy(yh[:, to, :], B[7][:]))
                        dve.tensor_tensor(yl[:, to, :], B[7][:], yh[:, to, :], ALU.subtract).then_inc(s["pair_done"], 1)

                for i in range(-LOOK, ng + OUT_LAG):
                    if 0 <= i + LOOK < ng:
                        mask1(i + LOOK)
                    if 0 <= i + LOOK - 1 < ng:
                        mask2(i + LOOK - 1)
                    if 0 <= i < ng:
                        copy_out(i)
                    if 0 <= i - FIN_LAG < ng and groups[i - FIN_LAG]["n"] == TB - 1:
                        finish(groups[i - FIN_LAG]["b"])
                    if i in evac_at:
                        item(evac_at[i])
                    if i - OUT_LAG in pairs:
                        pair_out(pairs.index(i - OUT_LAG))

            return pe_part, act_part, dve_part, len(pairs)

        def slope10(i):
            return float(np.exp2(np.float32(-8.0) * np.float32(i + 1) / np.float32(10)))

        nsink = sb("nsink", [P, 16])
        ATT1, ATT2 = make_attention(1), make_attention(2)

        @block.tensor
        def _(pe):
            def three(out, lh, ll, rh, rl, start, stop):
                pe.matmul(out, lh, rh, start=start, stop=False)
                pe.matmul(out, lh, rl, start=False, stop=False)
                return pe.matmul(out, ll, rh, start=False, stop=stop)

            def tile(w, j, k):
                return w[:, j, k * P:(k + 1) * P]

            def feature_major(u, j, out, ah, al, n=KD, ready=None, ks=None):
                pe.wait_ge(split_done, u + 1)
                for k in ks or range(n):
                    if ready:
                        pe.wait_ge(ready[0], ready[1] + ready[2] * k)
                    mm = three(out, tile(wh, j, k), tile(wl, j, k), ah[:, k, :], al[:, k, :], k == 0, k == n - 1)
                if k == n - 1:
                    mm.then_inc(units_done, 1)

            def free(key):
                if BEFORE[key]:
                    who, value = BEFORE[key]
                    pe.wait_ge(FREESEM[who], value)

            def token_major(u0, units, width, name, ah, al, ready=None):
                per = KD // units
                for u in range(u0, u0 + units):
                    pe.wait_ge(split_done, u + 1)
                    for kk in range(per):
                        k = (u - u0) * per + kk
                        if ready:
                            pe.wait_ge(ready[0], ready[1] + ready[2] * k)
                        cols = slice(kk * (UNIT // per), kk * (UNIT // per) + width)
                        for t in range(TB):
                            if k == 0:
                                free((name, t))
                            ts = slice(t * P, (t + 1) * P)
                            mm = three(B[BANK[(name, t)]][:, 0:width], ah[:, k, ts], al[:, k, ts],
                                       wh[:, u % RING, cols], wl[:, u % RING, cols], k == 0, k == KD - 1)
                    mm.then_inc(units_done, 1)

            def gate_tile(j, ks=None):
                u = done[("gate", j)][1] - 1
                if j < 4:
                    free(("gate", j))
                feature_major(u, u % RING, B[BANK[("gate", j)]][:], xh, xl,
                              ready=(xl_ready, 2 * KD + 1, 1) if j == 0 else None, ks=ks)

            def sum_squares(q, bank):
                pe.wait_ge(sq_added, (KD - 1) * (q + 1))
                for t in range(TB):
                    mm = pe.matmul(bank[:, t:t + 1], ar(A_P, S)[:, t * P:(t + 1) * P], ones[:, 0:1],
                                   start=t == 0, stop=t == TB - 1, skip_group_check=True)
                mm.then_inc(pe_misc, 1)

            def spread_rstd(q, bank):
                pe.wait_ge(diag_ready, q + 1)
                pe.matmul(bank[:], ones[:], ar(A_BIAS, 512), start=True, stop=True).then_inc(pe_misc, 1)

            pe.wait_ge(ones_set, 1)

            def rg_group(g, later):
                for i in range(3):
                    if later:
                        pe.wait_ge(sig_done, 6 * g - 3 + i)
                    feature_major(8 * g + i, i, B[i][:], xh, xl, ready=(xl_ready, 1, 1) if not later and i == 0 else None)
                    if not later and i == 1:
                        sum_squares(0, B[6])
                    if not later and i == 2:
                        spread_rstd(0, B[7])
                for i in range(3):
                    if later:
                        if i == 0:
                            pe.wait_ge(sig_done, 6 * g)
                        else:
                            pe.wait_ge(gate_evac, 3 * g - 2 + i)
                    feature_major(8 * g + 3 + i, (3 + i) % RING, B[3 + i][:], xh, xl)
                pe.wait_ge(xc_ready, 3 * g + 3)
                for r in range(2):
                    pe.wait_ge(split_done, 8 * g + 7 + r)
                    for n, (ki, o) in enumerate(GATE_TILES):
                        bank = (6 + 3 * r + o) % 8
                        first = n == 0 or GATE_TILES[n - 1][1] != o
                        if first:
                            if bank < 3:
                                pe.wait_ge(xb_evac, 3 * g + bank + 1)
                            elif bank == 3:
                                pe.wait_ge(gate_evac, 3 * g + 1)
                            elif later:
                                pe.wait_ge(sig_done, 6 * g - 11 + bank)
                            else:
                                pe.wait_ge((ssq_read, rstd_ready)[bank - 6], 1)
                        mm = three(B[bank][:], tile(wh, 2 + r, n), tile(wl, 2 + r, n), yh[:, 9 + ki, :], yl[:, 9 + ki, :],
                                   first, n == 6 or GATE_TILES[n + 1][1] != o)
                    mm.then_inc(units_done, 1)

            rg_group(0, False)
            with pe.Fori(1, NG) as g:
                rg_group(g, True)

            pe.wait_ge(gate_evac, 3 * NG)
            for k in range(9):
                u = U_WOUT + k
                pe.wait_ge(split_done, u + 1)
                pe.wait_ge(y_ready, k // 3 + 1)
                for m in (4, 5, 6, 7, 0, 1, 2, 3):
                    if k == 0 and m not in (4, 5):
                        pe.wait_ge(sig_done, 6 * NG - 5 + (m - 6) % 8)
                    mm = three(B[m][:], tile(wh, u % RING, m), tile(wl, u % RING, m), yh[:, k, :], yl[:, k, :], k == 0, False)
                mm.then_inc(units_done, 1)
            pe.wait_ge(split_done, U_WOUT + 12)
            pe.wait_ge(y_ready, NG)
            for m in range(KD):
                for k in range(9, 12):
                    u = U_WOUT + k
                    mm = three(B[m][:], tile(wh, u % RING, m), tile(wl, u % RING, m), yh[:, k, :], yl[:, k, :], False, k == 11)
                    if m == KD - 1:
                        mm.then_inc(units_done, 1)
                if m < KD - 1:
                    mm.then_inc(pe_misc, 1)

            token_major(U_KV, 2, 256, "kv", yh, yl, ready=(xl_ready, KD + 1, 1))
            free(("ssq", 1))
            sum_squares(1, B[BANK[("ssq", 1)]])
            gate_tile(0)
            gate_tile(1)
            free(("rstd", 1))
            spread_rstd(1, B[BANK[("rstd", 1)]])
            token_major(U_Q0, 4, 512, "q0", xh, xl)
            token_major(U_Q1, 4, 512, "q1", xh, xl)
            pe.wait_ge(heads_normed, 1)
            kd = ar(A_OT, TB, 2, P)
            for j in range(2):
                free(("kT", j))
                for t in range(TB):
                    mm = pe.transpose(B[BANK[("kT", j)]][:, t * P:(t + 1) * P], kd[:, t, j, :], ident[:])
                mm.then_inc(pe_misc, 1)
            def turn_queries(half):
                qr = ar((A_QRAW, A_QRAW1)[half], TB, 512)
                pe.wait_ge(heads_normed, 2 + half)
                for j in range(4):
                    key = ("qT", 4 * half + j)
                    free(key)
                    for t in range(TB):
                        mm = pe.transpose(B[BANK[key]][:, t * P:(t + 1) * P], qr[:, t, j * P:(j + 1) * P], ident[:])
                    mm.then_inc(pe_misc, 1)

            turn_queries(0)
            gate_tile(2)
            gate_tile(3)
            turn_queries(1)
            pe.wait_ge(evac_a, FREE[("qT", 7)][1])
            pe.wait_ge(evac_d, FREE[("gate", 3)][1])

            def output_tile(a, m, ks):
                u, n = ((U_BOUT, KD), (U_OUT2, 6))[a - 1]
                if ks[0] < n - 1:
                    pe.wait_ge(*((y_ready, NG + 7) if a == 1 else (att[2]["pair_done"], 5)))
                if ks[-1] == n - 1:
                    pe.wait_ge(*((y_ready, NG + 8) if a == 1 else (att[2]["pair_done"], 6)))
                feature_major(u + m, (u + m) % RING, B[m][:], yh, yl, n=n, ks=ks)

            ATT1[0](pe, lambda key, ks: gate_tile(key[1], ks), lambda m: output_tile(1, m, range(KD - 1)))

            for m in range(KD):
                if m == KD - 1:
                    pe.wait_ge(att[1]["pair_done"], ATT1[3])
                output_tile(1, m, range(KD - 1 if m < BEGUN else 0, KD))

            token_major(U_G0, 4, 512, "G0", xh, xl, ready=(xl_ready, 3 * KD + 1, 1))
            free(("ssq", 2))
            sum_squares(2, B[BANK[("ssq", 2)]])
            token_major(U_G1, 4, 396, "G1", xh, xl)
            free(("rstd", 2))
            spread_rstd(2, B[BANK[("rstd", 2)]])

            def f_tile(j, ks=None):
                u = done[("F", j)][1] - 1
                if j in (0, 1, 4):
                    free(("F", j))
                feature_major(u, u % RING, B[BANK[("F", j)]][:], xh, xl, ks=ks)

            f_tile(0)
            token_major(U_G2, 4, 384, "G2", xh, xl)
            pe.wait_ge(cmp_ready, 1)
            ch, cl = (w[:, 0:2, :].rearrange("p a (l n) -> p (a l) n", n=32) for w in (yh, yl))
            for c in range(2):
                free(("hid", c))
            for u in range(U_W1, U_W1 + 4):
                pe.wait_ge(split_done, u + 1)
                for l8 in range(8):
                    l = (u - U_W1) * 8 + l8
                    for c in range(2):
                        rows = slice(HD * c, HD * c + HD)
                        cols = slice(l8 * P, (l8 + 1) * P)
                        mm = three(B[BANK[("hid", c)]][0:32, 0:P], ch[rows, l, :], cl[rows, l, :],
                                   wh[rows, u % RING, cols], wl[rows, u % RING, cols], l == 0, l == 31)
                mm.then_inc(units_done, 1)
            f_tile(1)
            pe.wait_ge(evac_a, FREE[("hid", 1)][1])
            free(("hT", 0))
            for c in range(2):
                mm = pe.transpose(B[BANK[("hT", 0)]][:, 32 * c:32 * c + 31], hidt[0:31, c, :], ident[0:31, 0:31])
            mm.then_inc(pe_misc, 1)
            pe.wait_ge(heads_normed, 4)
            r0, r1, r2 = ar(A_R0, TB, 384), ar(A_R1, TB, 384), ar(A_R2, TB, 384)
            kdn = ar(A_OT, TB, 2, P)
            for j in range(4):
                key = ("nT", j)
                free(key)
                for t in range(TB):
                    src = r0[:, t, j * P:(j + 1) * P] if j < 2 else kdn[:, t, j - 2, :]
                    mm = pe.transpose(B[BANK[key]][:, t * P:(t + 1) * P], src, ident[:])
                mm.then_inc(pe_misc, 1)
            pe.wait_ge(evac_a, FREE[("hT", 0)][1])
            free(("kc", 0))
            w2 = par[:, PC["w2"]:PC["w2"] + 2 * HD]
            bk = B[BANK[("kc", 0)]]
            pe.matmul(bk[0:31, 0:HD], hid[:, 0, 0:31], w2[:, 0:HD], start=True, stop=True)
            pe.matmul(bk[0:31, HD:2 * HD], hid[:, 1, 0:31], w2[:, HD:2 * HD], start=True, stop=True).then_inc(pe_misc, 1)
            f_tile(4)

            def value_piece(name, t, ks):
                u0 = U_G3 if name == "G3" else U_G4
                ts = slice(t * P, (t + 1) * P)
                for k in ks:
                    u, cols = u0 + k // 2, slice(k % 2 * 512, k % 2 * 512 + 384)
                    if k % 2 == 0:
                        pe.wait_ge(split_done, u + 1)
                    mm = three(B[7][:, 0:384], xh[:, k, ts], xl[:, k, ts], wh[:, u % RING, cols], wl[:, u % RING, cols],
                               k == 0, k == KD - 1)
                    if t == TB - 1 and k % 2 == 1:
                        mm.then_inc(units_done, 1)
                if t < TB - 1 and k == KD - 1:
                    mm.then_inc(pe_misc, 1)

            def item(key, ks):
                name, j = key
                if name == "F":
                    f_tile(j, ks)
                elif name in ("G3", "G4"):
                    value_piece(name, j, ks)
                elif name == "kcT":
                    pe.wait_ge(heads_normed, 5)
                    pe.transpose(B[7][:, 0:31], kcd[0:31, :], ident[0:31, 0:31]).then_inc(pe_misc, 1)
                else:
                    for t in range(TB):
                        src = (r1 if j < 3 else r2)[:, t, (j % 3) * P:(j % 3 + 1) * P]
                        mm = pe.transpose(B[7][:, t * P:(t + 1) * P], src, ident[:])
                    mm.then_inc(pe_misc, 1)

            pe.wait_ge(evac_a, FREE[("kc", 0)][1])
            pe.wait_ge(evac_d, FREE[("F", 1)][1])
            pe.wait_ge(in_tab, 32)
            ATT2[0](pe, item, lambda m: output_tile(2, m, range(5)))

            pe.wait_ge(att[2]["pair_done"], ATT2[3])
            for m in range(KD):
                output_tile(2, m, range(5 if m < BEGUN else 0, 6))

            def mlp_chunk(c, first, later):
                for i in range(KD):
                    if later:
                        pe.wait_ge(up_read, KD * c + i - 3)
                    elif i >= 6:
                        pe.wait_ge(up_read, i - 5)
                    elif i < 4:
                        pe.wait_ge(x_new, 2 * KD + i + 1)
                    feature_major(U_MLP + 16 * c + i, (U_MLP + i) % RING, up_bank(i, first), xh, xl,
                                  ready=(xl_ready, 4 * KD + 1, 1) if first and i == 0 else None)
                    if first and i == 1:
                        pe.wait_ge(x_new, 3 * KD)
                        sum_squares(3, B[4])
                    if first and i == 3:
                        spread_rstd(3, B[5])
                for m in range(KD):
                    if later or m >= 4:
                        pe.wait_ge(down_read, KD * c + m - 3)
                    elif m < 2:
                        pe.wait_ge((ssq_read, rstd_ready)[m], 4)
                    else:
                        pe.wait_ge(up_read, m + 3)
                    feature_major(U_MLP + 16 * c + 8 + m, (U_MLP + m) % RING, B[4 + m % 4][:], yh, yl,
                                  ready=(ff_ready, KD * c + 1, 1) if m == 0 else None)

            mlp_chunk(0, True, False)
            with pe.Fori(1, MLP_CHUNKS) as c:
                mlp_chunk(c, False, True)

        @block.scalar
        def _(act):
            roots = [0]

            def gain(name, k):
                return par[:, PC[name] + k:PC[name] + k + 1]

            def root(rows=P, cols=TB):
                roots[0] += 1
                act.wait_ge(root_ask, roots[0])
                act.activation(v4[0:rows, 1, 0:cols], v4[0:rows, 1, 0:cols], ACT.Sqrt).then_inc(root_done, 1)

            def high_and_square(q, k, ready):
                act.wait_ge(*ready)
                act.activation(xh[:, k, :], x[:, k, :], ACT.Copy, scale=gain(NORM_UNITS[q], k)).then_inc(xh_ready, 1)
                act.activation(ar(A_P, KD, S)[:, k, :], x[:, k, :], ACT.Square).then_inc(sq_ready, 1)

            def take_rstd(q, bank):
                wait_done(act, ("rstd", q))
                act.activation(rstd[:], bank[:], ACT.Copy).then_inc(rstd_ready, 1)

            act.preload_act_table_set("exp_and_others")
            act.wait_ge(in_par, 16)
            for k in range(KD):
                high_and_square(0, k, (in_x[k // 2], 16))
            act.wait_ge(lam_ask, 1)
            act.activation(sp[:, 1, :], sp[:, 1, :], ACT.Exp).then_inc(lam_done, 1)
            root()
            take_rstd(0, B[7])

            rg = [ar(1545 + 1536 * i, 3, 512) for i in range(6)]
            xc, gt, rr, ii, aa, th = rg

            def rg_group(g, later):
                if later:
                    act.wait_ge(y_ready, g)
                for r, dst in ((0, rr), (1, ii)):
                    act.wait_ge(units_done, 8 * g + 7 + r)
                    for o in range(3):
                        act.activation(dst[:, o, :], B[(6 + 3 * r + o) % 8][:], ACT.Sigmoid,
                                       bias=gp[:, o, 5 + r:6 + r]).then_inc(sig_done, 1)
                act.wait_ge(gate_evac, 3 * g + 3)
                act.activation(gt[:], gt[:], ACT.Silu)
                act.wait_ge(sig_done, 6 * g + 3)
                for o in range(3):
                    act.activation(aa[:, o, :], rr[:, o, :], ACT.Exp, scale=gp[:, o, 7:8])
                    e = act.activation(th[:, o, :], rr[:, o, :], ACT.Tanh, scale=gp[:, o, 8:9])
                e.then_inc(decay_done, 1)
                act.wait_ge(var_ready, g + 1)
                act.activation(th[:], th[:], ACT.Sqrt).then_inc(var_root, 1)

            rg_group(0, False)
            with act.Fori(1, NG) as g:
                rg_group(g, True)

            for m in range(KD):
                act.wait_ge(x_new, m + 1)
                act.activation(yh[:, m, :], x[:, m, :], ACT.Copy, scale=gain("g_kv", m)).then_inc(xh_ready, 1)
                act.activation(ar(A_P, KD, S)[:, m, :], x[:, m, :], ACT.Square).then_inc(sq_ready, 1)
            for m in range(KD):
                act.activation(xh[:, m, :], x[:, m, :], ACT.Copy, scale=gain("g_b", m)).then_inc(xh_ready, 1)
            root()
            kraw = ar(A_KT, TB, P)
            sqk = ar(A_KT + 512, TB, P)
            act.wait_ge(rx_ready, 2)
            for t in range(TB):
                wait_done(act, ("kv", t))
                bk = B[BANK[("kv", t)]]
                act.activation(kraw[:, t, :], bk[:, 0:P], ACT.Copy)
                e = act.activation(sqk[:, t, :], bk[:, 0:P], ACT.Square)
                if t == TB - 1:
                    e.then_inc(heads_raw, 1)
                act.activation(vS[:, t, :], bk[:, P:2 * P], ACT.Copy, scale=rx[:, t:t + 1]).then_inc(evac_a, 1)
            root(P, TB * 2)
            take_rstd(1, B[BANK[("rstd", 1)]])

            qr, sqh = ar(A_QRAW, TB, 512), ar(A_SQH, TB, 512)

            def raw_heads(name, cols, dst, sq, summed=None, extra=None):
                if summed:
                    act.wait_ge(heads_summed, summed)
                for t in range(TB):
                    wait_done(act, (name, t))
                    bk = B[BANK[(name, t)]]
                    act.activation(dst[:, t, :], bk[:, 0:cols], ACT.Copy)
                    if extra:
                        extra(t, bk)
                    e = act.activation(sq[:, t, :], bk[:, 0:cols], ACT.Square)
                    e.then_inc(evac_a, 1)

            def turned(key, dst, scale):
                wait_done(act, key)
                act.activation(dst, B[BANK[key]][:], ACT.Copy, scale=scale).then_inc(evac_a, 1)

            raw_heads("q0", 512, qr, sqh)
            root(P, TB * 8)
            raw_heads("q1", 512, ar(A_QRAW1, TB, 512), sqh, summed=1)
            for j in range(2):
                turned(("kT", j), kT2[:, j, :], gain("k", 0))
            for j in range(4):
                turned(("qT", j), qT[:, j, :], hsc[:, 0:1])
            root(P, TB * 8)
            for j in range(4, 8):
                turned(("qT", j), qT[:, j, :], hsc[:, 0:1])
            ATT1[1](act, lambda key: None)

            for m in range(KD):
                high_and_square(2, m, (x_new, KD + m + 1))
            root()
            r0, r1, r2 = ar(A_R0, TB, 384), ar(A_R1, TB, 384), ar(A_R2, TB, 384)
            sqg = ar(A_SQG, TB, 384)
            act.wait_ge(rx_ready, 3)
            raw_heads("G0", 384, r0, sqg, extra=lambda t, bk: act.activation(
                vn[:, t, :], bk[:, 384:512], ACT.Copy, scale=rx[:, t:t + 1]))
            raw_heads("G1", 384, r1, sqg, summed=3, extra=lambda t, bk: act.activation(
                gates[:, t, :], bk[:, 384:396], ACT.Sigmoid, scale=rx[:, t:t + 1]))
            take_rstd(2, B[BANK[("rstd", 2)]])
            raw_heads("G2", 384, r2, sqg, summed=4)
            root(P, TB * 18)
            for c in range(2):
                wait_done(act, ("hid", c))
                act.activation(hidt[0:31, c, :], B[BANK[("hid", c)]][0:31, 0:P], ACT.Gelu_apprx_tanh).then_inc(evac_a, 1)
            wait_done(act, ("hT", 0))
            act.activation(hid[:, :, 0:31], B[BANK[("hT", 0)]][:, 0:64].rearrange("p (c n) -> p c n", c=2)[:, :, 0:31],
                           ACT.Copy).then_inc(evac_a, 1)
            for j in range(4):
                turned(("nT", j), (qn[:, j, :] if j < 2 else kn[:, j - 2, :]),
                       hsc[:, 1:2] if j < 2 else gain("nsa", j))
            wait_done(act, ("kc", 0))
            bk = B[BANK[("kc", 0)]]
            act.activation(vc[0:31, :], bk[0:31, HD:2 * HD], ACT.Copy)
            act.activation(kcr[0:31, :], bk[0:31, 0:HD], ACT.Copy)
            act.activation(ar(A_SQG, HD)[0:31, :], bk[0:31, 0:HD], ACT.Square, accum_out=skc[0:31, :]).then_inc(evac_a, 1)
            root(31, 1)

            def item(key):
                name, j = key
                if name in ("G3", "G4"):
                    wait_done(act, key)
                    act.activation((vd if name == "G3" else vst)[:, j, :], B[7][:, 0:384], ACT.Copy,
                                   scale=rx[:, j:j + 1]).then_inc(evac_a, 1)
                elif name == "kcT":
                    wait_done(act, key)
                    act.activation(kcT[:, 0:31], B[7][:, 0:31], ACT.Copy, scale=gain("nsa", 1)).then_inc(evac_a, 1)
                elif name == "dT":
                    wait_done(act, key)
                    to = (dq if j < 3 else dk)[:, :, (j % 3) * P:(j % 3 + 1) * P]
                    act.activation(to, B[7][:].rearrange("p (t q) -> p t q", t=TB), ACT.Copy,
                                   scale=hsc[:, 2:3] if j < 3 else gain("dil", 1)).then_inc(evac_a, 1)

            act.preload_act_table_set("natural_log_exp_and_others")
            ATT2[1](act, item)

            for m in range(KD):
                high_and_square(3, m, (x_new, 2 * KD + m + 1))
            root()

            up = ar(A_P + 4096, 2, 512)
            sq2 = ar(A_P + 5120, 2, 512)

            def mlp_chunk(c, first):
                for i in range(KD):
                    if first and i == 0:
                        take_rstd(3, B[5])
                    act.wait_ge(up_read, KD * c + i + 1)
                    if not first or i >= 2:
                        act.wait_ge(ff_ready, KD * c + i - 1)
                    act.activation(sq2[:, i % 2, :], up[:, i % 2, :], ACT.Square)
                    act.activation(yh[:, i, :], up[:, i % 2, :], ACT.Square).then_inc(up_sq, 1)

            mlp_chunk(0, True)
            with act.Fori(1, MLP_CHUNKS) as c:
                mlp_chunk(c, False)

        @block.vector
        def _(dve):
            steps = [0]
            base = [0]
            asks = [0]

            def link(ins):
                steps[0] += 1
                ins.then_inc(dve_step, 1)
                dve.wait_ge(dve_step, base[0] + steps[0])

            def gain(name, k):
                return par[:, PC[name] + k:PC[name] + k + 1]

            def rsqrt(rows, cols, y):
                v, r, t = (v4[0:rows, i, 0:cols] for i in range(3))
                dve.reciprocal(r, v).then_inc(root_ask, 1)
                asks[0] += 1
                dve.wait_ge(root_done, asks[0])
                link(dve.tensor_tensor(t, v, r, ALU.mult))
                link(dve.tensor_tensor(t, t, r, ALU.mult))
                link(dve.tensor_scalar(t, t, -0.5, 1.5, ALU.mult, ALU.add))
                return dve.tensor_tensor(y, r, t, ALU.mult)

            def low_part(k, dh, dl, name, high_count):
                dve.wait_ge(xh_ready, high_count)
                dve.scalar_tensor_tensor(out=dl[:, k, :], in0=x[:, k, :], scalar=gain(name, k), in1=dh[:, k, :],
                                         op0=ALU.mult, op1=ALU.subtract).then_inc(xl_ready, 1)

            def add_square(q, k):
                if k > 0:
                    sq = ar(A_P, KD, S)
                    dve.wait_ge(sq_ready, KD * q + k + 1)
                    dve.tensor_tensor(sq[:, 0, :], sq[:, 0, :], sq[:, k, :], ALU.add).then_inc(sq_added, 1)
                    dve.wait_ge(sq_added, (KD - 1) * q + k)

            def token_norm(q, bank):
                wait_done(dve, ("ssq", q))
                dve.tensor_scalar(v4[:, 0, 0:TB], bank[:, 0:TB], 1.0 / D, EPS, ALU.mult, ALU.add).then_inc(ssq_read, 1)
                dve.wait_ge(ssq_read, q + 1)
                rsqrt(P, TB, rx[:]).then_inc(rx_ready, 1)
                dve.wait_ge(rx_ready, q + 1)
                diag = ar(A_BIAS, TB, P)
                for t in range(TB):
                    d_ = dve.tensor_scalar(diag[:, t, :], ident[:], rx[:, t:t + 1], None, ALU.mult)
                d_.then_inc(diag_ready, 1)

            dve.memset(kcT[:], 0.0)
            dve.memset(ones[:], 1.0).then_inc(ones_set, 1)
            dve.wait_ge(ones_set, 1)
            dve.wait_ge(in_par, 16)
            ub = ar(0, 3, 515)
            xc, gt, rr, ii, aa, th = [ar(1545 + 1536 * i, 3, 512) for i in range(6)]
            for k in range(KD):
                dve.wait_ge(in_x[k // 2], 16)
                low_part(k, xh, xl, "g_a", k + 1)
                add_square(0, k)
            lam = par[:, 0:NG * 3 * NRG].rearrange("p (t c) -> p t c", c=NRG)[:, :, 7]
            nlam = par[:, 0:NG * 3 * NRG].rearrange("p (t c) -> p t c", c=NRG)[:, :, 8]
            s0, s1, s2, s3 = (sp[:, i, :] for i in range(4))
            dve.scalar_tensor_tensor(out=s1, in0=lam, scalar=-1.0, in1=lam, op0=ALU.mult, op1=ALU.min).then_inc(lam_ask, 1)
            dve.wait_ge(lam_done, 1)
            link(dve.tensor_scalar(s2, s1, 2.0, None, ALU.add))
            link(dve.reciprocal(s2, s2))
            link(dve.tensor_tensor(s1, s1, s2, ALU.mult))
            link(dve.tensor_tensor(s2, s1, s1, ALU.mult))
            link(dve.tensor_scalar(s3, s2, 1.0 / 17.0, None, ALU.mult))
            for c in (15, 13, 11, 9, 7, 5, 3):
                link(dve.scalar_tensor_tensor(out=s3, in0=s3, scalar=1.0 / c, in1=s2, op0=ALU.add, op1=ALU.mult))
            link(dve.scalar_tensor_tensor(out=s3, in0=s3, scalar=1.0, in1=s1, op0=ALU.add, op1=ALU.mult))
            link(dve.tensor_scalar(s0, lam, -1.0, 0.0, ALU.mult, ALU.max))
            link(dve.scalar_tensor_tensor(out=s0, in0=s3, scalar=2.0, in1=s0, op0=ALU.mult, op1=ALU.add))
            link(dve.tensor_scalar(lam, s0, -8.0, None, ALU.mult))
            link(dve.tensor_scalar(nlam, s0, 8.0, None, ALU.mult))
            dve.wait_ge(in_ident, 16)
            token_norm(0, B[6])
            dve.tensor_scalar(hsc[:, 0:1], gain("q", 0), HD ** -0.5, None, ALU.mult)
            dve.tensor_scalar(hsc[:, 1:2], gain("nsa", 0), HD ** -0.5, None, ALU.mult)
            dve.tensor_scalar(hsc[:, 2:3], gain("dil", 0), HD ** -0.5, None, ALU.mult)
            dve.tensor_scalar(nsink[:], par[:, PC["sinks"]:PC["sinks"] + 16], -1.0, None, ALU.mult)
            link(dve.memset(ub[:, :, 0:3], 0.0))

            def rg_conv(g):
                at = slice(3 * NRG * g, 3 * NRG * (g + 1)) if isinstance(g, int) else bass.ds(3 * NRG * g, 3 * NRG)
                link(dve.tensor_copy(gp[:].rearrange("p a b -> p (a b)"), par[:, at]))
                for i in range(3):
                    dve.wait_ge(units_done, 8 * g + i + 1)
                    dve.tensor_tensor(ub[:, i, 3:515], B[i][:], rstd[:], ALU.mult).then_inc(xb_evac, 1)
                    dve.wait_ge(xb_evac, 3 * g + i + 1)
                    link(dve.tensor_scalar(xc[:, i, :], ub[:, i, 0:512], gp[:, i, 0:1], gp[:, i, 4:5], ALU.mult, ALU.add))
                    for j in range(1, 4):
                        link(dve.scalar_tensor_tensor(out=xc[:, i, :], in0=ub[:, i, j:j + 512], scalar=gp[:, i, j:j + 1],
                                                      in1=xc[:, i, :], op0=ALU.mult, op1=ALU.add))
                    link(dve.tensor_copy(yh[:, 9 + i, :], xc[:, i, :]))
                    dve.tensor_tensor(yl[:, 9 + i, :], xc[:, i, :], yh[:, 9 + i, :], ALU.subtract).then_inc(xc_ready, 1)

            def rg_gate(g):
                for i in range(3):
                    dve.wait_ge(units_done, 8 * g + 4 + i)
                    dve.tensor_tensor(gt[:, i, :], B[3 + i][:], rstd[:], ALU.mult).then_inc(gate_evac, 1)

            def rg_variance(g):
                dve.wait_ge(sig_done, 6 * g + 6)
                link(dve.tensor_tensor(ii[:], ii[:], xc[:], ALU.mult))
                dve.wait_ge(decay_done, g + 1)
                link(dve.tensor_tensor(rr[:], aa[:], aa[:], ALU.mult))
                dve.scalar_tensor_tensor(out=th[:], in0=rr[:], scalar=1.0, in1=th[:], op0=ALU.add, op1=ALU.mult)\
                   .then_inc(var_ready, 1)

            def rg_recurrence(g):
                dve.wait_ge(var_root, g + 1)
                link(dve.tensor_tensor(ii[:], ii[:], th[:], ALU.mult))
                for i in range(3):
                    link(dve.tensor_tensor_scan(rr[:, i, :], aa[:, i, :], ii[:, i, :], 0.0, ALU.mult, ALU.add))
                link(dve.tensor_tensor(rr[:], rr[:], gt[:], ALU.mult))
                at = slice(3 * g, 3 * g + 3) if isinstance(g, int) else bass.ds(3 * g, 3)
                dve.tensor_scalar(yh[:, at, :], rr[:], 1.0, None, ALU.mult).then_inc(rg_high, 1)
                dve.wait_ge(rg_high, g + 1)
                dve.tensor_tensor(yl[:, at, :], rr[:], yh[:, at, :], ALU.subtract).then_inc(y_ready, 1)

            RG_LINKS = 1 + 3 * 5 + 7
            dve.wait_ge(rstd_ready, 1)
            rg_conv(0)
            rg_gate(0)
            before = steps[0]
            with dve.Fori(1, NG) as g:
                base[0], steps[0] = (g - 1) * RG_LINKS + before, 0
                rg_variance(g - 1)
                rg_conv(g)
                rg_recurrence(g - 1)
                rg_gate(g)
                assert steps[0] == RG_LINKS, steps
            base[0], steps[0] = before + (NG - 1) * RG_LINKS, 0
            rg_variance(NG - 1)
            rg_recurrence(NG - 1)

            dve.wait_ge(y_ready, NG)
            for m in range(KD):
                wait_done(dve, ("wout", m))
                dve.tensor_tensor(x[:, m, :], B[m][:], x[:, m, :], ALU.add).then_inc(x_new, 1)
                dve.wait_ge(x_new, m + 1)
                low_part(m, yh, yl, "g_kv", KD + m + 1)
                add_square(1, m)
            for m in range(KD):
                low_part(m, xh, xl, "g_b", 2 * KD + m + 1)

            token_norm(1, B[BANK[("ssq", 1)]])

            def head_scales(n):
                v = head_view(0, n)
                link(dve.tensor_tensor(rx2[:], rx[:], rx[:], ALU.mult))
                link(dve.tensor_tensor(v, v, rx2[:].unsqueeze(2).to_broadcast([P, TB, n]), ALU.mult))
                link(dve.tensor_scalar(v4[:, 0, 0:TB * n], v4[:, 0, 0:TB * n], 1.0 / HD, EPS, ALU.mult, ALU.add))
                link(rsqrt(P, TB * n, v4[:, 1, 0:TB * n]))
                link(dve.tensor_tensor(head_view(2, n), head_view(1, n), rx[:].unsqueeze(2).to_broadcast([P, TB, n]),
                                       ALU.mult))

            kraw, sqk = ar(A_KT, TB, P), ar(A_KT + 512, TB, P)
            kd = ar(A_OT, TB, 2, P)
            dve.wait_ge(heads_raw, 1)
            link(dve.tensor_reduce(head_view(0, 2), sqk[:].rearrange("p t (h d) -> p t h d", d=HD), AX.X, ALU.add))
            head_scales(2)
            rq = head_view(2, 2)
            for j in range(2):
                for t in range(TB):
                    e = dve.tensor_scalar(kd[:, t, j, :].rearrange("p (c d) -> p c d", c=2),
                                          kraw[:, t, HD * j:HD * j + HD].unsqueeze(1).to_broadcast([P, 2, HD]),
                                          rq[:, t, j:j + 1], None, ALU.mult)
            e.then_inc(heads_normed, 1)

            def gate_tile(j):
                wait_done(dve, ("gate", j))
                dve.scalar_tensor_tensor(out=sg[:, j, :], in0=B[BANK[("gate", j)]][:], scalar=0.5, in1=rstd[:],
                                         op0=ALU.mult, op1=ALU.mult).then_inc(evac_d, 1)

            dve.wait_ge(rstd_ready, 2)
            gate_tile(0)
            gate_tile(1)
            sqh = ar(A_SQH, TB, 512)

            def norm_queries(half):
                qr = ar((A_QRAW, A_QRAW1)[half], TB, 512)
                dve.wait_ge(evac_a, FREE[(f"q{half}", TB - 1)][1])
                dve.tensor_reduce(head_view(0, 8), sqh[:].rearrange("p t (h d) -> p t h d", d=HD), AX.X, ALU.add)\
                   .then_inc(heads_summed, 1)
                dve.wait_ge(heads_summed, half + 1)
                head_scales(8)
                rq = head_view(2, 8)
                for t in range(TB):
                    q4 = qr[:, t, :].rearrange("p (h d) -> p h d", d=HD)
                    e = dve.tensor_tensor(q4, q4, rq[:, t, 0:8].unsqueeze(2).to_broadcast([P, 8, HD]), ALU.mult)
                e.then_inc(heads_normed, 1)

            norm_queries(0)
            norm_queries(1)
            gate_tile(2)
            gate_tile(3)
            dve.wait_ge(in_tab, 32)
            dve.wait_ge(evac_a, FREE[("qT", 7)][1])
            ATT1[2](dve, link, lambda key: gate_tile(key[1]))

            for m in range(KD):
                wait_done(dve, ("bout", m))
                dve.tensor_tensor(x[:, m, :], B[m][:], x[:, m, :], ALU.add).then_inc(x_new, 1)
                dve.wait_ge(x_new, KD + m + 1)
                low_part(m, xh, xl, "g_mix", 3 * KD + m + 1)
                add_square(2, m)
            token_norm(2, B[BANK[("ssq", 2)]])

            r0, r1, r2 = ar(A_R0, TB, 384), ar(A_R1, TB, 384), ar(A_R2, TB, 384)
            sqg = ar(A_SQG, TB, 384)

            def sum_heads(name, at, count):
                dve.wait_ge(evac_a, FREE[(name, TB - 1)][1])
                dve.tensor_reduce(head_view(0, 18)[:, :, at:at + 6], sqg[:].rearrange("p t (h d) -> p t h d", d=HD), AX.X, ALU.add)\
                   .then_inc(heads_summed, 1)
                dve.wait_ge(heads_summed, count)

            sum_heads("G0", 0, 3)
            sum_heads("G1", 6, 4)
            dve.wait_ge(rstd_ready, 3)
            ct, rawc = ar(A_CT, 512), ar(A_RAW, 32, 32)
            wait_done(dve, ("F", 0))
            dve.tensor_tensor(ct, B[BANK[("F", 0)]][:], rstd[:], ALU.mult).then_inc(evac_d, 1)
            dve.wait_ge(evac_d, FREE[("F", 0)][1])
            link(dve.memset(rawc[:, :, 31:32], 0.0))
            cv = ct.rearrange("p (n s) -> p s n", s=16)
            pe_ = par[:, PC["pe"]:PC["pe"] + 32]
            for half in range(2):
                e = dve.tensor_tensor(rawc[:, 16 * half:16 * half + 16, 0:31], cv[:, :, half:half + 31],
                                      pe_[:, 16 * half:16 * half + 16].unsqueeze(2).to_broadcast([P, 16, 31]), ALU.add)
            link(e)
            rc = rawc[:].rearrange("p l n -> p (l n)").rearrange("p (a b) -> p a b", a=2)
            link(dve.tensor_copy(yh[:, 0:2, :], rc))
            dve.tensor_tensor(yl[:, 0:2, :], rc, yh[:, 0:2, :], ALU.subtract).then_inc(cmp_ready, 1)
            sum_heads("G2", 12, 5)
            head_scales(18)
            rq = head_view(2, 18)
            for t in range(TB):
                for rr_, at, n in ((r0, 0, 4), (r1, 6, 6), (r2, 12, 6)):
                    h4 = rr_[:, t, 0:HD * n].rearrange("p (h d) -> p h d", d=HD)
                    dve.tensor_tensor(h4, h4, rq[:, t, at:at + n].unsqueeze(2).to_broadcast([P, n, HD]), ALU.mult)
                for j in range(2):
                    e = dve.tensor_scalar(kd[:, t, j, :].rearrange("p (c d) -> p c d", c=2),
                                          r0[:, t, 256 + HD * j:256 + HD * j + HD].unsqueeze(1).to_broadcast([P, 2, HD]),
                                          rq[:, t, 4 + j:5 + j], None, ALU.mult)
            e.then_inc(heads_normed, 1)
            st = ar(A_ST, 512)

            def split_f(j):
                wait_done(dve, ("F", j))
                dve.scalar_tensor_tensor(out=st, in0=B[BANK[("F", j)]][:], scalar=HD ** -0.5 if j < 4 else 1.0,
                                         in1=rstd[:], op0=ALU.mult, op1=ALU.mult).then_inc(evac_d, 1)
                dve.wait_ge(evac_d, FREE[("F", j)][1])
                link(dve.tensor_copy(yh[:, 5 + j, :], st))
                dve.tensor_tensor(yl[:, 5 + j, :], st, yh[:, 5 + j, :], ALU.subtract).then_inc(heads_split, 1)
                dve.wait_ge(heads_split, {1: 1, 4: 2, 2: 3, 5: 4, 3: 5, 6: 6}[j])

            wait_done(dve, ("hT", 0))
            split_f(1)
            dve.wait_ge(evac_a, FREE[("kc", 0)][1])
            link(dve.tensor_scalar(v4[0:31, 0, 0:1], skc[0:31, :], 1.0 / HD, EPS, ALU.mult, ALU.add))
            link(rsqrt(31, 1, v4[0:31, 1, 0:1]))
            dve.tensor_scalar(kcd[0:31, :].rearrange("p (c d) -> p c d", c=2),
                              kcr[0:31, :].unsqueeze(1).to_broadcast([31, 2, HD]),
                              v4[0:31, 1, 0:1], None, ALU.mult).then_inc(heads_normed, 1)
            split_f(4)

            def item(key):
                name, j = key
                if name == "F":
                    split_f(j)

            ATT2[2](dve, link, item)

            for m in range(KD):
                wait_done(dve, ("out2", m))
                dve.tensor_tensor(x[:, m, :], B[m][:], x[:, m, :], ALU.add).then_inc(x_new, 1)
                dve.wait_ge(x_new, 2 * KD + m + 1)
                low_part(m, xh, xl, "g_mlp", 4 * KD + m + 1)
                add_square(3, m)
            token_norm(3, B[4])

            up, sq2 = ar(A_P + 4096, 2, 512), ar(A_P + 5120, 2, 512)
            dve.wait_ge(rstd_ready, 4)

            def mlp_chunk(c, first):
                def relu(i):
                    dve.wait_ge(units_done, U_MLP + 16 * c + i + 1)
                    if not first or i >= 2:
                        dve.wait_ge(up_sq, KD * c + i - 1)
                    dve.scalar_tensor_tensor(out=up[:, i % 2, :], in0=up_bank(i, first), scalar=0.0, in1=rstd[:],
                                             op0=ALU.max, op1=ALU.mult).then_inc(up_read, 1)

                def low(i):
                    dve.wait_ge(up_sq, KD * c + i + 1)
                    dve.tensor_tensor(yl[:, i, :], sq2[:, i % 2, :], yh[:, i, :], ALU.subtract).then_inc(ff_ready, 1)

                for i in range(KD):
                    relu(i)
                    low(i)
                for m in range(KD):
                    dve.wait_ge(units_done, U_MLP + 16 * c + 8 + m + 1)
                    dve.tensor_tensor(x[:, m, :], B[4 + m % 4][:], x[:, m, :], ALU.add).then_inc(down_read, 1)

            mlp_chunk(0, True)
            with dve.Fori(1, MLP_CHUNKS) as c:
                mlp_chunk(c, False)


def _tables():
    FAR = 1e33
    i = np.arange(P)[:, None]

    def dist(cols, first, ok):
        d = (first + i - np.arange(cols)[None, :]).astype(np.float64)
        return np.where(ok(d), d, FAR)

    t = np.zeros((P, NTAB), np.float32)
    t[:, T_D0:T_D0 + 256] = dist(256, 128, lambda d: (d >= 0) & (d <= 128))
    t[:, T_D1:T_D1 + 512] = dist(512, 384, lambda d: (d >= 0) & (d % 4 == 0))
    t[:, T_D2:T_D2 + 512] = dist(512, 384, lambda d: (d >= 0) & (d % 16 == 0))
    t[:, T_DC:T_DC + 512] = dist(512, 384, lambda d: d >= 0)
    t[:, T_STK:T_STK + P] = np.where(dist(P, 0, lambda d: d > 0) < FAR, 0.0, -BIG)
    for n in range(TB):
        for w in range(32):
            d = n * P + np.arange(P) - (16 * w + 31)
            t[:, T_CMP + 32 * n + w] = np.where((d >= 0) & (w < 31), d, FAR)
    return t, np.ascontiguousarray(dist(256, 128, lambda d: (d >= 0) & (d < 128)).astype(np.float32))


def _feature_units(w):
    k, m = w.shape[0] // P, w.shape[1] // P
    u = w.reshape(k, P, m, P).transpose(2, 1, 0, 3).reshape(m, P, k * P)
    return np.pad(u, ((0, 0), (0, 0), (0, UNIT - k * P)))


def _token_units(w, units):
    cols = UNIT * units // KD
    w = np.pad(w, ((0, 0), (0, cols - w.shape[1])))
    return w.reshape(units, KD // units, P, cols).transpose(0, 2, 1, 3).reshape(units, P, UNIT)


def _gate_unit(blocks):
    full = np.zeros((3 * P, 3 * P), np.float32)
    n = blocks.shape[1]
    for b in range(blocks.shape[0]):
        full[b * n:(b + 1) * n, b * n:(b + 1) * n] = blocks[b]
    unit = np.zeros((1, P, 8, P), np.float32)
    for t, (i, o) in enumerate(GATE_TILES):
        unit[0, :, t] = full[i * P:(i + 1) * P, o * P:(o + 1) * P]
    return unit.reshape(1, P, UNIT)


def kernel(**inputs):
    import concourse.bacc as _bacc
    from concourse.bass_utils import run_bass_kernel_spmd as _run

    a = {k: np.asarray(v) for k, v in inputs.items()}
    xb, gate = _feature_units(a["a_w_in"][0][:, :R]), _feature_units(a["a_w_in"][0][:, R:])
    parts = []
    for g in range(NG):
        parts += [xb[3 * g:3 * g + 3], gate[3 * g:3 * g + 3], _gate_unit(a["a_gate_r_w"][0][4 * g:4 * g + 4]),
                  _gate_unit(a["a_gate_i_w"][0][4 * g:4 * g + 4])]
    parts.append(a["a_w_out"][0].reshape(RT, P, D))
    parts.append(_token_units(a["w_kv"], 2))
    bq, bg = a["b_w_in"][0][:, :D], _feature_units(a["b_w_in"][0][:, D:])
    parts += [bg[0:2], _token_units(bq[:, 0:512], 4), _token_units(bq[:, 512:], 4), bg[2:8]]
    parts.append(_feature_units(a["b_w_out"][0]))
    w = a["w_in_2"][0]
    q_, kc, vc, ks, vs, kw, vw, gl = np.split(w[:, 0:652], [256, 320, 384, 448, 512, 576, 640], axis=1)
    dq, dk, dv = np.split(w[:, 652:652 + 1152], 3, axis=1)
    sq, sk, sv = np.split(w[:, 652 + 1152:], 3, axis=1)
    parts.append(_token_units(np.concatenate([q_, ks, kw, vs, vw], 1), 4))
    parts.append(_token_units(np.concatenate([dq, gl], 1), 4))
    parts.append(_feature_units(np.concatenate([kc, vc], 1)))
    parts.append(_token_units(dk, 4))
    parts.append(a["cmp_w1_2"][0].reshape(2, 4, 8, HD, P).transpose(1, 0, 3, 2, 4).reshape(4, P, UNIT))
    qk = _feature_units(np.concatenate([sq, sk], 1))
    parts += [qk[0:6:3], _token_units(sv, 4), qk[1:6:3], _token_units(dv, 4), qk[2:6:3], _feature_units(a["w_out_2"][0])]
    up = _feature_units(a["w_up_2"][0])
    for c in range(MLP_CHUNKS):
        parts += [up[8 * c:8 * c + 8], _feature_units(a["w_down_2"][0][c * D:(c + 1) * D])]
    weights = np.ascontiguousarray(np.concatenate(parts, 0))
    assert weights.shape == (UNITS, P, UNIT), weights.shape
    rg = np.stack([*a["a_conv_w"][0], a["a_conv_b"][0], a["a_gate_r_b"][0], a["a_gate_i_b"][0], a["a_lambda"][0],
                   a["a_lambda"][0]])
    twice = lambda g: np.concatenate([g, g], -1).T
    cols = [rg.reshape(NRG, RT, P).transpose(2, 1, 0).reshape(P, RT * NRG)]
    cols += [a[n].reshape(KD, P).T for n in ("a_norm_g", "kv_norm_g", "b_norm_g", "norm_mix_2", "norm_mlp_2")]
    cols += [twice(a["q_norm_g"]), twice(a["k_norm_g"][None]), twice(a["qk_gain_nsa_2"][0]), twice(a["qk_gain_dil_2"][0])]
    cols += [np.broadcast_to(a["sinks"], (P, 16)), a["cmp_pe_2"][0].transpose(0, 2, 1).reshape(P, 32)]
    cols += [a["cmp_w2_2"][0].transpose(1, 0, 2).reshape(P, 2 * HD)]
    params = np.ascontiguousarray(np.concatenate(cols, 1))
    assert params.shape == (P, NPAR), params.shape
    arrays = {
        "x_in": np.ascontiguousarray(a["x"][0].T.reshape(KD, P, S).transpose(1, 0, 2)),
        "weight_units": weights,
        "params": params,
        "tables": _tables()[0],
        "swa_table": _tables()[1],
        "identity": np.eye(P, dtype=np.float32),
    }
    nc = _bacc.Bacc("TRN2", target_bir_lowering=False, num_devices=1, dynamic_dma_scratch_size=1024)
    args = [nc.dram_tensor(n, v.shape, mybir.dt.from_np(v.dtype), kind="ExternalInput").ap() for n, v in arrays.items()]
    out = nc.dram_tensor("out_fm", (P, KD, S), F32, kind="ExternalOutput").ap()
    two_block_kernel(nc, *args, out)
    r = _run(nc, [arrays], core_ids=[0])
    y = np.asarray(r.results[0]["out_fm"])
    return np.ascontiguousarray(y.transpose(2, 1, 0).reshape(1, S, D))
```
